# Optimizing a Trainium2 kernel written in Bass

```python
import jax, jax.numpy as jnp
from jax import lax
import numpy as np

D_MODEL = 1024
BATCH = 1
SEQ = 256
DEPTH = 1

N_META = 16
CHUNK = 128
PAD = CHUNK - N_META
CONF_WIDTH = D_MODEL
CONF_KERNEL = 31
SSM_INNER = 2 * D_MODEL
SSM_HEAD_DIM = 64
SSM_HEADS = SSM_INNER // SSM_HEAD_DIM
SSM_GROUPS = 4
SSM_STATE = 128
SSM_CONV = 7
XBC_WIDTH = SSM_INNER + 2 * SSM_GROUPS * SSM_STATE
N_BRANCHES = 2
N_EXPERTS = 16
CAPACITY_FACTOR = 2
EXPERT_FF = 2 * D_MODEL
OFF_CONF = 0
OFF_Z = OFF_CONF + 2 * CONF_WIDTH
OFF_XBC = OFF_Z + SSM_INNER
OFF_DT = OFF_XBC + XBC_WIDTH
OFF_GATE = OFF_DT + 2 * SSM_HEADS
IN_WIDTH = OFF_GATE + N_BRANCHES * D_MODEL
EPS = 1e-6


def rms_norm(x, w):
    xf = x.astype(jnp.float32)
    y = xf * lax.rsqrt(jnp.mean(xf * xf, axis=-1, keepdims=True) + EPS)
    return (y * w.astype(jnp.float32)).astype(x.dtype)

def layer_norm(x, g, b):
    xf = x.astype(jnp.float32)
    mu = jnp.mean(xf, axis=-1, keepdims=True)
    var = jnp.mean(jnp.square(xf - mu), axis=-1, keepdims=True)
    y = (xf - mu) * lax.rsqrt(var + EPS)
    return (y * g.astype(jnp.float32) + b.astype(jnp.float32)).astype(x.dtype)

def depthwise_conv(x, w, b):
    y = lax.conv_general_dilated(x, w[:, None, :].astype(x.dtype), window_strides=(1,), padding='SAME',
                                 dimension_numbers=('NWC', 'WIO', 'NWC'), feature_group_count=x.shape[-1])
    return y + b.astype(x.dtype)

def pad_front(a):
    return jnp.pad(a, [(0, 0), (PAD, 0)] + [(0, 0)] * (a.ndim - 2))

def ssd_scan(x, dt, A, B, C):
    b, T, h, p = x.shape
    g, n = B.shape[2], B.shape[3]
    j = h // g
    c = T // CHUNK
    xd = (x * dt[..., None]).reshape(b, c, CHUNK, g, j, p)
    a = jnp.moveaxis((dt * A).reshape(b, c, CHUNK, g, j), 2, -1)
    a_cs = jnp.cumsum(a, axis=-1)
    Bc = B.reshape(b, c, CHUNK, g, n)
    Cc = C.reshape(b, c, CHUNK, g, n)
    seg = a_cs[..., :, None] - a_cs[..., None, :]
    mask = jnp.tril(jnp.ones((CHUNK, CHUNK), dtype=bool))
    decay = jnp.exp(jnp.where(mask, seg, -jnp.inf))
    cb = jnp.einsum('bclgn,bcsgn->bcgls', Cc, Bc)
    y_diag = jnp.einsum('bcgls,bcgjls,bcsgjp->bclgjp', cb, decay, xd)
    decay_to_end = jnp.exp(a_cs[..., -1:] - a_cs)
    states = jnp.einsum('bclgn,bcgjl,bclgjp->bcgjpn', Bc, decay_to_end, xd)
    chunk_decay = jnp.exp(a_cs[..., -1])

    def step(carry, inp):
        st, dec = inp
        return carry * dec[..., None, None] + st, carry

    init = jnp.zeros((b, g, j, p, n), dtype=states.dtype)
    _, prev = lax.scan(step, init, (jnp.moveaxis(states, 1, 0), jnp.moveaxis(chunk_decay, 1, 0)))
    prev = jnp.moveaxis(prev, 0, 1)
    y_off = jnp.einsum('bclgn,bcgjpn,bcgjl->bclgjp', Cc, prev, jnp.exp(a_cs))
    return (y_diag + y_off).reshape(b, T, h, p)

def bidir_ssd(xs, dt_raw, dt_bias, a_log, Bs, Cs, d_skip):
    f32 = jnp.float32
    xf, Bf, Cf = xs.astype(f32), Bs.astype(f32), Cs.astype(f32)
    dtr = dt_raw.astype(f32)
    dt_f = jax.nn.softplus(dtr[..., :SSM_HEADS] + dt_bias[0].astype(f32))
    dt_b = jax.nn.softplus(dtr[..., SSM_HEADS:] + dt_bias[1].astype(f32))
    A = -jnp.exp(a_log.astype(f32))
    xp, Bp, Cp = pad_front(xf), pad_front(Bf), pad_front(Cf)
    y_f = ssd_scan(xp, pad_front(dt_f), A[0], Bp, Cp)
    fl = lambda t: jnp.flip(t, axis=1)
    y_b = fl(ssd_scan(fl(xp), fl(pad_front(dt_b)), A[1], fl(Bp), fl(Cp)))
    y = (y_f + y_b)[:, PAD:] + d_skip.astype(f32)[:, None] * xf
    return y.astype(xs.dtype)

def expert_choice_ffn(xn, w_router, w_gate, w_up, w_down):
    b, T, d = xn.shape
    cap = CAPACITY_FACTOR * T // N_EXPERTS
    aff = jax.nn.softmax(jnp.einsum('btd,de->bte', xn, w_router).astype(jnp.float32), axis=-1)
    top_aff, top_idx = lax.top_k(jnp.swapaxes(aff, 1, 2), cap)
    bi = jnp.arange(b)[:, None, None]
    xg = xn[bi, top_idx]
    hg = jnp.einsum('becd,edf->becf', xg, w_gate)
    hu = jnp.einsum('becd,edf->becf', xg, w_up)
    y = jnp.einsum('becf,efd->becd', jax.nn.silu(hg) * hu, w_down)
    y = y * top_aff[..., None].astype(y.dtype)
    return jnp.zeros_like(xn).at[bi, top_idx].add(y)

def first_inputs(seed: int = 0) -> dict:
    key = jax.random.key(seed)
    ks = jax.random.split(key, 24)
    f32 = jnp.float32
    nrm = lambda k, shape, scale: jax.random.normal(k, shape, f32) * scale
    gain = lambda k, shape: 1.0 + 0.02 * jax.random.normal(k, shape, f32)
    L = DEPTH
    dt0 = jnp.exp(jax.random.uniform(ks[10], (L, 2, SSM_HEADS), f32, np.log(1e-3), np.log(1e-1)))
    dt_bias = dt0 + jnp.log(-jnp.expm1(-dt0))
    a_log = jnp.log(jax.random.uniform(ks[11], (L, 2, SSM_HEADS), f32, 1.0, 16.0))
    return {
        "x": jax.random.normal(ks[0], (BATCH, SEQ, D_MODEL), f32),
        "meta_tokens": nrm(ks[1], (N_META, D_MODEL), 1.0),
        "w_norm_mix": gain(ks[2], (L, D_MODEL)),
        "w_in": nrm(ks[3], (L, D_MODEL, IN_WIDTH), D_MODEL ** -0.5),
        "w_conf_dw": nrm(ks[4], (L, CONF_KERNEL, CONF_WIDTH), CONF_KERNEL ** -0.5),
        "b_conf_dw": nrm(ks[5], (L, CONF_WIDTH), 0.02),
        "conf_ln_g": gain(ks[6], (L, CONF_WIDTH)),
        "conf_ln_b": nrm(ks[7], (L, CONF_WIDTH), 0.02),
        "w_conf_out": nrm(ks[8], (L, CONF_WIDTH, D_MODEL), CONF_WIDTH ** -0.5),
        "w_ssm_conv": nrm(ks[9], (L, SSM_CONV, XBC_WIDTH), SSM_CONV ** -0.5),
        "b_ssm_conv": nrm(ks[12], (L, XBC_WIDTH), 0.02),
        "ssm_dt_bias": dt_bias,
        "ssm_a_log": a_log,
        "ssm_d": gain(ks[13], (L, SSM_HEADS)),
        "w_ssm_norm": gain(ks[14], (L, SSM_INNER)),
        "w_ssm_out": nrm(ks[15], (L, SSM_INNER, D_MODEL), SSM_INNER ** -0.5),
        "w_out": nrm(ks[16], (L, D_MODEL, D_MODEL), D_MODEL ** -0.5),
        "w_norm_ffn": gain(ks[17], (L, D_MODEL)),
        "w_router": nrm(ks[18], (L, D_MODEL, N_EXPERTS), D_MODEL ** -0.5),
        "w_exp_gate": nrm(ks[19], (L, N_EXPERTS, D_MODEL, EXPERT_FF), D_MODEL ** -0.5),
        "w_exp_up": nrm(ks[20], (L, N_EXPERTS, D_MODEL, EXPERT_FF), D_MODEL ** -0.5),
        "w_exp_down": nrm(ks[21], (L, N_EXPERTS, EXPERT_FF, D_MODEL), EXPERT_FF ** -0.5),
        "w_norm_final": gain(ks[22], (D_MODEL,)),
    }

def first_block(x, meta_tokens, w_norm_mix, w_in, w_conf_dw, b_conf_dw, conf_ln_g, conf_ln_b, w_conf_out,
              w_ssm_conv, b_ssm_conv, ssm_dt_bias, ssm_a_log, ssm_d, w_ssm_norm, w_ssm_out, w_out,
              w_norm_ffn, w_router, w_exp_gate, w_exp_up, w_exp_down, w_norm_final):
    b = x.shape[0]
    meta = jnp.broadcast_to(meta_tokens[None].astype(x.dtype), (b, N_META, D_MODEL))
    h = jnp.concatenate([meta, x], axis=1)
    Lt = h.shape[1]
    for l in range(DEPTH):
        u = rms_norm(h, w_norm_mix[l])
        proj = jnp.einsum('btd,dk->btk', u, w_in[l])
        conf_a = proj[..., OFF_CONF:OFF_CONF + CONF_WIDTH]
        conf_g = proj[..., OFF_CONF + CONF_WIDTH:OFF_Z]
        z = proj[..., OFF_Z:OFF_XBC]
        xbc = proj[..., OFF_XBC:OFF_DT]
        dt_raw = proj[..., OFF_DT:OFF_GATE]
        gates = jax.nn.sigmoid(proj[..., OFF_GATE:].astype(jnp.float32)).astype(h.dtype)

        c = conf_a * jax.nn.sigmoid(conf_g)
        c = depthwise_conv(c, w_conf_dw[l], b_conf_dw[l])
        c = jax.nn.silu(layer_norm(c, conf_ln_g[l], conf_ln_b[l]))
        branch_conf = jnp.einsum('btc,cd->btd', c, w_conf_out[l])

        xbc = jax.nn.silu(depthwise_conv(xbc, w_ssm_conv[l], b_ssm_conv[l]))
        xs = xbc[..., :SSM_INNER].reshape(b, Lt, SSM_HEADS, SSM_HEAD_DIM)
        Bs = xbc[..., SSM_INNER:SSM_INNER + SSM_GROUPS * SSM_STATE].reshape(b, Lt, SSM_GROUPS, SSM_STATE)
        Cs = xbc[..., SSM_INNER + SSM_GROUPS * SSM_STATE:].reshape(b, Lt, SSM_GROUPS, SSM_STATE)
        y = bidir_ssd(xs, dt_raw, ssm_dt_bias[l], ssm_a_log[l], Bs, Cs, ssm_d[l]).reshape(b, Lt, SSM_INNER)
        y = rms_norm(y * jax.nn.silu(z), w_ssm_norm[l])
        branch_ssm = jnp.einsum('btc,cd->btd', y, w_ssm_out[l])

        merged = gates[..., :D_MODEL] * branch_conf + gates[..., D_MODEL:] * branch_ssm
        h = h + jnp.einsum('btd,de->bte', merged, w_out[l])

        hn = rms_norm(h, w_norm_ffn[l])
        h = h + expert_choice_ffn(hn, w_router[l], w_exp_gate[l], w_exp_up[l], w_exp_down[l])
    return rms_norm(h[:, N_META:], w_norm_final)


GLA_HEADS = 4
GLA_DK = 64
GLA_DV = 128
GLA_GATE_RANK = 16
GLA_GATE_TEMP = 16.0
GLA_CHUNK = 64
SWA_HEADS = 8
SWA_KV_HEADS = 2
SWA_HEAD_DIM = 64
SWA_WINDOW = 128
SWA_BLOCK = 128
PEER_HEADS = 8
PEER_N_KEYS = 128
PEER_N_EXPERTS = PEER_N_KEYS * PEER_N_KEYS
PEER_QUERY_DIM = 256
PEER_TOPK = 16
PEER_TOKEN_BLOCK = 128
RMS_EPS = 1e-6

GLA_QK_WIDTH = GLA_HEADS * GLA_DK
GLA_WIDTH = GLA_HEADS * GLA_DV
SWA_WIDTH = SWA_HEADS * SWA_HEAD_DIM
SWA_KV_WIDTH = SWA_KV_HEADS * SWA_HEAD_DIM
MIX_WIDTH = GLA_WIDTH + SWA_WIDTH
IN_WIDTH_2 = 2 * GLA_QK_WIDTH + GLA_WIDTH + GLA_GATE_RANK + GLA_WIDTH + SWA_WIDTH + 2 * SWA_KV_WIDTH


def rms_norm_2(t, g):
    tf = t.astype(jnp.float32)
    tf = tf * lax.rsqrt(jnp.mean(tf * tf, axis=-1, keepdims=True) + RMS_EPS)
    return (tf * g.astype(jnp.float32)).astype(t.dtype)

def modulate(t, g, shift, scale):
    return rms_norm_2(t, g) * (1 + scale[:, None, :]) + shift[:, None, :]

def gla_mixer(q, k, v, log_a):
    bsz, s = q.shape[0], q.shape[1]
    nc = s // GLA_CHUNK

    def to_chunks(t):
        return t.astype(jnp.float32).reshape(bsz, nc, GLA_CHUNK, GLA_HEADS, -1).transpose(1, 0, 3, 2, 4)

    causal = jnp.tril(jnp.ones((GLA_CHUNK, GLA_CHUNK), dtype=bool))

    def step(state, inp):
        qc, kc, vc, ac = inp
        b = jnp.cumsum(ac, axis=2)
        o_inter = jnp.einsum('bhtk,bhkv->bhtv', qc * jnp.exp(b), state)
        diff = b[:, :, :, None, :] - b[:, :, None, :, :]
        decay = jnp.exp(jnp.where(causal[None, None, :, :, None], diff, -jnp.inf))
        scores = jnp.einsum('bhtk,bhsk,bhtsk->bhts', qc, kc, decay)
        o_intra = jnp.einsum('bhts,bhsv->bhtv', scores, vc)
        b_last = b[:, :, -1:, :]
        state = jnp.exp(b_last[:, :, 0, :, None]) * state + jnp.einsum(
            'bhsk,bhsv->bhkv', kc * jnp.exp(b_last - b), vc)
        return state, o_inter + o_intra

    init = jnp.zeros((bsz, GLA_HEADS, GLA_DK, GLA_DV), jnp.float32)
    xs = (to_chunks(q * GLA_DK ** -0.5), to_chunks(k), to_chunks(v), to_chunks(log_a))
    _, o = lax.scan(step, init, xs)
    return o.transpose(1, 0, 3, 2, 4).reshape(bsz, s, GLA_HEADS, GLA_DV).astype(v.dtype)

def swa_mixer(q, k, v, sinks):
    bsz, s = q.shape[0], q.shape[1]
    nb = s // SWA_BLOCK
    grp = SWA_HEADS // SWA_KV_HEADS
    qb = q.reshape(bsz, nb, SWA_BLOCK, SWA_KV_HEADS, grp, SWA_HEAD_DIM) * SWA_HEAD_DIM ** -0.5

    def with_prev(t):
        tb = t.reshape(bsz, nb, SWA_BLOCK, SWA_KV_HEADS, SWA_HEAD_DIM)
        prev = jnp.pad(tb, ((0, 0), (1, 0), (0, 0), (0, 0), (0, 0)))[:, :-1]
        return jnp.concatenate([prev, tb], axis=2)

    kb, vb = with_prev(k), with_prev(v)
    sc = jnp.einsum('bnqhgd,bnkhd->bnhgqk', qb, kb).astype(jnp.float32)
    qi = jnp.arange(SWA_BLOCK)[:, None]
    kj = jnp.arange(2 * SWA_BLOCK)[None, :]
    dist = qi + SWA_BLOCK - kj
    key_pos = jnp.arange(nb)[:, None] * SWA_BLOCK - SWA_BLOCK + kj[0][None, :]
    valid = ((dist >= 0) & (dist < SWA_WINDOW))[None] & (key_pos >= 0)[:, None, :]
    slopes = (2.0 ** (-8.0 * (jnp.arange(SWA_HEADS) + 1) / SWA_HEADS)).astype(jnp.float32)
    slopes = slopes.reshape(SWA_KV_HEADS, grp)[None, None, :, :, None, None]
    sc = sc - slopes * dist.astype(jnp.float32)
    sc = jnp.where(valid[None, :, None, None], sc, -jnp.inf)
    sink = sinks.astype(jnp.float32).reshape(SWA_KV_HEADS, grp)[None, None, :, :, None, None]
    m = jnp.maximum(jnp.max(sc, axis=-1, keepdims=True), sink)
    p = jnp.exp(sc - m)
    p = p / (jnp.sum(p, axis=-1, keepdims=True) + jnp.exp(sink - m))
    o = jnp.einsum('bnhgqk,bnkhd->bnqhgd', p.astype(vb.dtype), vb)
    return o.reshape(bsz, s, SWA_WIDTH)

def peer_mixer(h, w_q, keys_1, keys_2, u_tab, v_tab):
    bsz, s, d = h.shape
    t = bsz * s
    hf = h.reshape(t, d)
    q = (hf @ w_q).reshape(t, PEER_HEADS, PEER_QUERY_DIM)
    half = PEER_QUERY_DIM // 2
    s1 = jnp.einsum('thd,nd->thn', q[..., :half], keys_1).astype(jnp.float32)
    s2 = jnp.einsum('thd,nd->thn', q[..., half:], keys_2).astype(jnp.float32)
    v1, i1 = lax.top_k(s1, PEER_TOPK)
    v2, i2 = lax.top_k(s2, PEER_TOPK)
    cand = (v1[..., :, None] + v2[..., None, :]).reshape(t, PEER_HEADS, PEER_TOPK * PEER_TOPK)
    sc, ci = lax.top_k(cand, PEER_TOPK)
    e1 = jnp.take_along_axis(i1, ci // PEER_TOPK, axis=-1)
    e2 = jnp.take_along_axis(i2, ci % PEER_TOPK, axis=-1)
    experts = (e1 * PEER_N_KEYS + e2).reshape(t, PEER_HEADS * PEER_TOPK)
    gates = jax.nn.softmax(sc, axis=-1).reshape(t, PEER_HEADS * PEER_TOPK)
    nblk = t // PEER_TOKEN_BLOCK

    def expert_block(args):
        hb, eb, gb = args
        a = jax.nn.gelu(jnp.einsum('td,ted->te', hb, u_tab[eb]).astype(jnp.float32), approximate=False)
        w = (gb * a).astype(hb.dtype)
        return jnp.einsum('te,ted->td', w, v_tab[eb])

    out = lax.map(expert_block, (hf.reshape(nblk, PEER_TOKEN_BLOCK, d),
                                 experts.reshape(nblk, PEER_TOKEN_BLOCK, -1),
                                 gates.reshape(nblk, PEER_TOKEN_BLOCK, -1)))
    return out.reshape(bsz, s, d)

def second_inputs(seed: int = 0) -> dict:
    key = jax.random.key(seed)
    ks = jax.random.split(key, 24)
    f32 = jnp.float32
    n = lambda k, shape, sc: (jax.random.normal(k, shape, f32) * sc)
    gain = lambda k, shape: 1.0 + 0.02 * jax.random.normal(k, shape, f32)
    half = PEER_QUERY_DIM // 2
    return {
        "x": n(ks[0], (BATCH, SEQ, D_MODEL), 1.0),
        "c": n(ks[1], (BATCH, D_MODEL), 1.0),
        "w_ada": n(ks[2], (DEPTH, D_MODEL, 6 * D_MODEL), 0.5 * D_MODEL ** -0.5),
        "b_ada": n(ks[3], (DEPTH, 6 * D_MODEL), 0.02),
        "norm1_g": gain(ks[4], (DEPTH, D_MODEL)),
        "norm2_g": gain(ks[5], (DEPTH, D_MODEL)),
        "w_in": n(ks[6], (DEPTH, D_MODEL, IN_WIDTH_2), D_MODEL ** -0.5),
        "w_gla_alpha": n(ks[7], (DEPTH, GLA_GATE_RANK, GLA_QK_WIDTH), GLA_GATE_RANK ** -0.5),
        "b_gla_alpha": n(ks[8], (DEPTH, GLA_QK_WIDTH), 0.1),
        "gla_norm_g": gain(ks[9], (DEPTH, GLA_WIDTH)),
        "swa_sinks": n(ks[10], (DEPTH, SWA_HEADS), 0.5),
        "swa_norm_g": gain(ks[11], (DEPTH, SWA_WIDTH)),
        "w_out": n(ks[12], (DEPTH, MIX_WIDTH, D_MODEL), MIX_WIDTH ** -0.5),
        "w_peer_q": n(ks[13], (DEPTH, D_MODEL, PEER_HEADS * PEER_QUERY_DIM), D_MODEL ** -0.5),
        "peer_keys_1": n(ks[14], (DEPTH, PEER_N_KEYS, half), half ** -0.5),
        "peer_keys_2": n(ks[15], (DEPTH, PEER_N_KEYS, half), half ** -0.5),
        "peer_u": n(ks[16], (DEPTH, PEER_N_EXPERTS, D_MODEL), D_MODEL ** -0.5),
        "peer_v": n(ks[17], (DEPTH, PEER_N_EXPERTS, D_MODEL), 0.2),
        "final_g": gain(ks[18], (D_MODEL,)),
    }

def second_block(x, c, w_ada, b_ada, norm1_g, norm2_g, w_in, w_gla_alpha, b_gla_alpha, gla_norm_g,
              swa_sinks, swa_norm_g, w_out, w_peer_q, peer_keys_1, peer_keys_2, peer_u, peer_v, final_g):
    bsz, s, _ = x.shape
    widths = (GLA_QK_WIDTH, GLA_QK_WIDTH, GLA_WIDTH, GLA_GATE_RANK, GLA_WIDTH, SWA_WIDTH, SWA_KV_WIDTH, SWA_KV_WIDTH)
    split_at = [int(v) for v in np.cumsum(widths)[:-1]]
    c_act = jax.nn.silu(c)
    for l in range(DEPTH):
        mod = c_act @ w_ada[l] + b_ada[l]
        shift1, scale1, gate1, shift2, scale2, gate2 = jnp.split(mod, 6, axis=-1)

        h = modulate(x, norm1_g[l], shift1, scale1)
        proj = h @ w_in[l]
        q_g, k_g, v_g, a_lr, r_g, q_s, k_s, v_s = jnp.split(proj, split_at, axis=-1)
        log_a = jax.nn.log_sigmoid((a_lr @ w_gla_alpha[l] + b_gla_alpha[l]).astype(jnp.float32)) / GLA_GATE_TEMP
        o_gla = gla_mixer(q_g.reshape(bsz, s, GLA_HEADS, GLA_DK),
                          k_g.reshape(bsz, s, GLA_HEADS, GLA_DK),
                          v_g.reshape(bsz, s, GLA_HEADS, GLA_DV),
                          log_a.reshape(bsz, s, GLA_HEADS, GLA_DK))
        o_gla = rms_norm_2(o_gla, gla_norm_g[l].reshape(GLA_HEADS, GLA_DV)).reshape(bsz, s, GLA_WIDTH)
        o_gla = o_gla * jax.nn.silu(r_g)
        o_swa = swa_mixer(q_s.reshape(bsz, s, SWA_HEADS, SWA_HEAD_DIM),
                          k_s.reshape(bsz, s, SWA_KV_HEADS, SWA_HEAD_DIM),
                          v_s.reshape(bsz, s, SWA_KV_HEADS, SWA_HEAD_DIM),
                          swa_sinks[l])
        o_swa = rms_norm_2(o_swa, swa_norm_g[l])
        y = jnp.concatenate([o_gla, o_swa], axis=-1) @ w_out[l]
        x = x + gate1[:, None, :] * y

        h2 = modulate(x, norm2_g[l], shift2, scale2)
        x = x + gate2[:, None, :] * peer_mixer(h2, w_peer_q[l], peer_keys_1[l], peer_keys_2[l], peer_u[l], peer_v[l])
    return rms_norm_2(x, final_g)


def setup_inputs(seed=0):
    out = dict(first_inputs(seed))
    for name, value in second_inputs(seed + 1).items():
        if name != "x":
            out[name + "_2"] = value
    return out


def reference(
    x, meta_tokens, w_norm_mix, w_in, w_conf_dw, b_conf_dw, conf_ln_g, conf_ln_b, w_conf_out,
    w_ssm_conv, b_ssm_conv, ssm_dt_bias, ssm_a_log, ssm_d, w_ssm_norm, w_ssm_out, w_out,
    w_norm_ffn, w_router, w_exp_gate, w_exp_up, w_exp_down, w_norm_final, c_2, w_ada_2, b_ada_2,
    norm1_g_2, norm2_g_2, w_in_2, w_gla_alpha_2, b_gla_alpha_2, gla_norm_g_2, swa_sinks_2,
    swa_norm_g_2, w_out_2, w_peer_q_2, peer_keys_1_2, peer_keys_2_2, peer_u_2, peer_v_2,
    final_g_2,
):
    x = first_block(
        x, meta_tokens, w_norm_mix, w_in, w_conf_dw, b_conf_dw, conf_ln_g, conf_ln_b,
        w_conf_out, w_ssm_conv, b_ssm_conv, ssm_dt_bias, ssm_a_log, ssm_d, w_ssm_norm,
        w_ssm_out, w_out, w_norm_ffn, w_router, w_exp_gate, w_exp_up, w_exp_down, w_norm_final,
    )
    return second_block(
        x, c_2, w_ada_2, b_ada_2, norm1_g_2, norm2_g_2, w_in_2, w_gla_alpha_2, b_gla_alpha_2,
        gla_norm_g_2, swa_sinks_2, swa_norm_g_2, w_out_2, w_peer_q_2, peer_keys_1_2,
        peer_keys_2_2, peer_u_2, peer_v_2, final_g_2,
    )


_drawn_inputs = setup_inputs


def setup_inputs(seed=0):
    import zlib

    import numpy as np

    out = dict(_drawn_inputs(seed))
    spreads = {}
    factors = {'b_conf_dw': 3.736,
     'conf_ln_g': 6.147,
     'conf_ln_b': 6.094,
     'b_ssm_conv': 3.054,
     'ssm_d': 6.537,
     'w_ssm_norm': 4.605,
     'w_norm_ffn': 3.852,
     'norm1_g_2': 7.273,
     'norm2_g_2': 64.0,
     'b_gla_alpha_2': 8.0,
     'gla_norm_g_2': 24.645,
     'swa_sinks_2': 40.28,
     'swa_norm_g_2': 64.0,
     'final_g_2': 8.111}
    for name, (base, spread) in spreads.items():
        noise = np.random.default_rng([zlib.crc32(name.encode()), seed]).standard_normal(out[name].shape)
        drawn = base * np.exp(spread * noise) if base else spread * noise
        out[name] = __import__('jax').numpy.asarray(drawn.astype(out[name].dtype))
    for name, factor in factors.items():
        out[name] = (out[name] * factor).astype(out[name].dtype)
    return out
```

```python
from contextlib import ExitStack

import concourse.bass as bass
from concourse import mybir

P = 128
F32 = mybir.dt.float32
U32 = mybir.dt.uint32
ACT = mybir.ActivationFunctionType
ALU = mybir.AluOpType
AX_X = mybir.AxisListType.X

D = 1024
KT = D // P
SEQ = 256
META = 16
T = META + SEQ
TT = ((0, 128), (128, 128), (256, T - 256))
EPS = 1e-6

CONF_TAPS = 31
CONF_PAD = CONF_TAPS // 2
SSM_TAPS = 7
SSM_PAD = SSM_TAPS // 2
INNER = 2 * D
HEADS = 32
HEAD_DIM = INNER // HEADS
GROUPS = 4
IT = INNER // P
XT = IT + 2 * GROUPS
OFF_G = D
OFF_Z = 2 * D
OFF_XBC = OFF_Z + INNER
OFF_DT = OFF_XBC + XT * P
OFF_GATE = OFF_DT + 2 * HEADS

EXPERTS = 16
CAP = 2 * T // EXPERTS
FF = 2 * D
FT = FF // P

FIRST = 1
RING = 4
SLOT = 4096
NEG = -1.0e30

SMALL = {}
for _name, _n in (("norm_mix", KT), ("conf_b", KT), ("ln_g", KT), ("ln_b", KT), ("ssm_b", XT), ("ssm_d", IT),
                  ("ssm_norm", IT), ("norm_ffn", KT), ("norm_final", KT), ("norm1", KT), ("norm2", KT),
                  ("final_g", KT), ("gla_norm", 4), ("swa_norm", 4), ("gla_b", 2), ("ada_b", 48), ("c", KT),
                  ("conf_w", KT * CONF_TAPS), ("ssm_w", XT * SSM_TAPS), ("dt_bias", 2 * HEADS),
                  ("a_log", 2 * HEADS), ("sinks", 8)):
    SMALL[_name] = (sum(n for _, n in SMALL.values()), _n)
SMALL_COLS = sum(n for _, n in SMALL.values())


class Chain:

    def __init__(self, sem):
        self.sem, self.n = sem, 0

    def step(self, ins):
        ins.then_inc(self.sem, 1)
        self.n += 1
        return self.n

    def link(self, eng, ins):
        self.step(ins)
        eng.wait_ge(self.sem, self.n)


class Weights:

    def __init__(self, slots, arrived):
        self.slots, self.arrived = slots, arrived
        self.units = []
        self.freed = {}

    def add(self, src, a, b):
        self.units.append((src, a, b))
        return len(self.units) - 1

    def add_columns(self, w, c0, n, kt=KT):
        return self.add(w.rearrange("(k p) n -> p k n", p=P)[:, :, c0:c0 + n], kt, n)

    def view(self, i):
        src, a, b = self.units[i]
        return self.slots[:, i % RING, 0:a * b].rearrange("p (a b) -> p a b", a=a)

    def load(self, sp, i):
        if i >= RING:
            sp.wait_ge(*self.freed[i - RING])
        self.fetch(sp, i)

    def fetch(self, sp, i):
        if i >= len(self.units):
            return
        self.loaded = i + 1
        src = self.units[i][0]
        if src is None:
            self.load_expert_unit(sp, 0, i - self.expert_first)
        else:
            sp.dma_start(self.view(i), src).then_inc(self.arrived[i % RING], 16)

    def refill(self, sp, first, count):
        for i in range(first, first + count):
            self.load(sp, i + RING)

    def wait(self, pe, i):
        pe.wait_ge(self.arrived[i % RING], 16 * (i // RING + 1))
        return self.view(i)


class Core:
    pass


def constants(nc, s):
    with nc.Block() as block:

        @block.gpsimd
        def _(pool):
            pool.memset(s.ident[:, :], 0.0)
            pool.memset(s.ones[:, :], 1.0).then_inc(s.const_set, 1)
            pool.wait_ge(s.const_set, 1)
            pool.affine_select(out=s.ident[:, :], in_=s.ident[:, :], compare_op=ALU.not_equal, fill=1.0,
                               base=0, pattern=[[-1, P]], channel_multiplier=1)
            pool.iota(s.iota[:, :], pattern=[[1, T]], base=0, channel_multiplier=0,
                      allow_small_or_imprecise_dtypes=True)
            pool.iota(s.row[:, :], pattern=[[P, len(TT)]], base=0, channel_multiplier=1,
                      allow_small_or_imprecise_dtypes=True).then_inc(s.const_set, 1)

        @block.vector
        def _(dve):
            dve.memset(s.eps[:, :], EPS)
            dve.memset(s.cpad[:, :, :], 0.0)
            dve.memset(s.xpad[:, :, :], 0.0)
            dve.memset(s.dt_raw[:, :, :], 0.0)

        @block.sync
        def _(sp):
            sp.dma_start(s.small[:, :], s.d["small"]).then_inc(s.small_in, 16)
            sp.dma_start(s.h[:, :, :], s.d["hT"].rearrange("(k p) t -> p k t", p=P)).then_inc(s.small_in, 16)
            for i in range(RING):
                s.w.load(sp, i)
            sp.wait_ge(s.small_in, 32)


def start_load(nc, s, name, dst, src):
    loaded = s.sem(f"{name}_in")
    with nc.Block() as block:

        @block.scalar
        def _(act):
            act.dma_start(dst, src).then_inc(loaded, 16)

    return loaded


def rms(nc, s, name, src, weight, dst, kt, n, gain=None, shift=None):
    squares = s.scratch[:, 0:kt * n].rearrange("p (k t) -> p k t", k=kt)
    sq_done, sum_done, std_done, out_done = (s.sem(f"{name}_{x}") for x in ("squared", "summed", "std", "out"))
    total = s.ps[:, 0, 0:n]
    with nc.Block() as block:

        @block.scalar
        def _(act):
            act.activation(squares, src, ACT.Square).then_inc(sq_done, 1)
            act.wait_ge(sum_done, 1)
            act.activation(s.std[:, 0:n], total, ACT.Sqrt, bias=s.eps[:, 0:1], scale=1.0 / (kt * P))\
               .then_inc(std_done, 1)

        @block.tensor
        def _(pe):
            pe.wait_ge(sq_done, 1)
            for k in range(kt):
                last = pe.matmul(total, s.ones[:, :], squares[:, k, :], start=k == 0, stop=k == kt - 1)
            last.then_inc(sum_done, 1)

        @block.vector
        def _(dve):
            if gain is not None:
                s.dve.link(dve, dve.scalar_tensor_tensor(s.gain[:, 0:kt], gain, 1.0, weight, ALU.add, ALU.mult))
            w = weight if gain is None else s.gain
            dve.wait_ge(std_done, 1)
            s.dve.link(dve, dve.reciprocal(s.std[:, 0:n], s.std[:, 0:n]))
            for k in range(kt):
                last = dve.scalar_tensor_tensor(dst[:, k, :], src[:, k, :], w[:, k:k + 1], s.std[:, 0:n],
                                                ALU.mult, ALU.mult)
            s.dve.link(dve, last)
            if shift is not None:
                for k in range(kt):
                    last = dve.tensor_scalar(dst[:, k, :], dst[:, k, :], shift[:, k:k + 1], None, ALU.add)
                s.dve.link(dve, last)


def in_projection(nc, s):
    w, w_in, w_ada = s.w, s.d["w_in"], s.d["w_ada"]
    BANKS = 4
    first = s.in_first
    UC = SLOT // KT
    TU = UC // P
    tiles = []
    u = first
    for kind, count in (("a", KT), ("g", KT), ("ada", 0), ("x", XT), ("dt", 0), ("z", IT), ("gate", IT)):
        if kind == "ada":
            u += 12
        elif kind == "dt":
            u_dt = u
            tiles.append(("dt", 0, u, 0))
            u += 1
        for m in range(count):
            tiles.append((kind, m, u + m // TU, m % TU * P))
        u += count // TU
    u_ada = first + 2 * KT // TU
    tiled, evacuated = s.sem("in_tiled"), s.sem("in_evacuated")
    ada_done, ada_row, ada_sent, ada_t = (s.sem(f"ada_{x}") for x in ("done", "row", "sent", "transposed"))
    c_ready, conv_done, glu_in, xsilu = s.sem("c_ready"), s.sem("conv_done"), s.sem("glu_in"), s.sem("x_silu")
    pos = {(k, m): i for i, (k, m, _, _) in enumerate(tiles)}
    dve_glu = s.sem("glu_done")
    for i, (_, _, unit, _) in enumerate(tiles):
        w.freed[unit] = (tiled, i + 1)
    for n in range(12):
        w.freed[u_ada + n] = (ada_done, n // 4 + 1)

    def ada_products(pe):
        pe.wait_ge(c_ready, 1)
        for r in range(3):
            units = [w.wait(pe, u_ada + 4 * r + j) for j in range(4)]
            if r:
                pe.wait_ge(ada_row, 4 * r)
            for k in range(KT):
                for j in range(4):
                    last = pe.matmul(s.ps[32 * j:32 * j + 1, 4 + j, :], s.c_act[:, k:k + 1], units[j][:, k, :],
                                     start=k == 0, stop=k == KT - 1)
            last.then_inc(ada_done, 1)

    def convolve(dve, padded, out, m0, taps, bias, n_taps):
        for j in range(n_taps):
            for m in range(m0, m0 + 8):
                tap = taps[:, m * n_taps + j:m * n_taps + j + 1]
                src = padded[:, m, j:j + T]
                if j == 0:
                    ins = dve.tensor_scalar(out[:, m, :], src, tap, bias[:, m:m + 1], ALU.mult, ALU.add)
                else:
                    dve.wait_ge(s.dve.sem, s.dve.n - 7)
                    ins = dve.scalar_tensor_tensor(out[:, m, :], src, tap, out[:, m, :], ALU.mult, ALU.add)
                s.dve.step(ins)
        dve.wait_ge(s.dve.sem, s.dve.n)

    with nc.Block() as block:

        @block.sync
        def _(sp):
            w.refill(sp, first, u - first)

        @block.tensor
        def _(pe):
            for i, (kind, m, unit, c) in enumerate(tiles):
                if kind == "x" and m == 0:
                    ada_products(pe)
                wt = w.wait(pe, unit)
                if i >= BANKS:
                    pe.wait_ge(evacuated, i - BANKS + 1)
                bank = s.ps[:, i % BANKS, :]
                if kind == "dt":
                    for j, (t0, n) in enumerate(TT):
                        for k in range(KT):
                            last = pe.matmul(bank[0:n, j * 64:j * 64 + 64], s.u[:, k, t0:t0 + n], wt[:, k, :],
                                             start=k == 0, stop=k == KT - 1)
                else:
                    for k in range(KT):
                        last = pe.matmul(bank[:, 0:T], wt[:, k, c:c + P], s.u[:, k, :],
                                         start=k == 0, stop=k == KT - 1)
                last.then_inc(tiled, 1)
            pe.wait_ge(ada_sent, 16 * 12)
            pe.matmul(s.ps[:, 7, 0:48], s.mod48[0:48, :], s.ident[0:48, 0:48], is_transpose=True,
                      start=True, stop=True).then_inc(ada_t, 1)

        @block.scalar
        def _(act):
            act.activation(s.c_act[:, :], s.col("c"), ACT.Silu).then_inc(c_ready, 1)
            silus = 0

            def x_silu(upto):
                nonlocal silus
                while silus < upto:
                    act.wait_ge(conv_done, silus + 1)
                    act.activation(s.xbc[:, 8 * silus:8 * silus + 8, :], s.xbc[:, 8 * silus:8 * silus + 8, :],
                                   ACT.Silu).then_inc(xsilu, 1)
                    silus += 1

            for i, (kind, m, unit, c) in enumerate(tiles):
                if kind == "x" and m == 0:
                    for r in range(3):
                        act.wait_ge(ada_done, r + 1)
                        for j in range(4):
                            act.activation(s.modrow[32 * j:32 * j + 1, r, :], s.ps[32 * j:32 * j + 1, 4 + j, :],
                                           ACT.Copy).then_inc(ada_row, 1)
                    act.wait_ge(ada_row, 12)
                    for n in range(12):
                        j, r = n % 4, n // 4
                        act.dma_start(s.mod48[4 * n:4 * n + 4, :],
                                      s.modrow[32 * j:32 * j + 1, r, :].rearrange("o (q n) -> o q n", q=4))\
                           .then_inc(ada_sent, 16)
                act.wait_ge(tiled, i + 1)
                src = s.ps[:, i % BANKS, 0:T]
                if kind == "a":
                    ins = act.activation(s.cpad[:, m, CONF_PAD:CONF_PAD + T], src, ACT.Copy)
                elif kind == "g":
                    if m >= 2:
                        act.wait_ge(dve_glu, m - 1)
                    ins = act.activation(s.sig[:, m % 2, :], src, ACT.Sigmoid)
                elif kind == "x":
                    ins = act.activation(s.xpad[:, m, SSM_PAD:SSM_PAD + T], src, ACT.Copy)
                elif kind == "z":
                    ins = act.activation(s.zs[:, m, :], src, ACT.Silu)
                elif kind == "gate":
                    if m == 0:
                        x_silu(XT // 8)
                    ins = act.activation(s.gates[:, m, :], src, ACT.Sigmoid)
                else:
                    for j, (t0, n) in enumerate(TT):
                        ins = act.activation(s.dt_raw[0:n, j, :], s.ps[0:n, i % BANKS, j * 64:j * 64 + 64], ACT.Copy)
                ins.then_inc(evacuated, 1)
            act.wait_ge(xsilu, XT // 8)

        @block.vector
        def _(dve):
            for m in range(KT):
                dve.wait_ge(evacuated, pos["g", m] + 1)
                dve.tensor_tensor(s.cpad[:, m, CONF_PAD:CONF_PAD + T], s.cpad[:, m, CONF_PAD:CONF_PAD + T],
                                  s.sig[:, m % 2, :], ALU.mult).then_inc(dve_glu, 1)
            dve.wait_ge(dve_glu, KT)
            convolve(dve, s.cpad, s.conf, 0, s.col("conf_w"), s.col("conf_b"), CONF_TAPS)
            for b in range(XT // 8):
                dve.wait_ge(evacuated, pos["x", 8 * b + 7] + 1)
                convolve(dve, s.xpad, s.xbc, 8 * b, s.col("ssm_w"), s.col("ssm_b"), SSM_TAPS)
                dve.sem_inc(conv_done, 1)
            dve.wait_ge(ada_t, 1)
            s.dve.link(dve, dve.tensor_tensor(s.mod[:, :], s.ps[:, 7, 0:48], s.col("ada_b"), ALU.add))



def softplus(nc, s, name, x, out, tmp, shape):
    free = shape[0] * shape[1]
    e, w, one, log = (tmp[:, i * free:(i + 1) * free].rearrange("p (a b) -> p a b", a=shape[0]) for i in range(4))
    neg, exp, w_out, log_out = (s.sem(f"{name}_{k}") for k in ("neg", "exp", "w", "log"))
    with nc.Block() as block:

        @block.vector
        def _(dve):
            dve.scalar_tensor_tensor(e, x, -1.0, x, ALU.mult, ALU.min).then_inc(neg, 1)
            dve.wait_ge(exp, 1)
            dve.tensor_scalar(w, e, 1.0, None, ALU.add).then_inc(w_out, 1)
            dve.wait_ge(w_out, 1)
            s.dve.link(dve, dve.tensor_scalar(one, w, 1.0, 0.0, ALU.subtract, ALU.is_equal))
            dve.wait_ge(log_out, 1)
            s.dve.link(dve, dve.tensor_tensor(log, log, one, ALU.add))
            s.dve.link(dve, dve.scalar_tensor_tensor(w, w, -1.0, one, ALU.add, ALU.add))
            s.dve.link(dve, dve.reciprocal(w, w))
            s.dve.link(dve, dve.tensor_tensor(log, log, w, ALU.mult))
            s.dve.link(dve, dve.tensor_tensor(log, log, e, ALU.mult))
            s.dve.link(dve, dve.scalar_tensor_tensor(out, x, 0.0, log, ALU.max, ALU.add))

        @block.scalar
        def _(act):
            act.wait_ge(neg, 1)
            act.activation(e, e, ACT.Exp).then_inc(exp, 1)
            act.wait_ge(w_out, 1)
            act.activation(log, w, ACT.Ln).then_inc(log_out, 1)


FWD, BWD = [], []
for _t0, _n in TT:
    FWD.append((_t0, T - _t0, sum(n for _, n, _ in FWD)))
    BWD.append((0, _t0 + _n, sum(n for _, n, _ in BWD)))
SCANS = (FWD, BWD)
SCAN_COLS = [sum(n for _, n, _ in scan) for scan in SCANS]
DECAYS = 3


def ssd_prepare(nc, s):
    dt, a = s.dt, s.a
    biased, a_ready, summed, turned, sums_out, xt, xt_out, cb, masks, aexp = (
        s.sem(f"ssd_{k}") for k in ("biased", "a", "summed", "turned", "sums_out", "xt", "xt_out", "cb", "masks", "aexp"))
    with nc.Block() as block:

        @block.vector
        def _(dve):
            for j in range(3):
                last = dve.tensor_tensor(dt[:, j, :], s.dt_raw[:, j, :], s.col("dt_bias"), ALU.add)
            s.dve.link(dve, last)

        @block.gpsimd
        def _(pool):
            pool.memset(s.upto[:, :, :], 1.0)
            pool.memset(s.since[:, :, :], 1.0).then_inc(masks, 1)
            pool.wait_ge(masks, 1)
            pool.affine_select(out=s.upto[:, :, :], in_=s.upto[:, :, :], compare_op=ALU.is_ge, fill=0.0,
                               base=0, pattern=[[-P, len(TT)], [1, T]], channel_multiplier=-1)
            pool.affine_select(out=s.since[:, :, :], in_=s.since[:, :, :], compare_op=ALU.is_ge, fill=0.0,
                               base=0, pattern=[[P, len(TT)], [-1, T]], channel_multiplier=1)\
                .then_inc(masks, 1)

        @block.scalar
        def _(act):
            act.activation(s.a_exp[:, :], s.col("a_log"), ACT.Exp)

    softplus(nc, s, "dt", dt[:, :, :], dt[:, :, :], s.xd[:, 0:4 * 192], (3, 64))

    with nc.Block() as block:

        @block.vector
        def _(dve):
            for j in range(3):
                last = dve.scalar_tensor_tensor(a[:, j, :], dt[:, j, :], -1.0, s.a_exp[:, :], ALU.mult, ALU.mult)
            last.then_inc(a_ready, 1)
            dve.wait_ge(summed, 1)
            dve.tensor_copy(s.csT[:, :], s.ps[0:64, 0, 0:T]).then_inc(sums_out, 1)
            dve.wait_ge(turned, 1)
            for j, (t0, n) in enumerate(TT):
                last = dve.tensor_scalar(s.neg_cs[0:n, j, :], s.ps[0:n, 1, 64 * j:64 * j + 64], -1.0, None, ALU.mult)
            s.dve.link(dve, last)
            for g in range(GROUPS):
                dve.wait_ge(cb, 3 * (g + 1))
                for j, (t0, n) in enumerate(TT):
                    for scan, mask, off in ((FWD, s.upto, 0), (BWD, s.since, SCAN_COLS[0])):
                        c0, width, at = scan[j]
                        last = dve.tensor_tensor(s.cb[0:n, g, off + at:off + at + width],
                                                 s.ps[0:n, 2 + (3 * g + j) % 3, c0:c0 + width],
                                                 mask[0:n, j, c0:c0 + width], ALU.mult)
                s.dve.step(last)
                last_cb = s.dve.n
                dve.wait_ge(s.dve.sem, last_cb)
                dve.sem_inc(s.cb_out, 1)

        @block.scalar
        def _(act):
            for j, (t0, n) in enumerate(TT):
                for q in range(IT // 4):
                    i = 4 * j + q
                    act.wait_ge(xt, i + 1)
                    act.activation(s.x_tok[0:n, j, 512 * q:512 * q + 512], s.ps[0:n, 5 + i % 3, :], ACT.Copy)\
                       .then_inc(xt_out, 1)
            act.wait_ge(xt_out, 12)

        @block.tensor
        def _(pe):
            pe.wait_ge(a_ready, 1)
            for d, mask in ((0, s.upto), (1, s.since)):
                for j, (t0, n) in enumerate(TT):
                    last = pe.matmul(s.ps[32 * d:32 * d + 32, 0, 0:T], a[0:n, j, 32 * d:32 * d + 32],
                                     mask[0:n, j, :], start=j == 0, stop=j == 2)
            last.then_inc(summed, 1)
            for g in range(GROUPS):
                for j, (t0, n) in enumerate(TT):
                    if g:
                        pe.wait_ge(s.cb_out, g)
                    pe.matmul(s.ps[0:n, 2 + (3 * g + j) % 3, 0:T], s.xbc[:, IT + g, t0:t0 + n],
                              s.xbc[:, IT + GROUPS + g, :], start=True, stop=True).then_inc(cb, 1)
                if g == 0:
                    pe.wait_ge(sums_out, 1)
                    for j, (t0, n) in enumerate(TT):
                        last = pe.matmul(s.ps[0:n, 1, 64 * j:64 * j + 64], s.csT[:, t0:t0 + n],
                                         s.ident[0:64, 0:64], is_transpose=True, start=True, stop=True)
                    last.then_inc(turned, 1)
            for j, (t0, n) in enumerate(TT):
                for q in range(IT // 4):
                    i = 4 * j + q
                    if i >= 3:
                        pe.wait_ge(xt_out, i - 2)
                    for r in range(4):
                        last = pe.matmul(s.ps[0:n, 5 + i % 3, P * r:P * r + P], s.xbc[:, 4 * q + r, t0:t0 + n],
                                         s.ident[:, :], is_transpose=True, start=True, stop=True)
                    last.then_inc(xt, 1)


def ssd_scan(nc, s):
    row, held, decayed, weighted, scaled, head_done, y_mid, y_out = (
        s.sem(f"scan_{k}") for k in ("row", "held", "decayed", "weighted", "scaled", "head_done", "y_mid", "y_out"))
    PASSES = 2 * HEADS
    AHEAD = 2
    ROWS = 4
    XD = 4

    SPANS = [((P, 0, scan[2][2]), (TT[2][1], scan[2][2], scan[2][2] + scan[2][1])) for scan in SCANS]

    def span_held(i, rows):
        return 3 * i + (2 if rows == P else 3)

    def xd(i):
        return s.xd[:, (i % XD) * 192:(i % XD) * 192 + 192].rearrange("p (j c) -> p j c", j=3)

    with nc.Block() as block:

        @block.tensor
        def _(pe):
            def decay_row(i):
                h, d = i // 2, i % 2
                if i >= ROWS:
                    pe.wait_ge(held, 3 * (i - ROWS + 1))
                pe.matmul(s.ps[:, i % ROWS, 0:T], s.ident[0:64, 32 * d + h:32 * d + h + 1].to_broadcast([64, P]),
                          s.csT[:, :], start=True, stop=True).then_inc(row, 1)

            for i in range(AHEAD):
                decay_row(i)
            for i in range(PASSES):
                h, d = i // 2, i % 2
                if i + AHEAD < PASSES:
                    decay_row(i + AHEAD)
                if h % 2 == 0 and d == 0 and h >= 4:
                    pe.wait_ge(y_out, h // 2 - 1)
                out = s.ps[64 * (h % 2):64 * (h % 2) + 64, 4 + h // 2 % 2, :]
                pe.wait_ge(scaled, i + 1)
                pe.wait_ge(weighted, 2 * (i + 1))
                for j, (t0, n) in enumerate(TT):
                    c0, width, at = SCANS[d][j]
                    last = pe.matmul(out[:, c0:c0 + width], xd(i)[0:n, j, :], s.decay[0:n, i % DECAYS, at:at + width],
                                     start=d == 0 and j == 0, stop=d == 1 and j == 2, skip_group_check=True)
                last.then_inc(head_done, 1)

        @block.scalar
        def _(act):
            for i in range(PASSES):
                h, d = i // 2, i % 2
                for rows, c0, c1 in SPANS[d]:
                    act.wait_ge(held, span_held(i, rows))
                    act.activation(s.decay[0:rows, i % DECAYS, c0:c1], s.decay[0:rows, i % DECAYS, c0:c1],
                                   ACT.Exp).then_inc(decayed, 1)

        @block.gpsimd
        def _(pool):
            for i in range(PASSES):
                h, d = i // 2, i % 2
                if i >= XD:
                    pool.wait_ge(head_done, i - XD + 1)
                for j, (t0, n) in enumerate(TT):
                    last = pool.tensor_scalar(xd(i)[0:n, j, :], s.x_tok[0:n, j, 64 * h:64 * h + 64],
                                              s.dt[0:n, j, 32 * d + h:32 * d + h + 1], None, ALU.mult)
                last.then_inc(scaled, 1)

        @block.vector
        def _(dve):
            def finish(m):
                dve.wait_ge(head_done, 4 * (m + 1))
                dve.scalar_tensor_tensor(s.xbc[:, m, :], s.xbc[:, m, :], s.col("ssm_d")[:, m:m + 1],
                                         s.ps[:, 4 + m % 2, 0:T], ALU.mult, ALU.add).then_inc(y_out, 1)
                dve.wait_ge(y_out, m + 1)
                dve.tensor_tensor(s.xbc[:, m, :], s.xbc[:, m, :], s.zs[:, m, :], ALU.mult).then_inc(y_mid, 1)

            def exponents(i):
                h, d = i // 2, i % 2
                dve.wait_ge(row, i + 1)
                if i >= DECAYS:
                    dve.wait_ge(head_done, i - DECAYS + 1)
                for j, (t0, n) in enumerate(TT):
                    c0, width, at = SCANS[d][j]
                    dve.tensor_scalar(s.decay[0:n, i % DECAYS, at:at + width], s.ps[0:n, i % ROWS, c0:c0 + width],
                                      s.neg_cs[0:n, j, 32 * d + h:32 * d + h + 1], 0.0, ALU.add, ALU.min)\
                       .then_inc(held, 1)

            exponents(0)
            for i in range(PASSES):
                h, d = i // 2, i % 2
                off = d * SCAN_COLS[0]
                if i + 1 < PASSES:
                    exponents(i + 1)
                for q, (rows, c0, c1) in enumerate(SPANS[d]):
                    dve.wait_ge(decayed, 2 * i + q + 1)
                    dve.tensor_tensor(s.decay[0:rows, i % DECAYS, c0:c1], s.decay[0:rows, i % DECAYS, c0:c1],
                                      s.cb[0:rows, h // 8, off + c0:off + c1], ALU.mult).then_inc(weighted, 1)
                if i % 4 == 1 and i > 4:
                    finish(i // 4 - 1)
            finish(HEADS // 2 - 1)
            dve.wait_ge(y_mid, HEADS // 2)


def conformer_norm(nc, s):
    c, n = s.conf, T
    squares = s.scratch[:, 0:KT * n].rearrange("p (k t) -> p k t", k=KT)
    summed, centred, squared, var, std = (s.sem(f"ln_{k}") for k in ("summed", "centred", "squared", "var", "std"))
    scaled, silus = s.sem("ln_scaled"), s.sem("ln_silu")
    with nc.Block() as block:

        @block.tensor
        def _(pe):
            for k in range(KT):
                last = pe.matmul(s.ps[:, 0, 0:n], s.ones[:, :], c[:, k, :], start=k == 0, stop=k == KT - 1)
            last.then_inc(summed, 1)
            pe.wait_ge(squared, 1)
            for k in range(KT):
                last = pe.matmul(s.ps[:, 1, 0:n], s.ones[:, :], squares[:, k, :], start=k == 0, stop=k == KT - 1)
            last.then_inc(var, 1)

        @block.vector
        def _(dve):
            dve.wait_ge(summed, 1)
            s.dve.link(dve, dve.tensor_scalar(s.std[:, 0:n], s.ps[:, 0, 0:n], 1.0 / D, None, ALU.mult))
            for k in range(KT):
                last = dve.tensor_tensor(c[:, k, :], c[:, k, :], s.std[:, 0:n], ALU.subtract)
            last.then_inc(centred, 1)
            dve.wait_ge(centred, 1)
            dve.wait_ge(std, 1)
            s.dve.link(dve, dve.reciprocal(s.std[:, 0:n], s.std[:, 0:n]))
            for k in range(KT):
                dve.scalar_tensor_tensor(c[:, k, :], c[:, k, :], s.col("ln_g")[:, k:k + 1], s.std[:, 0:n],
                                         ALU.mult, ALU.mult).then_inc(scaled, 1)

        @block.scalar
        def _(act):
            act.wait_ge(centred, 1)
            act.activation(squares, c[:, :, :], ACT.Square).then_inc(squared, 1)
            act.wait_ge(var, 1)
            act.activation(s.std[:, 0:n], s.ps[:, 1, 0:n], ACT.Sqrt, bias=s.eps[:, 0:1], scale=1.0 / D)\
               .then_inc(std, 1)
            for k in range(KT):
                act.wait_ge(scaled, k + 1)
                act.activation(c[:, k, :], c[:, k, :], ACT.Silu, bias=s.col("ln_b")[:, k:k + 1]).then_inc(silus, 1)
            act.wait_ge(silus, KT)


def project(nc, s, name, units, tiles, src, n, evacuate):
    BANKS = 8
    tiled, out = s.sem(f"{name}_tiled"), s.sem(f"{name}_out")
    kt = src.shape[1]
    for i, (unit, _, _) in enumerate(tiles):
        s.w.freed[unit] = (tiled, i + 1)
    with nc.Block() as block:

        @block.sync
        def _(sp):
            s.w.refill(sp, units[0], len(units))

        @block.tensor
        def _(pe):
            for i, (unit, c, width) in enumerate(tiles):
                wt = s.w.wait(pe, unit)
                if i >= BANKS:
                    pe.wait_ge(out, i - BANKS + 1)
                for k in range(kt):
                    last = pe.matmul(s.ps[0:width, i % BANKS, 0:n], wt[:, k, c:c + width], src[:, k, :],
                                     start=k == 0, stop=k == kt - 1)
                last.then_inc(tiled, 1)

        @block.vector
        def _(dve):
            for i, (_, _, width) in enumerate(tiles):
                dve.wait_ge(tiled, i + 1)
                evacuate(dve, i, s.ps[0:width, i % BANKS, 0:n]).then_inc(out, 1)
            dve.wait_ge(out, len(tiles))


def grid(first, tiles_per_unit, count):
    return [(first + m // tiles_per_unit, m % tiles_per_unit * P, P) for m in range(count)]


def mixer_out(nc, s):
    merged, gated = s.u, s.sem("branch_gated")
    u0 = s.conf_first
    project(nc, s, "conf_out", range(u0, u0 + 2), grid(u0, 4, KT), s.conf, T,
            lambda dve, m, prod: dve.tensor_tensor(merged[:, m, :], prod, s.gates[:, m, :], ALU.mult))

    def add_ssm(dve, m, prod):
        dve.tensor_tensor(s.gates[:, KT + m, :], prod, s.gates[:, KT + m, :], ALU.mult).then_inc(gated, 1)
        dve.wait_ge(gated, m + 1)
        return dve.tensor_tensor(merged[:, m, :], merged[:, m, :], s.gates[:, KT + m, :], ALU.add)

    project(nc, s, "ssm_out", range(u0 + 2, u0 + 6), grid(u0 + 2, 2, KT), s.xbc[:, 0:IT, :], T, add_ssm)
    project(nc, s, "mix_out", range(u0 + 6, u0 + 8), grid(u0 + 6, 4, KT), merged, T,
            lambda dve, m, prod: dve.tensor_tensor(s.h[:, m, :], s.h[:, m, :], prod, ALU.add))



SLOTS = EXPERTS * CAP
HALF = 64
PAIR = HALF + CAP
ROUNDS = -(-CAP // 8)


def route(nc, s):
    hn, aff, exp = s.u, s.aff, s.aff_exp
    names = ("logits", "copied", "shifted", "exp", "aff", "turned", "lists", "lists_t", "index_rows", "index_out",
             "onehot", "tok", "tok_out", "gathered", "gathered_out")
    (logits, copied, shifted, exped, aff_ready, turned, lists, lists_t, index_rows, index_out, onehot, tok, tok_out,
     gathered, gathered_out) = (s.sem(f"route_{k}") for k in names)
    wr = s.w_router

    with nc.Block() as block:

        @block.tensor
        def _(pe):
            pe.wait_ge(s.router_in, 16)
            for j, (t0, n) in enumerate(TT):
                for k in range(KT):
                    last = pe.matmul(s.ps[0:n, 0, EXPERTS * j:EXPERTS * j + EXPERTS], hn[:, k, t0:t0 + n], wr[:, k, :],
                                     start=k == 0, stop=k == KT - 1)
            last.then_inc(logits, 1)
            for j, (t0, n) in enumerate(TT):
                for q in range(2):
                    i = 2 * j + q
                    if i >= 3:
                        pe.wait_ge(tok_out, i - 2)
                    for r in range(4):
                        last = pe.matmul(s.ps[0:n, 5 + i % 3, P * r:P * r + P], hn[:, 4 * q + r, t0:t0 + n],
                                         s.ident[:, :], is_transpose=True, start=True, stop=True)
                    last.then_inc(tok, 1)
            pe.wait_ge(aff_ready, 1)
            for j, (t0, n) in enumerate(TT):
                last = pe.matmul(s.ps[0:EXPERTS, 1, t0:t0 + n], aff[0:n, j, :], s.ident[0:n, 0:n],
                                 is_transpose=True, start=True, stop=True)
            last.then_inc(turned, 1)
            pe.wait_ge(lists, 1)
            for q, rows in enumerate((s.index2, s.aff2)):
                last = pe.matmul(s.ps[0:PAIR, 2, EXPERTS * q:EXPERTS * q + EXPERTS], rows[:, :],
                                 s.ident[0:EXPERTS, 0:EXPERTS], is_transpose=True, start=True, stop=True)
            last.then_inc(lists_t, 1)
            for e in range(EXPERTS):
                last = pe.matmul(s.ps[:, 3 + e // 8, CAP * (e % 8):CAP * (e % 8) + CAP],
                                 s.ident[0:EXPERTS, e:e + 1].to_broadcast([EXPERTS, P]), s.index2[:, 0:CAP],
                                 start=True, stop=True)
            last.then_inc(index_rows, 1)
            pe.wait_ge(onehot, 1)
            pe.wait_ge(tok_out, 6)
            for half in range(2):
                for m in range(KT):
                    i = KT * half + m
                    if i >= 3:
                        pe.wait_ge(gathered_out, i - 2)
                    for j, (t0, n) in enumerate(TT):
                        last = pe.matmul(s.ps[:, 5 + i % 3, 0:SLOTS // 2], s.tok[0:n, j, P * m:P * m + P],
                                         s.onehot[0:n, j, SLOTS // 2 * half:SLOTS // 2 * (half + 1)],
                                         start=j == 0, stop=j == 2)
                    last.then_inc(gathered, 1)

        @block.scalar
        def _(act):
            for j, (t0, n) in enumerate(TT):
                for q in range(2):
                    i = 2 * j + q
                    act.wait_ge(tok, i + 1)
                    act.activation(s.tok[0:n, j, 512 * q:512 * q + 512], s.ps[0:n, 5 + i % 3, :], ACT.Copy)\
                       .then_inc(tok_out, 1)
            act.wait_ge(shifted, 1)
            act.activation(exp[:, :, :], exp[:, :, :], ACT.Exp).then_inc(exped, 1)
            for half in range(2):
                for m in range(KT):
                    i = KT * half + m
                    act.wait_ge(gathered, i + 1)
                    act.activation(s.picked[:, m, SLOTS // 2 * half:SLOTS // 2 * (half + 1)],
                                   s.ps[:, 5 + i % 3, 0:SLOTS // 2], ACT.Copy).then_inc(gathered_out, 1)
            act.wait_ge(gathered_out, 2 * KT)

        @block.vector
        def _(dve):
            link = lambda ins: s.dve.link(dve, ins)
            dve.memset(exp[:, :, :], 0.0)
            dve.memset(s.index2[:, :], -1.0)
            link(dve.memset(s.aff2[:, :], 0.0))
            dve.wait_ge(logits, 1)
            dve.tensor_copy(exp[:, 0:2, :], s.ps[:, 0, 0:2 * EXPERTS].rearrange("p (j e) -> p j e", j=2))
            link(dve.tensor_copy(exp[0:TT[2][1], 2, :], s.ps[0:TT[2][1], 0, 2 * EXPERTS:3 * EXPERTS]))
            link(dve.tensor_reduce(s.row3[:, 0:3], exp[:, :, :], AX_X, ALU.max))
            dve.tensor_tensor(exp[:, :, :], exp[:, :, :], s.row3[:, 0:3].unsqueeze(2).to_broadcast([P, 3, EXPERTS]),
                              ALU.subtract).then_inc(shifted, 1)
            dve.wait_ge(exped, 1)
            link(dve.tensor_reduce(s.row3[:, 0:3], exp[:, :, :], AX_X, ALU.add))
            link(dve.reciprocal(s.row3[:, 0:3], s.row3[:, 0:3]))
            dve.tensor_tensor(aff[:, :, :], exp[:, :, :], s.row3[:, 0:3].unsqueeze(2).to_broadcast([P, 3, EXPERTS]),
                              ALU.mult).then_inc(aff_ready, 1)
            dve.wait_ge(turned, 1)
            link(dve.tensor_copy(s.work[:, :], s.ps[0:EXPERTS, 1, 0:T]))
            for r in range(ROUNDS):
                at = slice(8 * r, 8 * r + 8)
                link(dve.max(s.top[:, at], s.work[:, :]))
                link(dve.max_index(s.top_at[:, at], s.top[:, at], s.work[:, :]))
                if r + 1 < ROUNDS:
                    link(dve.match_replace(s.work[:, :], s.top[:, at], s.work[:, :], -1.0))
            for c in (0, HALF):
                dve.tensor_copy(s.index2[:, c:c + CAP], s.top_at[:, 0:CAP])
                last = dve.tensor_copy(s.aff2[:, c:c + CAP], s.top[:, 0:CAP])
            last.then_inc(lists, 1)
            dve.wait_ge(lists_t, 1)
            link(dve.tensor_copy(s.list_t[:, :], s.ps[0:PAIR, 2, 0:2 * EXPERTS]))
            dve.wait_ge(index_rows, 1)
            for j in range(3):
                for half in range(2):
                    last = dve.tensor_scalar(s.onehot[:, j, SLOTS // 2 * half:SLOTS // 2 * (half + 1)],
                                             s.ps[:, 3 + half, 0:SLOTS // 2], s.row[:, j:j + 1], None, ALU.is_equal)
            last.then_inc(onehot, 1)


def expert_loader(s):
    def load(sp, e, u):
        i = s.expert_first + u
        if u < 8:
            src = (s.d["w_gate"], s.d["w_up"])[u // 2 % 2][e].rearrange("(k p) f -> p k f", p=P)
            c = FF // 2 * (u // 4) + 512 * (u % 2)
            src, a = src[:, :, c:c + 512], KT
        else:
            src, a = s.d["w_down"][e, 512 * (u - 8):512 * (u - 8) + 512, :].rearrange("(k p) n -> p k n", p=P), 4
        sp.dma_start(s.w.slots[:, i % RING, :].rearrange("p (a b) -> p a b", a=a), src).then_inc(s.w.arrived[i % RING], 16)

    return load


def experts(nc, s):
    names = ("picked", "products", "silu", "hidden", "turned", "turned_out", "down", "y", "onehot", "scattered", "added")
    (picked, products, silu, hidden, turned, turned_out, down, y_out, onehot, scattered, added) = (
        s.sem(f"expert_{k}") for k in names)
    w, u0, load = s.w, s.expert_first, s.w.load_expert_unit
    UNITS = 12

    def arrived(pe, e, u):
        i = u0 + u
        pe.wait_ge(w.arrived[i % RING], 16 * (i // RING + 1) + 16 * (UNITS // RING) * e)
        return w.slots[:, i % RING, :]

    def freed(sp, e, u):
        if u < 8:
            sp.wait_ge(products, 4 * e + u // 2 + 1 + FIRST)
        else:
            sp.wait_ge(down, 4 * e + u - 8 + 1 + FIRST)

    with nc.Block() as block:

        @block.sync
        def _(sp):
            with sp.Fori(0, EXPERTS - 1) as e:
                following = sp.snap(e + 1)
                for pair in range(0, UNITS, 2):
                    freed(sp, e, pair + 1)
                    for u in (pair + 1, pair):
                        load(sp, e if u + RING < UNITS else following, (u + RING) % UNITS)
            for u in range(UNITS):
                freed(sp, EXPERTS - 1, u)
                if u + RING < UNITS:
                    load(sp, EXPERTS - 1, u + RING)
                else:
                    w.fetch(sp, u0 + EXPERTS * UNITS + u + RING - UNITS)

        @block.gpsimd
        def _(pool):
            with pool.Fori(0, EXPERTS) as e:
                pool.wait_ge(products, 4 * e + FIRST)
                pool.tensor_copy(s.tokens[:, :, :], s.picked[:, :, bass.ds(e * CAP, CAP)]).then_inc(picked, 1)

        @block.tensor
        def _(pe):
            for sem in (products, turned, down, scattered):
                pe.sem_inc(sem, FIRST)
            with pe.Fori(0, EXPERTS) as e:
                pe.wait_ge(picked, e + 1)
                for c in range(2):
                    for q in range(2):
                        halves = [arrived(pe, e, 4 * c + 2 * q + j).rearrange("p (k f) -> p k f", k=KT) for j in range(2)]
                        for k in range(KT):
                            for j in range(2):
                                last = pe.matmul(s.ps[HALF * j:HALF * j + CAP, 2 * c + q, :], s.tokens[:, k, :],
                                                 halves[j][:, k, :], start=k == 0, stop=k == KT - 1)
                        last.then_inc(products, 1)
                for c in range(2):
                    pe.wait_ge(hidden, 2 * e + c + 1 + FIRST)
                    for q in range(4):
                        last = pe.matmul(s.ps[:, 4, PAIR * q:PAIR * q + PAIR], s.hidden[:, c, P * q:P * q + P],
                                         s.ident[0:PAIR, 0:PAIR], is_transpose=True, start=True, stop=True)
                    last.then_inc(turned, 1)
                    pe.wait_ge(turned_out, 2 * e + c + 1)
                    for j in range(2):
                        wd = arrived(pe, e, 8 + 2 * c + j).rearrange("p (q n) -> p q n", q=4)
                        for q in range(4):
                            for half in range(2):
                                last = pe.matmul(s.ps[HALF * half:HALF * half + CAP, 5, :],
                                                 s.hidden_t[:, c, q, HALF * j:HALF * j + CAP],
                                                 wd[:, q, 512 * half:512 * half + 512],
                                                 start=c + j + q == 0, stop=c == 1 and j == 1 and q == 3)
                        last.then_inc(down, 1)
                pe.wait_ge(y_out, e + 1)
                pe.wait_ge(onehot, e + 1)
                for m in range(KT):
                    r = HALF * (m // 4)
                    pe.wait_ge(added, KT * e + max(m - 1, 0) + FIRST)
                    pe.matmul(s.ps[:, 6 + m % 2, 0:T], s.y[r:r + CAP, P * (m % 4):P * (m % 4) + P],
                              s.spread[r:r + CAP, :], start=True, stop=True).then_inc(scattered, 1)

        @block.scalar
        def _(act):
            with act.Fori(0, EXPERTS) as e:
                for c in range(2):
                    act.wait_ge(products, 4 * e + 2 * c + 1 + FIRST)
                    act.wait_ge(hidden, 2 * e + FIRST)
                    act.activation(s.silu[:, c, :], s.ps[0:PAIR, 2 * c, :], ACT.Silu).then_inc(silu, 1)
                act.wait_ge(down, 4 * e + 4 + FIRST)
                act.wait_ge(scattered, KT * e + FIRST)
                act.activation(s.y[:, :], s.ps[0:PAIR, 5, :], ACT.Copy).then_inc(y_out, 1)

        @block.vector
        def _(dve):
            for sem in (hidden, added):
                dve.sem_inc(sem, FIRST)
            with dve.Fori(0, EXPERTS) as e:
                dve.wait_ge(scattered, KT * e + FIRST)
                dve.tensor_scalar(s.spread[:, :], s.iota[0:PAIR, :], s.list_t[:, bass.ds(e, 1)],
                                  s.list_t[:, bass.ds(e + EXPERTS, 1)], ALU.is_equal, ALU.mult).then_inc(onehot, 1)
                for c in range(2):
                    dve.wait_ge(silu, 2 * e + c + 1)
                    dve.wait_ge(products, 4 * e + 2 * c + 2 + FIRST)
                    dve.wait_ge(turned, 2 * e + FIRST)
                    dve.tensor_tensor(s.hidden[:, c, :], s.silu[:, c, :], s.ps[0:PAIR, 2 * c + 1, :], ALU.mult)\
                       .then_inc(hidden, 1)
                    dve.wait_ge(turned, 2 * e + c + 1 + FIRST)
                    dve.wait_ge(down, 4 * e + FIRST)
                    dve.tensor_copy(s.hidden_t[:, c, :, :], s.ps[:, 4, 0:4 * PAIR].rearrange("p (q t) -> p q t", q=4))\
                       .then_inc(turned_out, 1)
                for m in range(KT):
                    dve.wait_ge(scattered, KT * e + m + 1 + FIRST)
                    dve.tensor_tensor(s.h[:, m, :], s.h[:, m, :], s.ps[:, 6 + m % 2, 0:T], ALU.add).then_inc(added, 1)
            dve.wait_ge(added, KT * EXPERTS + FIRST)



GLA_HEADS, GLA_DK, GLA_DV = 4, 64, 128
GLA_BLOCK = 16
GLA_BLOCKS = SEQ // GLA_BLOCK
KEPT = [GLA_BLOCK * b * (b + 1) // 2 for b in range(GLA_BLOCKS + 1)]
LIMIT = 80.0
QT = SEQ // P
SWA_HEADS = 8


def by_tokens(nc, s):
    m1, w = s.m1, s.w
    done, out, alpha = s.sem("values_done"), s.sem("values_out"), s.sem("alpha_done")
    u_mix, u_v = s.in2_first + 3, s.in2_first + 4
    w.freed[u_mix] = w.freed[u_v] = (done, 4)
    with nc.Block() as block:

        @block.sync
        def _(sp):
            w.refill(sp, u_mix, 2)

        @block.tensor
        def _(pe):
            pe.wait_ge(s.alpha_in, 16)
            for m in range(2):
                last = pe.matmul(s.ps[:, 4 + m, 0:SEQ], s.gla_alpha[:, P * m:P * m + P], s.a_lr[:, :], start=True, stop=True)
            last.then_inc(alpha, 1)
            wm, wv = w.wait(pe, u_mix), w.wait(pe, u_v)
            for j in range(QT):
                for q, (wt, c0, n) in enumerate(((wv, 0, 512), (wm, P + 16, P))):
                    for k in range(KT):
                        last = pe.matmul(s.ps[:, 2 * j + q, 0:n], m1[:, k, P * j:P * j + P], wt[:, k, c0:c0 + n],
                                         start=k == 0, stop=k == KT - 1)
                    last.then_inc(done, 1)

        @block.scalar
        def _(act):
            for j in range(QT):
                act.wait_ge(done, 2 * j + 1)
                act.activation(s.v_gla[:, j, :], s.ps[:, 2 * j, :], ACT.Copy)
                act.wait_ge(done, 2 * j + 2)
                act.activation(s.v_swa[:, j, :], s.ps[:, 2 * j + 1, 0:P], ACT.Copy).then_inc(out, 1)
            act.activation(s.r_gla[:, :, :], s.r_gla[:, :, :], ACT.Silu)
            act.wait_ge(out, QT)

        @block.vector
        def _(dve):
            dve.memset(s.one_row[:, :], 1.0)
            dve.wait_ge(alpha, 1)
            for m in range(2):
                last = dve.tensor_scalar(s.cum[:, m, :], s.ps[:, 4 + m, 0:SEQ], s.col("gla_b")[:, m:m + 1], -1.0,
                                         ALU.add, ALU.mult)
            s.dve.link(dve, last)

    softplus(nc, s, "gla", s.cum[:, :, :], s.cum[:, :, :], s.scratch, (2, SEQ))


def linear_attention(nc, s):
    cum, names = s.cum, ("refs", "q_in", "q_exp", "q_out", "k_in", "k_exp", "k_out", "scores", "masked", "o", "o_copied",
                         "squared", "summed", "std", "done")
    refs, q_in, q_exp, q_out, k_in, k_exp, k_out, scores, masked, o_done, o_out, squared, summed, std, done = (
        s.sem(f"gla_{k}") for k in names)
    tiles = [(b, j) for b in range(GLA_BLOCKS) for j in range(QT) if GLA_BLOCK * (b + 1) > P * j]

    with nc.Block() as block:

        @block.vector
        def _(dve):
            link = lambda ins: s.dve.link(dve, ins)
            dve.memset(s.ps[:, 0:4, :], 0.0).then_inc(refs, 1)
            link(dve.tensor_scalar(cum[:, :, :], cum[:, :, :], -1.0 / 16.0, None, ALU.mult))
            for m in range(2):
                last = dve.tensor_tensor_scan(s.b[:, m, :], s.one_row[:, :], cum[:, m, :], 0.0, ALU.mult, ALU.add)
            link(last)
            b4 = s.b[:, :, :].rearrange("p m (b t) -> p (m b) t", t=GLA_BLOCK)
            ref = b4[:, :, GLA_BLOCK // 2:GLA_BLOCK // 2 + 1]
            link(dve.tensor_copy(s.ref[:, :], ref.rearrange("p a o -> p (a o)")))
            dq = s.dq[:, :, :].rearrange("p m (b t) -> p (m b) t", t=GLA_BLOCK)
            link(dve.tensor_tensor(dq, b4, s.ref[:, :].unsqueeze(2).to_broadcast([P, 2 * GLA_BLOCKS, GLA_BLOCK]),
                                   ALU.subtract))
            dve.tensor_scalar(s.dq[:, :, :], s.dq[:, :, :], LIMIT, None, ALU.min).then_inc(q_in, 1)
            for b in range(GLA_BLOCKS):
                n = GLA_BLOCK * (b + 1)
                for m in range(2):
                    last = dve.tensor_scalar(s.keys[:, m, KEPT[b]:KEPT[b] + n], s.b[:, m, 0:n],
                                             s.ref[:, m * GLA_BLOCKS + b:m * GLA_BLOCKS + b + 1], -LIMIT,
                                             ALU.subtract, ALU.max)
            last.then_inc(k_in, 1)
            dve.wait_ge(q_exp, 1)
            dve.tensor_tensor(s.dq[:, :, :], s.dq[:, :, :], s.qk_gla[:, 0:2, :], ALU.mult).then_inc(q_out, 1)
            for m in range(2):
                dve.wait_ge(k_exp, m + 1)
                for b in range(GLA_BLOCKS):
                    n = GLA_BLOCK * (b + 1)
                    last = dve.tensor_tensor(s.keys[:, m, KEPT[b]:KEPT[b] + n], s.keys[:, m, KEPT[b]:KEPT[b] + n],
                                             s.qk_gla[:, 2 + m, 0:n], ALU.mult)
                last.then_inc(k_out, 1)
            dve.wait_ge(done, 2)
            for h in range(GLA_HEADS):
                dve.wait_ge(scores, h + 1)
                dve.tensor_tensor(s.sc_gla[:, h, :, :], s.ps[:, h, :].rearrange("p (j t) -> p j t", j=QT),
                                  s.causal[:, :, :], ALU.mult).then_inc(masked, 1)
            dve.wait_ge(std, 1)
            link(dve.reciprocal(s.rstd_gla[:, :], s.rstd_gla[:, :]))
            for h in range(GLA_HEADS):
                last = dve.scalar_tensor_tensor(s.cat[:, h, :], s.cat[:, h, :], s.col("gla_norm")[:, h:h + 1],
                                                s.rstd_gla[:, h * SEQ:(h + 1) * SEQ], ALU.mult, ALU.mult)
            link(last)
            link(dve.tensor_tensor(s.cat[:, 0:4, :], s.cat[:, 0:4, :], s.r_gla[:, :, :], ALU.mult))

        @block.gpsimd
        def _(pool):
            pool.memset(s.causal[:, :, :], 1.0).then_inc(done, 1)
            pool.wait_ge(done, 1)
            pool.affine_select(out=s.causal[:, :, :], in_=s.causal[:, :, :], compare_op=ALU.is_ge, fill=0.0,
                               base=0, pattern=[[-P, QT], [1, SEQ]], channel_multiplier=-1).then_inc(done, 1)

        @block.scalar
        def _(act):
            act.wait_ge(q_in, 1)
            act.activation(s.dq[:, :, :], s.dq[:, :, :], ACT.Exp).then_inc(q_exp, 1)
            act.wait_ge(k_in, 1)
            for m in range(2):
                act.activation(s.keys[:, m, :], s.keys[:, m, :], ACT.Exp, scale=-1.0).then_inc(k_exp, 1)
            for h in range(GLA_HEADS):
                act.wait_ge(o_done, h + 1)
                act.activation(s.cat[:, h, :], s.ps[:, 4 + h % 2, 0:SEQ], ACT.Copy).then_inc(o_out, 1)
            act.wait_ge(o_out, GLA_HEADS)
            act.activation(s.sq_gla[:, :], s.cat[:, 0:4, :].rearrange("p h t -> p (h t)"), ACT.Square).then_inc(squared, 1)
            act.wait_ge(summed, 1)
            act.activation(s.rstd_gla[:, :], s.ps[:, 6:8, :].rearrange("p a b -> p (a b)"), ACT.Sqrt,
                           bias=s.eps[:, 0:1], scale=1.0 / GLA_DV).then_inc(std, 1)

        @block.tensor
        def _(pe):
            pe.wait_ge(refs, 1)
            pe.wait_ge(q_out, 1)
            for h in range(GLA_HEADS):
                m, r = h // 2, 64 * (h % 2)
                if h % 2 == 0:
                    pe.wait_ge(k_out, m + 1)
                for b, j in tiles:
                    n = min(P, GLA_BLOCK * (b + 1) - P * j)
                    c = P * j + KEPT[b]
                    t0 = GLA_BLOCK * b
                    last = pe.matmul(s.ps[0:n, h, SEQ * j + t0:SEQ * j + t0 + GLA_BLOCK], s.keys[r:r + 64, m, c:c + n],
                                     s.dq[r:r + 64, m, t0:t0 + GLA_BLOCK], start=True, stop=True)
                last.then_inc(scores, 1)
            for h in range(GLA_HEADS):
                pe.wait_ge(masked, h + 1)
                if h >= 2:
                    pe.wait_ge(o_out, h - 1)
                for j in range(QT):
                    last = pe.matmul(s.ps[:, 4 + h % 2, 0:SEQ], s.v_gla[:, j, GLA_DV * h:GLA_DV * h + GLA_DV],
                                     s.sc_gla[:, h, j, :], start=j == 0, stop=j == QT - 1)
                last.then_inc(o_done, 1)
            pe.wait_ge(squared, 1)
            for q in range(2):
                last = pe.matmul(s.ps[:, 6 + q, :], s.ones[:, :], s.sq_gla[:, 512 * q:512 * q + 512], start=True, stop=True)
            last.then_inc(summed, 1)


def window_attention(nc, s):
    PARTS = ((0, P, P), (P, 2 * P, 0))
    names = ("consts", "far", "scores", "maxed", "exp", "normed", "turned", "copied", "o", "o_out", "shift")
    consts, far, scores, maxed, exped, normed, turned, copied, o_done, o_out, shift = (s.sem(f"swa_{k}") for k in names)
    W = 3 * P
    with nc.Block() as block:

        @block.gpsimd
        def _(pool):
            pool.iota(s.dist[:, :], pattern=[[-1, 2 * P]], base=P, channel_multiplier=1,
                      allow_small_or_imprecise_dtypes=True).then_inc(consts, 1)
            pool.wait_ge(consts, 1)
            pool.affine_select(out=s.dist[:, :], in_=s.dist[:, :], compare_op=ALU.is_ge, fill=-NEG,
                               base=P, pattern=[[-1, 2 * P]], channel_multiplier=1).then_inc(consts, 1)
            pool.wait_ge(consts, 2)
            pool.affine_select(out=s.dist[:, :], in_=s.dist[:, :], compare_op=ALU.is_ge, fill=-NEG,
                               base=-1, pattern=[[1, 2 * P]], channel_multiplier=-1).then_inc(far, 1)

        @block.tensor
        def _(pe):
            for h in range(SWA_HEADS):
                r, m = 64 * (h // 4), h % 4
                pe.matmul(s.ps[:, h, 0:P], s.q_swa[r:r + 64, m, 0:P], s.k_swa[r:r + 64, 0:P], start=True, stop=True)
                pe.matmul(s.ps[:, h, P:W], s.q_swa[r:r + 64, m, P:SEQ], s.k_swa[r:r + 64, 0:SEQ],
                          start=True, stop=True).then_inc(scores, 1)
            for h in range(SWA_HEADS):
                r, m = 64 * (h // 4), h % 4
                pe.wait_ge(normed, h + 1)
                if h >= 2:
                    pe.wait_ge(copied, h - 1)
                for q in range(3):
                    last = pe.matmul(s.ps[:, h % 2, P * q:P * q + P], s.sc_swa[:, h, P * q:P * q + P], s.ident[:, :],
                                     is_transpose=True, start=True, stop=True)
                last.then_inc(turned, 1)
                pe.wait_ge(copied, h + 1)
                out, v = s.ps[r:r + 64, 4 + m, :], s.v_swa
                pe.matmul(out[:, 0:P], v[:, 0, r:r + 64], s.p_t[:, h % 2, 0:P], start=True, stop=True)
                pe.matmul(out[:, P:SEQ], v[:, 0, r:r + 64], s.p_t[:, h % 2, P:2 * P], start=True, stop=False)
                pe.matmul(out[:, P:SEQ], v[:, 1, r:r + 64], s.p_t[:, h % 2, 2 * P:W], start=False, stop=True)\
                  .then_inc(o_done, 1)

        @block.vector
        def _(dve):
            link = lambda ins: s.dve.link(dve, ins)
            dve.wait_ge(far, 1)
            for h in range(SWA_HEADS):
                dve.wait_ge(scores, h + 1)
                for c, n, c0 in PARTS:
                    last = dve.scalar_tensor_tensor(s.sc_swa[:, h, c:c + n], s.dist[:, c0:2 * P],
                                                    -(2.0 ** -(h + 1)), s.ps[:, h, c:c + n], ALU.mult, ALU.add)
            link(last)
            for q, (c, n, _) in enumerate(PARTS):
                last = dve.tensor_reduce(s.max_swa[:, q, :], s.sc_swa[:, :, c:c + n], AX_X, ALU.max)
            link(last)
            for q in range(2):
                last = dve.tensor_tensor(s.max_swa[:, q, :], s.max_swa[:, q, :], s.col("sinks"), ALU.max)
            link(last)
            for q in range(2):
                last = dve.tensor_tensor(s.sink[:, q, :], s.col("sinks"), s.max_swa[:, q, :], ALU.subtract)
            link(last)
            dve.tensor_scalar(s.max_swa[:, :, :], s.max_swa[:, :, :], -1.0, None, ALU.mult).then_inc(maxed, 1)
            dve.wait_ge(exped, 1)
            link(dve.tensor_tensor(s.sum_swa[:, :, :], s.sum_swa[:, :, :], s.sink[:, :, :], ALU.add))
            link(dve.reciprocal(s.sum_swa[:, :, :], s.sum_swa[:, :, :]))
            for h in range(SWA_HEADS):
                for q, (c, n, _) in enumerate(PARTS):
                    last = dve.tensor_scalar(s.sc_swa[:, h, c:c + n], s.sc_swa[:, h, c:c + n],
                                             s.sum_swa[:, q, h:h + 1], None, ALU.mult)
                last.then_inc(normed, 1)
            for m in range(4):
                dve.wait_ge(o_done, m + 5)
                last = dve.tensor_copy(s.cat[:, 4 + m, :], s.ps[:, 4 + m, 0:SEQ])
            link(last)

        @block.scalar
        def _(act):
            act.wait_ge(maxed, 1)
            act.activation(s.sink[:, :, :], s.sink[:, :, :], ACT.Exp)
            for h in range(SWA_HEADS):
                for q, (c, n, _) in enumerate(PARTS):
                    last = act.activation(s.sc_swa[:, h, c:c + n], s.sc_swa[:, h, c:c + n], ACT.Exp,
                                          bias=s.max_swa[:, q, h:h + 1], accum_out=s.sum_swa[:, q, h:h + 1])
            last.then_inc(exped, 1)
            for h in range(SWA_HEADS):
                act.wait_ge(turned, h + 1)
                if h >= 2:
                    act.wait_ge(o_done, h - 1)
                act.activation(s.p_t[:, h % 2, :], s.ps[:, h % 2, 0:W], ACT.Copy).then_inc(copied, 1)


KEYS = 128
PEER_HEADS = 8
TOPK = 16
LISTS = PEER_HEADS * TOPK


def peer_lists(nc, s):
    link_of = lambda dve: (lambda ins: s.dve.link(dve, ins))
    names = ("scores", "scores_out", "shifted", "exp", "lists", "turned", "turned_out")
    scores, scores_out, shifted, exped, lists, turned, turned_out = (s.sem(f"peer_{k}") for k in names)
    lst = ("e1", "e2", "gate")

    with nc.Block() as block:

        @block.tensor
        def _(pe):
            pe.wait_ge(s.keys_in, 16)
            for j in range(QT):
                if j:
                    pe.wait_ge(scores_out, 4 * j)
                for half in range(2):
                    for h in range(PEER_HEADS):
                        last = pe.matmul(s.ps[:, 2 * half + h // 4, P * (h % 4):P * (h % 4) + P],
                                         s.q_peer[:, 2 * h + half, P * j:P * j + P], s.peer_keys[:, half, :],
                                         start=True, stop=True)
                        if h % 4 == 3:
                            last.then_inc(scores, 1)
            for j in range(QT):
                pe.wait_ge(lists, j + 1)
                for q, k in enumerate(lst):
                    last = pe.matmul(s.ps[:, 4 + j, P * q:P * q + P], s.lists[:, j, q, :], s.ident[:, :],
                                     is_transpose=True, start=True, stop=True)
                last.then_inc(turned, 1)

        @block.scalar
        def _(act):
            for j in range(QT):
                for q in range(4):
                    act.wait_ge(scores, 4 * j + q + 1)
                    act.activation(s.peer_s[:, j, 4 * q:4 * q + 4, :], s.ps[:, q, :].rearrange("p (h n) -> p h n", h=4),
                                   ACT.Copy).then_inc(scores_out, 1)
            for j in range(QT):
                act.wait_ge(shifted, j + 1)
                act.activation(s.lists[:, j, 2, :], s.lists[:, j, 2, :], ACT.Exp).then_inc(exped, 1)
            for j in range(QT):
                act.wait_ge(turned, j + 1)
                act.activation(s.lists_t[:, :, P * j:P * j + P], s.ps[:, 4 + j, 0:3 * P].rearrange("p (q t) -> p q t", q=3),
                               ACT.Copy).then_inc(turned_out, 1)
            act.wait_ge(turned_out, QT)

        @block.vector
        def _(dve):
            link = link_of(dve)

            def top16(values, best, where):
                n = len(values)
                for i in range(n):
                    last = dve.max(best[i][:, 0:8], values[i])
                link(last)
                for i in range(n):
                    last = dve.max_index(where[i][:, 0:8], best[i][:, 0:8], values[i])
                link(last)
                for i in range(n):
                    last = dve.match_replace(values[i], best[i][:, 0:8], values[i], -3.0e38)
                link(last)
                for i in range(n):
                    last = dve.max(best[i][:, 8:16], values[i])
                link(last)
                for i in range(n):
                    last = dve.max_index(where[i][:, 8:16], best[i][:, 8:16], values[i])
                link(last)

            for j in range(QT):
                dve.wait_ge(scores_out, 4 * (j + 1))
                if j:
                    dve.wait_ge(exped, j)
                L = 2 * PEER_HEADS
                top16([s.peer_s[:, j, i, :] for i in range(L)], [s.best[:, i, :] for i in range(L)],
                      [s.place[:, i, :] for i in range(L)])
                shape = [P, PEER_HEADS, TOPK, TOPK]
                v1, v2 = s.best[:, 0:PEER_HEADS, :], s.best[:, PEER_HEADS:L, :]
                dve.tensor_copy(s.place_f[:, :, :], s.place[:, :, :])
                link(dve.tensor_tensor(s.cand[:, :, :, :], v1.unsqueeze(3).to_broadcast(shape),
                                       v2.unsqueeze(2).to_broadcast(shape), ALU.add))
                flat = s.cand[:, :, :, :].rearrange("p h a b -> p h (a b)")
                gate = s.lists[:, j, 2, :].rearrange("p (h k) -> p h k", h=PEER_HEADS)
                top16([flat[:, h, :] for h in range(PEER_HEADS)], [gate[:, h, :] for h in range(PEER_HEADS)],
                      [s.pair[:, h, :] for h in range(PEER_HEADS)])
                dve.tensor_scalar(s.half_i[:, 0, :, :], s.pair[:, :, :], 4, None, ALU.logical_shift_right)
                link(dve.tensor_scalar(s.half_i[:, 1, :, :], s.pair[:, :, :], TOPK - 1, None, ALU.bitwise_and))
                link(dve.tensor_copy(s.half_f[:, :, :, :], s.half_i[:, :, :, :]))
                link(dve.tensor_copy(s.first[:, :], gate[:, :, 0:1].rearrange("p h o -> p (h o)")))
                dve.tensor_tensor(gate, gate, s.first[:, :].unsqueeze(2).to_broadcast([P, PEER_HEADS, TOPK]), ALU.subtract)\
                   .then_inc(shifted, 1)
                for q in range(2):
                    hit = s.cand[:, :, :, :]
                    link(dve.tensor_tensor(hit.rearrange("p h k a -> p (h k) a"),
                                           s.half_f[:, q, :, :].rearrange("p h k -> p (h k)").unsqueeze(2).to_broadcast([P, LISTS, TOPK]),
                                           s.iota[:, 0:TOPK].unsqueeze(1).to_broadcast([P, LISTS, TOPK]), ALU.is_equal))
                    link(dve.tensor_tensor(hit, hit, s.place_f[:, PEER_HEADS * q:PEER_HEADS * (q + 1), :].unsqueeze(2)
                                           .to_broadcast(shape), ALU.mult))
                    link(dve.tensor_reduce(s.lists[:, j, q, :], hit.rearrange("p h k a -> p (h k) a"), AX_X, ALU.add))
                dve.wait_ge(exped, j + 1)
                link(dve.tensor_reduce(s.first[:, :], gate, AX_X, ALU.add))
                link(dve.reciprocal(s.first[:, :], s.first[:, :]))
                dve.tensor_tensor(gate, gate, s.first[:, :].unsqueeze(2).to_broadcast([P, PEER_HEADS, TOPK]), ALU.mult)\
                   .then_inc(lists, 1)


TOKENS = 4
BODY = 2 * TOKENS


def peer_weights(nc, s):
    e1, e2, gate = (s.lists_t[:, q, :] for q in range(3))
    hot1, hot2, product, out = (s.sem(f"weights_{k}") for k in ("hot1", "hot2", "product", "out"))

    with nc.Block() as block:

        @block.sync
        def _(sp):
            for q in range(PEER_SLOTS):
                load_peer(s, sp, q)

        @block.vector
        def _(dve):
            with dve.Fori(0, SEQ // BODY) as g:
                for b in range(2):
                    dve.wait_ge(product, 2 * g + FIRST)
                    for t in range(TOKENS):
                        at = bass.ds(g * BODY + (b * TOKENS + t), 1)
                        last = dve.tensor_scalar(s.hot1[:, b, t, :], s.iota[:, 0:KEYS], e1[:, at], gate[:, at],
                                                 ALU.is_equal, ALU.mult)
                        last2 = dve.tensor_scalar(s.hot2[:, b, t, :], s.iota[:, 0:KEYS], e2[:, at], None, ALU.is_equal)
                    last.then_inc(hot1, 1)
                    last2.then_inc(hot2, 1)

        @block.tensor
        def _(pe):
            pe.sem_inc(product, FIRST)
            with pe.Fori(0, SEQ // BODY) as g:
                for b in range(2):
                    pe.wait_ge(hot1, 2 * g + b + 1)
                    pe.wait_ge(hot2, 2 * g + b + 1)
                    pe.wait_ge(out, 2 * g + FIRST)
                    for t in range(TOKENS):
                        last = pe.matmul(s.ps[:, b, P * t:P * t + P], s.hot1[:, b, t, :], s.hot2[:, b, t, :],
                                         start=True, stop=True)
                    last.then_inc(product, 1)

        @block.scalar
        def _(act):
            act.sem_inc(out, FIRST)
            with act.Fori(0, SEQ // BODY) as g:
                for b in range(2):
                    act.wait_ge(product, 2 * g + b + 1 + FIRST)
                    act.activation(s.weight[:, bass.ds(g * BODY + b * TOKENS, TOKENS), :],
                                   s.ps[:, b, :].rearrange("p (t e) -> p t e", t=TOKENS), ACT.Copy).then_inc(out, 1)
            act.wait_ge(out, SEQ // TOKENS + FIRST)


PEER_SLOTS = 4


def load_peer(s, sp, e2, q=None):
    q = e2 % PEER_SLOTS if q is None else q
    sp.dma_start(s.u_rows[:, q, :], s.d["peer_u"][e2]).then_inc(s.u_in[q], 16)
    sp.dma_start(s.v_rows[:, q, :], s.d["peer_v"][:, e2, :]).then_inc(s.v_in[q], 16)


def peer_experts(nc, s):
    names = ("hidden", "gelu", "weighted", "used", "zero", "y")
    hidden, gelu, weighted, used, zero, y_out = (s.sem(f"expert2_{k}") for k in names)
    GROUPS_OF_4 = KEYS // PEER_SLOTS
    m2 = s.m2

    def u_products(pe, g, q):
        g, q = (g + 1, 0) if q == PEER_SLOTS else (g, q)
        pe.wait_ge(s.u_in[q], 16 * g + 16)
        for k in range(KT):
            last = pe.matmul(s.ps[:, q % 2, 0:SEQ], s.u_rows[:, q, P * k:P * k + P], m2[:, k, :],
                             start=k == 0, stop=k == KT - 1)
        last.then_inc(hidden, 1)

    def v_products(pe, g, q, stop=False):
        pe.wait_ge(weighted, PEER_SLOTS * g + q + 1 + FIRST)
        pe.wait_ge(s.v_in[q], 16 * g + 16)
        for j in range(QT):
            for half in range(2):
                last = pe.matmul(s.ps[:, 4 + 2 * j + half, :], s.act2[:, q % 2, P * j:P * j + P],
                                 s.v_rows[:, q, 512 * half:512 * half + 512], start=False, stop=stop,
                                 skip_group_check=True)
        last.then_inc(used, 1)

    with nc.Block() as block:

        @block.sync
        def _(sp):
            with sp.Fori(0, GROUPS_OF_4 - 1) as g:
                for q in range(PEER_SLOTS):
                    sp.wait_ge(used, PEER_SLOTS * g + q + 1 + FIRST)
                    load_peer(s, sp, g * PEER_SLOTS + (PEER_SLOTS + q), q)

        @block.tensor
        def _(pe):
            pe.sem_inc(used, FIRST)
            pe.wait_ge(zero, 1)
            for bank in range(4):
                pe.matmul(s.ps[:, 4 + bank, :], s.zeros[:, 0:P], s.zeros[:, :], start=True, stop=False,
                          skip_group_check=True)
            u_products(pe, 0, 0)
            with pe.Fori(0, GROUPS_OF_4 - 1) as g:
                for q in range(PEER_SLOTS):
                    u_products(pe, g, q + 1)
                    v_products(pe, g, q)
            for q in range(PEER_SLOTS):
                if q + 1 < PEER_SLOTS:
                    u_products(pe, GROUPS_OF_4 - 1, q + 1)
                v_products(pe, GROUPS_OF_4 - 1, q, stop=q == PEER_SLOTS - 1)

        @block.scalar
        def _(act):
            with act.Fori(0, GROUPS_OF_4) as g:
                for q in range(PEER_SLOTS):
                    act.wait_ge(hidden, PEER_SLOTS * g + q + 1)
                    act.wait_ge(weighted, PEER_SLOTS * g + max(q - 1, 0) + FIRST)
                    act.activation(s.gelu2[:, q % 2, :], s.ps[:, q % 2, 0:SEQ], ACT.Gelu).then_inc(gelu, 1)
            act.wait_ge(used, KEYS + FIRST)
            for bank in range(4):
                act.activation(s.y2[:, bank // 2, 512 * (bank % 2):512 * (bank % 2) + 512], s.ps[:, 4 + bank, :],
                               ACT.Copy).then_inc(y_out, 1)
            act.wait_ge(y_out, 4)

        @block.vector
        def _(dve):
            dve.sem_inc(weighted, FIRST)
            dve.memset(s.zeros[:, :], 0.0).then_inc(zero, 1)
            with dve.Fori(0, GROUPS_OF_4) as g:
                for q in range(PEER_SLOTS):
                    dve.wait_ge(gelu, PEER_SLOTS * g + q + 1)
                    dve.wait_ge(used, PEER_SLOTS * g + max(q - 1, 0) + FIRST)
                    dve.tensor_tensor(s.act2[:, q % 2, :], s.gelu2[:, q % 2, :],
                                      s.weight[:, :, bass.ds(g * PEER_SLOTS + q, 1)].rearrange("p t o -> p (t o)"),
                                      ALU.mult).then_inc(weighted, 1)


def peer_residual(nc, s):
    turned, added = s.sem("resid_turned"), s.sem("resid_added")
    with nc.Block() as block:

        @block.tensor
        def _(pe):
            for k in range(KT):
                for j in range(QT):
                    last = pe.matmul(s.ps[:, k, P * j:P * j + P], s.y2[:, j, P * k:P * k + P], s.ident[:, :],
                                     is_transpose=True, start=True, stop=True)
                last.then_inc(turned, 1)

        @block.vector
        def _(dve):
            for k in range(KT):
                dve.wait_ge(turned, k + 1)
                dve.scalar_tensor_tensor(s.x[:, k, :], s.ps[:, k, 0:SEQ], s.mod[:, 5 * KT + k:5 * KT + k + 1],
                                         s.x[:, k, :], ALU.mult, ALU.add).then_inc(added, 1)
            dve.wait_ge(added, KT)


def second_block(nc, s, opener, first_part, stop):
    mod = lambda i: s.mod[:, KT * i:KT * i + KT]
    u0 = s.in2_first
    with ExitStack() as stage:
        sb = opener(stage)
        s.qk_gla, s.r_gla, s.q_swa = sb("qk_gla", [P, 4, SEQ]), sb("r_gla", [P, 4, SEQ]), sb("q_swa", [P, 4, SEQ])
        s.k_swa, s.a_lr, s.cat = sb("k_swa", [P, SEQ]), sb("a_lr", [16, SEQ]), sb("cat", [P, KT, SEQ])
        s.v_gla, s.v_swa = sb("v_gla", [P, QT, 512]), sb("v_swa", [P, QT, P])
        s.one_row, s.cum, s.b, s.dq = sb("one_row", [P, SEQ]), sb("cum", [P, 2, SEQ]), sb("b", [P, 2, SEQ]), sb("dq", [P, 2, SEQ])
        s.scratch = sb("scratch_2", [P, KT * T])
        s.gla_alpha = sb("gla_alpha", [16, 2 * P])
        s.alpha_in = start_load(nc, s, "alpha", s.gla_alpha[:, :], s.d["gla_alpha"])
        rms(nc, s, "final_norm", s.h[:, :, META:T], s.col("norm_final"), s.x, KT, SEQ)
        rms(nc, s, "norm1", s.x[:, :, :], s.col("norm1"), s.m1, KT, SEQ, gain=mod(1), shift=mod(0))
        tiles = grid(u0, 4, 12) + [(u0 + 3, 0, P), (u0 + 3, P, 16)]

        def evacuate(dve, i, prod):
            if i < 2 or 8 <= i < 12:
                out = s.qk_gla[:, i, :] if i < 2 else s.q_swa[:, i - 8, :]
                return dve.tensor_scalar(out, prod, 0.125, None, ALU.mult)
            out = s.qk_gla[:, i, :] if i < 4 else s.r_gla[:, i - 4, :] if i < 8 else s.k_swa[:, :] if i == 12 else s.a_lr[:, :]
            return dve.tensor_copy(out, prod)

        project(nc, s, "in2", range(u0, u0 + 3), tiles, s.m1, SEQ, evacuate)
        by_tokens(nc, s)
        if stop == "in2":
            return
        with ExitStack() as inner:
            sb = opener(inner)
            s.ref, s.keys = sb("ref", [P, 2 * GLA_BLOCKS]), sb("keys", [P, 2, KEPT[-1]])
            s.sc_gla, s.causal = sb("sc_gla", [P, GLA_HEADS, QT, SEQ]), sb("causal", [P, QT, SEQ])
            s.sq_gla, s.rstd_gla = s.scratch[:, 0:4 * SEQ], s.scratch[:, 4 * SEQ:8 * SEQ]
            linear_attention(nc, s)
        with ExitStack() as inner:
            sb = opener(inner)
            s.dist, s.sc_swa, s.p_t = sb("dist", [P, 2 * P]), sb("sc_swa", [P, SWA_HEADS, 3 * P]), sb("p_t", [P, 2, 3 * P])
            s.max_swa, s.sink, s.sum_swa = (sb(k, [P, 2, SWA_HEADS]) for k in ("max_swa", "sink", "sum_swa"))
            window_attention(nc, s)
        rms(nc, s, "swa_norm", s.cat[:, 4:8, :], s.col("swa_norm"), s.cat[:, 4:8, :], 4, SEQ)
        if stop == "cat":
            return
        project(nc, s, "out2", range(u0 + 5, u0 + 7), grid(u0 + 5, 4, KT), s.cat, SEQ,
                lambda dve, m, prod: dve.scalar_tensor_tensor(s.x[:, m, :], prod, mod(2)[:, m:m + 1], s.x[:, m, :],
                                                              ALU.mult, ALU.add))
        rms(nc, s, "norm2", s.x[:, :, :], s.col("norm2"), s.m2, KT, SEQ, gain=mod(4), shift=mod(3))
    if stop == "m2":
        return
    with ExitStack() as stage:
        sb = opener(stage)
        s.q_peer, s.peer_keys = sb("q_peer", [P, 2 * PEER_HEADS, SEQ]), sb("peer_keys", [P, 2, KEYS])
        s.keys_in = start_load(nc, s, "keys", s.peer_keys[:, :, :], s.d["peer_keys"].rearrange("a d n -> d a n"))
        project(nc, s, "peer_q", range(u0 + 7, u0 + 11), grid(u0 + 7, 4, 16), s.m2, SEQ,
                lambda dve, m, prod: dve.tensor_copy(s.q_peer[:, m, :], prod))
        s.peer_s = sb("peer_s", [P, QT, 2 * PEER_HEADS, KEYS])
        s.best, s.place = sb("best", [P, 2 * PEER_HEADS, TOPK]), sb("place", [P, 2 * PEER_HEADS, TOPK], U32)
        s.place_f, s.cand = sb("place_f", [P, 2 * PEER_HEADS, TOPK]), sb("cand", [P, PEER_HEADS, TOPK, TOPK])
        s.pair, s.half_i = sb("pair", [P, PEER_HEADS, TOPK], U32), sb("half_i", [P, 2, PEER_HEADS, TOPK], U32)
        s.half_f, s.first = sb("half_f", [P, 2, PEER_HEADS, TOPK]), sb("first", [P, PEER_HEADS])
        s.lists = sb("lists", [P, QT, 3, LISTS])
        peer_lists(nc, s)
    if stop == "lists":
        return
    first_part.close()
    with ExitStack() as stage:
        sb = opener(stage)
        s.weight = sb("weight", [P, SEQ, KEYS])
        s.u_rows, s.v_rows = sb("u_rows", [P, PEER_SLOTS, D]), sb("v_rows", [P, PEER_SLOTS, D])
        with ExitStack() as inner:
            hot = opener(inner)
            s.hot1, s.hot2 = hot("hot1", [P, 2, TOKENS, KEYS]), hot("hot2", [P, 2, TOKENS, KEYS])
            peer_weights(nc, s)
        s.zeros, s.gelu2, s.act2 = sb("zeros", [P, 512]), sb("gelu2", [P, 2, SEQ]), sb("act2", [P, 2, SEQ])
        s.y2 = sb("y2", [P, QT, D])
        peer_experts(nc, s)
        peer_residual(nc, s)
    with ExitStack() as stage:
        s.scratch = opener(stage)("scratch_3", [P, KT * SEQ])
        rms(nc, s, "out_norm", s.x[:, :, :], s.col("final_g"), s.x, KT, SEQ)


def build_program(nc, d, out, stop=None):
    s = Core()
    s.nc, s.d, s.out = nc, d, out
    with ExitStack() as whole:

        def opener(stack):
            return lambda name, shape, dt=F32: stack.enter_context(nc.sbuf_tensor(name, shape, dt))

        stage_sems = []
        s.sem = lambda name: whole.enter_context(nc.semaphore(name))
        s.ps = whole.enter_context(nc.psum_tensor("ps", [P, 8, 512], F32))
        keep = opener(whole)
        s.dve, s.const_set, s.small_in, s.cb_out = Chain(s.sem("dve_step")), s.sem("const_set"), s.sem("small_in"), s.sem("cb_out")
        s.small = keep("small", [P, SMALL_COLS])
        s.col = lambda name: s.small[:, SMALL[name][0]:SMALL[name][0] + SMALL[name][1]]
        s.ident, s.ones = keep("ident", [P, P]), keep("ones", [P, P])
        s.iota, s.row, s.eps = keep("iota", [P, T]), keep("row", [P, len(TT)]), keep("eps", [P, 1])
        s.std, s.gain, s.mod = keep("std", [P, T]), keep("gain", [P, KT]), keep("mod", [P, 48])

        s.h, s.u = keep("h", [P, KT, T]), keep("u", [P, KT, T])
        s.x, s.m1, s.m2 = s.h[:, :, META:T], s.u[:, :, 0:SEQ], s.u[:, :, 0:SEQ]
        s.lists_t = keep("lists_t", [P, 3, SEQ])
        s.u_in, s.v_in = ([s.sem(f"{k}_in{q}") for q in range(PEER_SLOTS)] for k in "uv")
        first_part = whole.enter_context(ExitStack())
        s.w = Weights(opener(first_part)("ring", [P, RING, SLOT]), [s.sem(f"slot{i}_in") for i in range(RING)])

        def stage_sem(name):
            stage_sems.append(nc.alloc_semaphore(name))
            return stage_sems[-1]

        s.sem = stage_sem
        plan_weights(s)
        s.w.load_expert_unit = expert_loader(s)

        with ExitStack() as mixer:
            sb = opener(mixer)
            s.zs, s.gates, s.conf = sb("zs", [P, IT, T]), sb("gates", [P, 2 * KT, T]), sb("conf", [P, KT, T])
            s.xbc, s.dt_raw = sb("xbc", [P, XT, T]), sb("dt_raw", [P, len(TT), 64])
            with ExitStack() as stage:
                sb = opener(stage)
                s.cpad, s.xpad = sb("cpad", [P, KT, T + 2 * CONF_PAD]), sb("xpad", [P, XT, T + 2 * SSM_PAD])
                s.sig, s.c_act = sb("sig", [P, 2, T]), sb("c_act", [P, KT])
                s.modrow, s.mod48 = sb("modrow", [P, 3, 512]), sb("mod48", [48, P])
                constants(nc, s)
                s.scratch = s.xbc[:, :, :].rearrange("p k t -> p (k t)")
                rms(nc, s, "mix_norm", s.h[:, :, :], s.col("norm_mix"), s.u, KT, T)
                in_projection(nc, s)
            if stop == "in":
                return finish(nc, s)
            with ExitStack() as stage:
                sb = opener(stage)
                s.x_tok = sb("x_tok", [P, len(TT), INNER])
                s.cb = sb("cb", [P, GROUPS, sum(SCAN_COLS)])
                s.decay = sb("decay", [P, DECAYS, max(SCAN_COLS)])
                flat = s.decay[:, :, :].rearrange("p a b -> p (a b)")
                s.upto, s.since = (flat[:, i * 3 * T:(i + 1) * 3 * T].rearrange("p (j t) -> p j t", j=3) for i in range(2))
                flat, at = s.u[:, :, :].rearrange("p k t -> p (k t)"), 0
                cut = {}
                for k, n in (("dt", 192), ("a", 192), ("neg_cs", 192), ("a_exp", 64), ("csT", T), ("xd", 4 * 192)):
                    cut[k], at = flat[:, at:at + n], at + n
                s.dt, s.a, s.neg_cs = (cut[k].rearrange("p (j h) -> p j h", j=3) for k in ("dt", "a", "neg_cs"))
                s.a_exp, s.csT, s.xd = cut["a_exp"], cut["csT"][0:64, :], cut["xd"]
                ssd_prepare(nc, s)
                if stop == "prep":
                    return finish(nc, s)
                ssd_scan(nc, s)
            if stop == "scan":
                return finish(nc, s)
            with ExitStack() as stage:
                s.scratch = opener(stage)("scratch", [P, IT * T])
                rms(nc, s, "ssm_norm", s.xbc[:, 0:IT, :], s.col("ssm_norm"), s.xbc[:, 0:IT, :], IT, T)
                conformer_norm(nc, s)
                mixer_out(nc, s)
        if stop == "mix":
            return finish(nc, s)
        s.w_router = opener(first_part)("w_router", [P, KT, EXPERTS])
        s.router_in = start_load(nc, s, "router", s.w_router[:, :, :], s.d["w_router"].rearrange("(k p) e -> p k e", p=P))
        with ExitStack() as stage:
            s.scratch = opener(stage)("scratch_ffn", [P, KT * T])
            rms(nc, s, "ffn_norm", s.h[:, :, :], s.col("norm_ffn"), s.u, KT, T)
        with ExitStack() as stage:
            sb = opener(stage)
            s.picked, s.list_t = sb("picked", [P, KT, SLOTS]), sb("list_t", [PAIR, 2 * EXPERTS])
            with ExitStack() as inner:
                sb = opener(inner)
                s.aff, s.aff_exp, s.row3 = sb("aff", [P, 3, EXPERTS]), sb("aff_exp", [P, 3, EXPERTS]), sb("row3", [P, 3])
                s.index2, s.aff2, s.work = sb("index2", [EXPERTS, PAIR]), sb("aff2", [EXPERTS, PAIR]), sb("work", [EXPERTS, T])
                s.top, s.top_at = sb("top", [EXPERTS, 8 * ROUNDS]), sb("top_at", [EXPERTS, 8 * ROUNDS], U32)
                s.tok, s.onehot = sb("tok", [P, 3, D]), sb("onehot", [P, 3, SLOTS])
                route(nc, s)
            if stop == "route":
                return finish(nc, s)
            sb = opener(stage)
            s.tokens, s.silu, s.hidden = sb("tokens", [P, KT, CAP]), sb("silu", [PAIR, 2, 512]), sb("hidden", [PAIR, 2, 512])
            s.hidden_t, s.y, s.spread = sb("hidden_t", [P, 2, 4, PAIR]), sb("y", [PAIR, 512]), sb("spread", [PAIR, T])
            clear_banks(nc, s)
            experts(nc, s)
        nc.clear_and_free_semaphores(list(stage_sems))
        nc.all_engine_barrier()
        second_block(nc, s, opener, first_part, stop)
        finish(nc, s)


def clear_banks(nc, s):
    with nc.Block() as block:

        @block.vector
        def _(dve):
            dve.memset(s.ps[0:P, 0:6, :], 0.0)


def plan_weights(s):
    w, d = s.w, s.d
    s.in_first = 0
    for c in range(0, 2 * D, 512):
        w.add_columns(d["w_in"], c, 512)
    for c in range(0, 6 * D, 512):
        w.add_columns(d["w_ada"], c, 512)
    for c in range(OFF_XBC, OFF_DT, 512):
        w.add_columns(d["w_in"], c, 512)
    w.add_columns(d["w_in"], OFF_DT, 2 * HEADS)
    for c in list(range(OFF_Z, OFF_XBC, 512)) + list(range(OFF_GATE, OFF_GATE + 2 * D, 512)):
        w.add_columns(d["w_in"], c, 512)
    s.conf_first = len(w.units)
    for c in range(0, D, 512):
        w.add_columns(d["w_conf_out"], c, 512)
    for c in range(0, D, 256):
        w.add_columns(d["w_ssm_out"], c, 256, IT)
    for c in range(0, D, 512):
        w.add_columns(d["w_out"], c, 512)
    s.expert_first = w.expert_first = len(w.units)
    for _ in range(12 * EXPERTS):
        w.add(None, 1, SLOT)
    s.in2_first = len(w.units)
    for c, n in ((0, 512), (512, 512), (1024, 512), (1536, 272), (1808, 512)):
        w.add_columns(d["w_in2"], c, n)
    for c in range(0, D, 512):
        w.add_columns(d["w_out2"], c, 512)
    for c in range(0, 2 * D, 512):
        w.add_columns(d["w_peer_q"], c, 512)


def finish(nc, s):
    done = s.sem("out_done")
    with nc.Block() as block:

        @block.sync
        def _(sp):
            for i in range(RING):
                n = sum(1 for u in range(s.w.loaded) if u % RING == i)
                sp.wait_ge(s.w.arrived[i], 16 * n)
            sp.dma_start(s.out.rearrange("(k p) t -> p k t", p=P), s.x[:, :, :]).then_inc(done, 16)
            sp.wait_ge(done, 16)


def declare(nc, arrays):
    d = {k: nc.dram_tensor(f"in_{k}", a.shape, mybir.dt.from_np(a.dtype), kind="ExternalInput").ap()
         for k, a in arrays.items()}
    return d, nc.dram_tensor("out_T", (D, SEQ), F32, kind="ExternalOutput").ap()


def layout(x):
    import numpy as np

    def cols(a):
        return np.asarray(a).reshape(-1, P).T

    def taps(a, kt):
        a = np.asarray(a)[0]
        return a.reshape(a.shape[0], kt, P).transpose(2, 1, 0).reshape(P, -1)

    def everywhere(a):
        a = np.asarray(a).reshape(1, -1)
        return np.broadcast_to(a, (P, a.shape[1]))

    order = [h for i in range(4) for h in (i, i + 4)]
    swa = np.concatenate([np.arange(64 * h, 64 * h + 64) for h in order])
    parts = {
        "norm_mix": cols(x["w_norm_mix"]), "conf_b": cols(x["b_conf_dw"]), "ln_g": cols(x["conf_ln_g"]),
        "ln_b": cols(x["conf_ln_b"]), "ssm_b": cols(x["b_ssm_conv"]),
        "ssm_d": cols(np.repeat(np.asarray(x["ssm_d"]).reshape(-1), HEAD_DIM)), "ssm_norm": cols(x["w_ssm_norm"]),
        "norm_ffn": cols(x["w_norm_ffn"]), "norm_final": cols(x["w_norm_final"]), "norm1": cols(x["norm1_g_2"]),
        "norm2": cols(x["norm2_g_2"]), "final_g": cols(x["final_g_2"]), "gla_norm": cols(x["gla_norm_g_2"]),
        "swa_norm": cols(np.asarray(x["swa_norm_g_2"])[0][swa]), "gla_b": cols(x["b_gla_alpha_2"]),
        "ada_b": cols(x["b_ada_2"]), "c": cols(x["c_2"]), "conf_w": taps(x["w_conf_dw"], KT),
        "ssm_w": taps(x["w_ssm_conv"], XT), "dt_bias": everywhere(x["ssm_dt_bias"]),
        "a_log": everywhere(x["ssm_a_log"]), "sinks": everywhere(x["swa_sinks_2"]),
    }
    small = np.concatenate([parts[k] for k in SMALL], axis=1)
    hT = np.concatenate([np.asarray(x["meta_tokens"]).T, np.asarray(x["x"])[0].T], axis=1)
    arrays = {"small": small, "hT": hT, "w_in": np.asarray(x["w_in"])[0], "w_ada": np.asarray(x["w_ada_2"])[0],
              "w_conf_out": np.asarray(x["w_conf_out"])[0], "w_ssm_out": np.asarray(x["w_ssm_out"])[0],
              "w_out": np.asarray(x["w_out"])[0], "w_router": np.asarray(x["w_router"])[0],
              "w_gate": np.asarray(x["w_exp_gate"])[0], "w_up": np.asarray(x["w_exp_up"])[0],
              "w_down": np.asarray(x["w_exp_down"])[0]}
    w_in2, w_out2 = np.asarray(x["w_in_2"])[0], np.asarray(x["w_out_2"])[0]
    q_g, v_g, a_lr, r_g, q_s, k_s, v_s = np.split(w_in2, [512, 1024, 1040, 1552, 2064, 2192], axis=1)
    arrays["w_in2"] = np.concatenate([q_g, r_g, q_s[:, swa], k_s, a_lr, v_s, v_g], axis=1)
    arrays["w_out2"] = np.concatenate([w_out2[:512], w_out2[512:][swa]], axis=0)
    arrays["w_peer_q"] = np.asarray(x["w_peer_q_2"])[0]
    arrays["gla_alpha"] = np.asarray(x["w_gla_alpha_2"])[0]
    arrays["peer_keys"] = np.stack([np.asarray(x["peer_keys_1_2"])[0].T, np.asarray(x["peer_keys_2_2"])[0].T])
    u = np.asarray(x["peer_u_2"])[0].reshape(KEYS, KEYS, KT, P)
    arrays["peer_u"] = u.transpose(1, 3, 2, 0).reshape(KEYS, P, D)
    arrays["peer_v"] = np.asarray(x["peer_v_2"])[0].reshape(KEYS, KEYS, D)
    return {k: np.ascontiguousarray(v) for k, v in arrays.items()}


def kernel(**inputs):
    import concourse.bacc as _bacc
    from concourse.bass_utils import run_bass_kernel_spmd as _run

    nc = _bacc.Bacc("TRN2", target_bir_lowering=False, num_devices=1)
    arrays = layout(inputs)
    build_program(nc, *declare(nc, arrays))
    r = _run(nc, [{f"in_{k}": a for k, a in arrays.items()}], core_ids=[0])
    return r.results[0]["out_T"].T.reshape(1, SEQ, D)
```

```python
from contextlib import ExitStack

import concourse.bass as bass
from concourse import mybir

P = 128
F32 = mybir.dt.float32
F32R = mybir.dt.float32r
U32 = mybir.dt.uint32
ACT = mybir.ActivationFunctionType
ALU = mybir.AluOpType
AX_X = mybir.AxisListType.X

D = 1024
KT = D // P
SEQ = 256
META = 16
T = META + SEQ
TT = ((0, 128), (128, 128), (256, T - 256))
EPS = 1e-6

CONF_TAPS = 31
CONF_PAD = CONF_TAPS // 2
SSM_TAPS = 7
SSM_PAD = SSM_TAPS // 2
INNER = 2 * D
HEADS = 32
HEAD_DIM = INNER // HEADS
GROUPS = 4
IT = INNER // P
XT = IT + 2 * GROUPS
OFF_G = D
OFF_Z = 2 * D
OFF_XBC = OFF_Z + INNER
OFF_DT = OFF_XBC + XT * P
OFF_GATE = OFF_DT + 2 * HEADS

EXPERTS = 16
CAP = 2 * T // EXPERTS
FF = 2 * D
FT = FF // P

FIRST = 1
RING = 4
SLOT = 4096
NEG = -1.0e30

SMALL = {}
for _name, _n in (("norm_mix", KT), ("conf_b", KT), ("ln_g", KT), ("ln_b", KT), ("ssm_b", XT), ("ssm_d", IT),
                  ("ssm_norm", IT), ("norm_ffn", KT), ("norm_final", KT), ("norm1", KT), ("norm2", KT),
                  ("final_g", KT), ("gla_norm", 4), ("swa_norm", 4), ("gla_b", 2), ("ada_b", 48), ("c", KT),
                  ("conf_w", KT * CONF_TAPS), ("ssm_w", XT * SSM_TAPS), ("dt_bias", 2 * HEADS),
                  ("a_log", 2 * HEADS), ("sinks", 8)):
    SMALL[_name] = (sum(n for _, n in SMALL.values()), _n)
SMALL_COLS = sum(n for _, n in SMALL.values())


class Chain:

    def __init__(self, sem):
        self.sem, self.n = sem, 0

    def step(self, ins):
        ins.then_inc(self.sem, 1)
        self.n += 1
        return self.n

    def link(self, eng, ins):
        self.step(ins)
        eng.wait_ge(self.sem, self.n)


class Weights:

    def __init__(self, slots, arrived):
        self.slots, self.arrived = slots, arrived
        self.loads = [0] * RING
        self.units = []
        self.ready = []
        self.freed = {}

    def add(self, src, a, b):
        slot = len(self.units) % RING
        self.loads[slot] += 1
        self.ready.append((self.arrived[slot], 16 * self.loads[slot]))
        self.units.append((src, a, b))

    def add_expert(self, u, expert_in):
        self.ready.append((expert_in[u], 16))
        self.units.append((None, u, 0))

    def add_columns(self, w, c0, n, kt=KT):
        return self.add(w.rearrange("(k p) n -> p k n", p=P)[:, :, c0:c0 + n], kt, n)

    def view(self, i):
        src, a, b = self.units[i]
        return self.slots[:, i % RING, 0:a * b].rearrange("p (a b) -> p a b", a=a)

    def load(self, sp, i):
        if i >= RING:
            sp.wait_ge(*self.freed[i - RING])
        self.fetch(sp, i)

    def fetch(self, sp, i):
        if i >= len(self.units):
            return
        src, u, _ = self.units[i]
        if src is None:
            self.load_expert_unit(sp, 0, u)
        else:
            sp.dma_start(self.view(i), src).then_inc(self.ready[i][0], 16)

    def refill(self, sp, first, count):
        for i in range(first, first + count):
            self.load(sp, i + RING)

    def wait(self, pe, i):
        pe.wait_ge(*self.ready[i])
        return self.view(i)


class Core:
    pass


def constants(nc, s):
    with nc.Block() as block:

        @block.gpsimd
        def _(pool):
            pool.memset(s.ident[:, :], 0.0)
            pool.memset(s.ones[:, :], 1.0).then_inc(s.const_set, 1)
            pool.wait_ge(s.const_set, 1)
            pool.affine_select(out=s.ident[:, :], in_=s.ident[:, :], compare_op=ALU.not_equal, fill=1.0,
                               base=0, pattern=[[-1, P]], channel_multiplier=1)
            pool.iota(s.iota[:, :], pattern=[[1, T]], base=0, channel_multiplier=0,
                      allow_small_or_imprecise_dtypes=True)
            pool.iota(s.row[:, :], pattern=[[P, len(TT)]], base=0, channel_multiplier=1,
                      allow_small_or_imprecise_dtypes=True).then_inc(s.const_set, 1)

        @block.vector
        def _(dve):
            dve.memset(s.eps[:, :], EPS)
            dve.memset(s.cpad[:, :, :], 0.0)
            dve.memset(s.xpad[:, :, :], 0.0)
            dve.memset(s.dt_raw[:, :, :], 0.0)

        @block.sync
        def _(sp):
            sp.dma_start(s.small[:, :], s.d["small"]).then_inc(s.small_in, 16)
            sp.dma_start(s.h[:, :, :], s.d["hT"].rearrange("(k p) t -> p k t", p=P)).then_inc(s.small_in, 16)
            for i in range(RING):
                s.w.load(sp, i)
            sp.wait_ge(s.small_in, 32)


def start_load(nc, s, name, dst, src):
    loaded = s.sem(f"{name}_in")
    with nc.Block() as block:

        @block.scalar
        def _(act):
            act.dma_start(dst, src).then_inc(loaded, 16)

    return loaded


def rms(nc, s, name, src, weight, dst, kt, n, gain=None, shift=None):
    squares = s.scratch[:, 0:kt * n].rearrange("p (k t) -> p k t", k=kt)
    sq_done, sum_done, std_done, scaled, out_done = (
        s.sem(f"{name}_{x}") for x in ("squared", "summed", "std", "scaled", "out"))
    total = s.ps[:, 0, 0:n]
    with nc.Block() as block:

        @block.scalar
        def _(act):
            for k in range(0, kt, 2):
                act.activation(squares[:, k:k + 2, :], src[:, k:k + 2, :], ACT.Square).then_inc(sq_done, 1)
            act.wait_ge(sum_done, 1)
            act.activation(s.std[:, 0:n], total, ACT.Sqrt, bias=s.eps[:, 0:1], scale=1.0 / (kt * P))\
               .then_inc(std_done, 1)
            if shift is not None:
                for k in range(kt):
                    act.wait_ge(scaled, k + 1)
                    act.activation(dst[:, k, :], dst[:, k, :], ACT.Identity, bias=shift[:, k:k + 1]).then_inc(out_done, 1)
                act.wait_ge(out_done, kt)

        @block.tensor
        def _(pe):
            for k in range(kt):
                if k % 2 == 0:
                    pe.wait_ge(sq_done, k // 2 + 1)
                last = pe.matmul(total, s.ones[:, :], squares[:, k, :], start=k == 0, stop=k == kt - 1)
            last.then_inc(sum_done, 1)

        @block.vector
        def _(dve):
            if gain is not None:
                s.dve.link(dve, dve.scalar_tensor_tensor(s.gain[:, 0:kt], gain, 1.0, weight, ALU.add, ALU.mult))
            w = weight if gain is None else s.gain
            dve.wait_ge(std_done, 1)
            s.dve.link(dve, dve.reciprocal(s.std[:, 0:n], s.std[:, 0:n]))
            for k in range(kt):
                dve.scalar_tensor_tensor(dst[:, k, :], src[:, k, :], w[:, k:k + 1], s.std[:, 0:n], ALU.mult, ALU.mult)\
                   .then_inc(scaled, 1)
            dve.wait_ge(scaled, kt)


def in_projection(nc, s):
    w = s.w
    BANKS = 4
    first = s.in_first
    UC = SLOT // KT
    TU = UC // P
    tiles = []
    u = first
    for kind, count in (("a", KT), ("g", KT), ("x", XT), ("dt", 0), ("z", IT), ("gate", IT)):
        if kind == "dt":
            tiles.append(("dt", 0, u, 0))
            u += 1
        for m in range(count):
            tiles.append((kind, m, u + m // TU, m % TU * P))
        u += count // TU
    tiled, evacuated = s.sem("in_tiled"), s.sem("in_evacuated")
    conv_done, xsilu = s.sem("conv_done"), s.sem("x_silu")
    pos = {(k, m): i for i, (k, m, _, _) in enumerate(tiles)}
    dve_glu = s.sem("glu_done")
    conf_done, summed, centred, squared, var, std, scaled, silus = (
        s.sem(f"ln_{k}") for k in ("conf", "summed", "centred", "squared", "var", "std", "scaled", "silu"))
    squares = s.cpad[:, :, 0:T]
    SUM_AT, SQUARE_AT, VAR_AT, STD_AT, SILU_AT = ("z", KT), ("gate", 7), ("gate", 8), ("gate", 10), ("gate", 14)
    for i, (_, _, unit, _) in enumerate(tiles):
        w.freed[unit] = (tiled, i + 1)

    def convolve(dve, padded, out, m0, taps, bias, n_taps):
        for j in range(n_taps):
            for m in range(m0, m0 + 8):
                tap = taps[:, m * n_taps + j:m * n_taps + j + 1]
                src = padded[:, m, j:j + T]
                if j == 0:
                    ins = dve.tensor_scalar(out[:, m, :], src, tap, bias[:, m:m + 1], ALU.mult, ALU.add)
                else:
                    dve.wait_ge(s.dve.sem, s.dve.n - 7)
                    ins = dve.scalar_tensor_tensor(out[:, m, :], src, tap, out[:, m, :], ALU.mult, ALU.add)
                s.dve.step(ins)
        dve.wait_ge(s.dve.sem, s.dve.n)

    with nc.Block() as block:

        @block.sync
        def _(sp):
            w.refill(sp, first, u - first)

        @block.tensor
        def _(pe):
            for i, (kind, m, unit, c) in enumerate(tiles):
                for at, ready, src, bank, done in ((SUM_AT, conf_done, s.conf, 4, summed), (VAR_AT, squared, squares, 5, var)):
                    if (kind, m) == at:
                        pe.wait_ge(ready, 1)
                        for k in range(KT):
                            last = pe.matmul(s.ps[:, bank, 0:T], s.ones[:, :], src[:, k, :], start=k == 0, stop=k == KT - 1)
                        last.then_inc(done, 1)
                wt = w.wait(pe, unit)
                if i >= BANKS:
                    pe.wait_ge(evacuated, i - BANKS + 1)
                bank = s.ps[:, i % BANKS, :]
                if kind == "dt":
                    for j, (t0, n) in enumerate(TT):
                        for k in range(KT):
                            last = pe.matmul(bank[0:n, j * 64:j * 64 + 64], s.u[:, k, t0:t0 + n], wt[:, k, :],
                                             start=k == 0, stop=k == KT - 1)
                else:
                    for k in range(KT):
                        last = pe.matmul(bank[:, 0:T], wt[:, k, c:c + P], s.u[:, k, :],
                                         start=k == 0, stop=k == KT - 1)
                last.then_inc(tiled, 1)

        @block.scalar
        def _(act):
            def x_silu():
                for g in range(XT // 8):
                    act.wait_ge(conv_done, g + 1)
                    act.activation(s.xbc[:, 8 * g:8 * g + 8, :], s.xbc[:, 8 * g:8 * g + 8, :], ACT.Silu).then_inc(xsilu, 1)

            for i, (kind, m, unit, c) in enumerate(tiles):
                if (kind, m) == SQUARE_AT:
                    act.wait_ge(centred, 1)
                    act.activation(squares, s.conf[:, :, :], ACT.Square).then_inc(squared, 1)
                elif (kind, m) == STD_AT:
                    act.wait_ge(var, 1)
                    act.activation(s.std[:, 0:T], s.ps[:, 5, 0:T], ACT.Sqrt, bias=s.eps[:, 0:1], scale=1.0 / D)\
                       .then_inc(std, 1)
                elif (kind, m) == SILU_AT:
                    for k in range(KT):
                        act.wait_ge(scaled, k + 1)
                        act.activation(s.conf[:, k, :], s.conf[:, k, :], ACT.Silu, bias=s.col("ln_b")[:, k:k + 1])\
                           .then_inc(silus, 1)
                act.wait_ge(tiled, i + 1)
                src = s.ps[:, i % BANKS, 0:T]
                if kind == "a":
                    ins = act.activation(s.cpad[:, m, CONF_PAD:CONF_PAD + T], src, ACT.Copy)
                elif kind == "g":
                    if m >= 2:
                        act.wait_ge(dve_glu, m - 1)
                    ins = act.activation(s.sig[:, m % 2, :], src, ACT.Sigmoid)
                elif kind == "x":
                    ins = act.activation(s.xpad[:, m, SSM_PAD:SSM_PAD + T], src, ACT.Copy)
                elif kind == "z":
                    ins = act.activation(s.zs[:, m, :], src, ACT.Silu)
                elif kind == "gate":
                    if m == 6:
                        x_silu()
                    ins = act.activation(s.gates[:, m, :], src, ACT.Sigmoid)
                else:
                    for j, (t0, n) in enumerate(TT):
                        ins = act.activation(s.dt_raw[0:n, j, :], s.ps[0:n, i % BANKS, j * 64:j * 64 + 64], ACT.Copy)
                ins.then_inc(evacuated, 1)
            act.wait_ge(xsilu, XT // 8)
            act.wait_ge(silus, KT)

        @block.vector
        def _(dve):
            for m in range(KT):
                dve.wait_ge(evacuated, pos["g", m] + 1)
                dve.tensor_tensor(s.cpad[:, m, CONF_PAD:CONF_PAD + T], s.cpad[:, m, CONF_PAD:CONF_PAD + T],
                                  s.sig[:, m % 2, :], ALU.mult).then_inc(dve_glu, 1)
            dve.wait_ge(dve_glu, KT)
            convolve(dve, s.cpad, s.conf, 0, s.col("conf_w"), s.col("conf_b"), CONF_TAPS)
            dve.sem_inc(conf_done, 1)
            for b in range(XT // 8):
                dve.wait_ge(evacuated, pos["x", 8 * b + 7] + 1)
                convolve(dve, s.xpad, s.xbc, 8 * b, s.col("ssm_w"), s.col("ssm_b"), SSM_TAPS)
                dve.sem_inc(conv_done, 1)
            c = s.conf
            dve.wait_ge(summed, 1)
            s.dve.link(dve, dve.tensor_scalar(s.std[:, 0:T], s.ps[:, 4, 0:T], 1.0 / D, None, ALU.mult))
            for k in range(KT):
                last = dve.tensor_tensor(c[:, k, :], c[:, k, :], s.std[:, 0:T], ALU.subtract)
            last.then_inc(centred, 1)
            dve.wait_ge(centred, 1)
            dve.wait_ge(std, 1)
            s.dve.link(dve, dve.reciprocal(s.std[:, 0:T], s.std[:, 0:T]))
            for k in range(KT):
                dve.scalar_tensor_tensor(c[:, k, :], c[:, k, :], s.col("ln_g")[:, k:k + 1], s.std[:, 0:T],
                                         ALU.mult, ALU.mult).then_inc(scaled, 1)



def softplus(nc, s, name, x, out, tmp, shape):
    free = shape[0] * shape[1]
    e, w, one, log = (tmp[:, i * free:(i + 1) * free].rearrange("p (a b) -> p a b", a=shape[0]) for i in range(4))
    neg, exp, w_out, log_out = (s.sem(f"{name}_{k}") for k in ("neg", "exp", "w", "log"))
    with nc.Block() as block:

        @block.vector
        def _(dve):
            dve.scalar_tensor_tensor(e, x, -1.0, x, ALU.mult, ALU.min).then_inc(neg, 1)
            dve.wait_ge(exp, 1)
            dve.tensor_scalar(w, e, 1.0, None, ALU.add).then_inc(w_out, 1)
            dve.wait_ge(w_out, 1)
            s.dve.link(dve, dve.tensor_scalar(one, w, 1.0, 0.0, ALU.subtract, ALU.is_equal))
            dve.wait_ge(log_out, 1)
            s.dve.link(dve, dve.tensor_tensor(log, log, one, ALU.add))
            s.dve.link(dve, dve.scalar_tensor_tensor(w, w, -1.0, one, ALU.add, ALU.add))
            s.dve.link(dve, dve.reciprocal(w, w))
            s.dve.link(dve, dve.tensor_tensor(log, log, w, ALU.mult))
            s.dve.link(dve, dve.tensor_tensor(log, log, e, ALU.mult))
            s.dve.link(dve, dve.scalar_tensor_tensor(out, x, 0.0, log, ALU.max, ALU.add))

        @block.scalar
        def _(act):
            act.wait_ge(neg, 1)
            act.activation(e, e, ACT.Exp).then_inc(exp, 1)
            act.wait_ge(w_out, 1)
            act.activation(log, w, ACT.Ln).then_inc(log_out, 1)


FWD, BWD = [], []
for _t0, _n in TT:
    FWD.append((_t0, T - _t0, sum(n for _, n, _ in FWD)))
    BWD.append((0, _t0 + _n, sum(n for _, n, _ in BWD)))
SCANS = (FWD, BWD)
SCAN_COLS = [sum(n for _, n, _ in scan) for scan in SCANS]
DECAYS = 4


def ssd_prepare(nc, s):
    dt, a = s.dt, s.a
    biased, a_ready, summed, turned, sums_out, xt, xt_out, cb, masks, aexp = (
        s.sem(f"ssd_{k}") for k in ("biased", "a", "summed", "turned", "sums_out", "xt", "xt_out", "cb", "masks", "aexp"))
    with nc.Block() as block:

        @block.vector
        def _(dve):
            for j in range(3):
                last = dve.tensor_tensor(dt[:, j, :], s.dt_raw[:, j, :], s.col("dt_bias"), ALU.add)
            s.dve.link(dve, last)

        @block.gpsimd
        def _(pool):
            pool.memset(s.upto[:, :, :], 1.0)
            pool.memset(s.since[:, :, :], 1.0).then_inc(masks, 1)
            pool.wait_ge(masks, 1)
            pool.affine_select(out=s.upto[:, :, :], in_=s.upto[:, :, :], compare_op=ALU.is_ge, fill=0.0,
                               base=0, pattern=[[-P, len(TT)], [1, T]], channel_multiplier=-1)
            pool.affine_select(out=s.since[:, :, :], in_=s.since[:, :, :], compare_op=ALU.is_ge, fill=0.0,
                               base=0, pattern=[[P, len(TT)], [-1, T]], channel_multiplier=1)\
                .then_inc(masks, 1)

        @block.scalar
        def _(act):
            act.activation(s.a_exp[:, :], s.col("a_log"), ACT.Exp)

    softplus(nc, s, "dt", dt[:, :, :], dt[:, :, :], s.xd[:, 0:4 * 192], (3, 64))

    with nc.Block() as block:

        @block.vector
        def _(dve):
            for j in range(3):
                last = dve.scalar_tensor_tensor(a[:, j, :], dt[:, j, :], -1.0, s.a_exp[:, :], ALU.mult, ALU.mult)
            last.then_inc(a_ready, 1)
            dve.wait_ge(summed, 1)
            dve.tensor_copy(s.csT[:, :], s.ps[0:64, 0, 0:T]).then_inc(sums_out, 1)
            dve.wait_ge(turned, 1)
            for j, (t0, n) in enumerate(TT):
                last = dve.tensor_scalar(s.neg_cs[0:n, j, :], s.ps[0:n, 1, 64 * j:64 * j + 64], -1.0, None, ALU.mult)
            s.dve.link(dve, last)
            for g in range(GROUPS):
                dve.wait_ge(cb, 3 * (g + 1))
                for j, (t0, n) in enumerate(TT):
                    for scan, mask, off in ((FWD, s.upto, 0), (BWD, s.since, SCAN_COLS[0])):
                        c0, width, at = scan[j]
                        last = dve.tensor_tensor(s.cb[0:n, g, off + at:off + at + width],
                                                 s.ps[0:n, 2 + (3 * g + j) % 3, c0:c0 + width],
                                                 mask[0:n, j, c0:c0 + width], ALU.mult)
                s.dve.step(last)
                last_cb = s.dve.n
                dve.wait_ge(s.dve.sem, last_cb)
                dve.sem_inc(s.cb_out, 1)

        @block.scalar
        def _(act):
            for j, (t0, n) in enumerate(TT):
                for q in range(IT // 4):
                    i = 4 * j + q
                    act.wait_ge(xt, i + 1)
                    act.activation(s.x_tok[0:n, j, 512 * q:512 * q + 512], s.ps[0:n, 5 + i % 3, :], ACT.Copy)\
                       .then_inc(xt_out, 1)
            act.wait_ge(xt_out, 12)

        @block.tensor
        def _(pe):
            pe.wait_ge(a_ready, 1)
            for d, mask in ((0, s.upto), (1, s.since)):
                for j, (t0, n) in enumerate(TT):
                    last = pe.matmul(s.ps[32 * d:32 * d + 32, 0, 0:T], a[0:n, j, 32 * d:32 * d + 32],
                                     mask[0:n, j, :], start=j == 0, stop=j == 2)
            last.then_inc(summed, 1)
            for g in range(GROUPS):
                for j, (t0, n) in enumerate(TT):
                    if g:
                        pe.wait_ge(s.cb_out, g)
                    pe.matmul(s.ps[0:n, 2 + (3 * g + j) % 3, 0:T], s.xbc[:, IT + g, t0:t0 + n],
                              s.xbc[:, IT + GROUPS + g, :], start=True, stop=True).then_inc(cb, 1)
                if g == 0:
                    pe.wait_ge(sums_out, 1)
                    for j, (t0, n) in enumerate(TT):
                        last = pe.matmul(s.ps[0:n, 1, 64 * j:64 * j + 64], s.csT[:, t0:t0 + n],
                                         s.ident[0:64, 0:64], is_transpose=True, start=True, stop=True)
                    last.then_inc(turned, 1)
            for j, (t0, n) in enumerate(TT):
                for q in range(IT // 4):
                    i = 4 * j + q
                    if i >= 3:
                        pe.wait_ge(xt_out, i - 2)
                    for r in range(4):
                        last = pe.matmul(s.ps[0:n, 5 + i % 3, P * r:P * r + P], s.xbc[:, 4 * q + r, t0:t0 + n],
                                         s.ident[:, :], is_transpose=True, start=True, stop=True)
                    last.then_inc(xt, 1)


def ssd_scan(nc, s):
    w, u_ada = s.w, s.ada_first
    c_ready, ada_done, ada_row, ada_sent, ada_t = (
        s.sem(f"ada_{k}") for k in ("c", "done", "row", "sent", "transposed"))
    ADA_PASSES = [range(22 * r + 4, 22 * r + 4 + KT) for r in range(3)]
    for n in range(12):
        w.freed[u_ada + n] = (ada_done, n // 4 + 1)
    row, held, decayed, weighted, weighted_last, scaled, head_done, y_mid, y_out = (
        s.sem(f"scan_{k}") for k in ("row", "held", "decayed", "weighted", "weighted_last", "scaled", "head_done", "y_mid",
                                     "y_out"))
    PASSES = 2 * HEADS
    AHEAD = 3
    ROWS = 4
    XD = 4

    SPANS = [((P, 0, scan[2][2]), (TT[2][1], scan[2][2], scan[2][2] + scan[2][1])) for scan in SCANS]

    def span_held(i, rows):
        return 3 * i + (2 if rows == P else 3)

    def weigh(eng, i, q):
        rows, c0, c1 = SPANS[i % 2][q]
        off = i % 2 * SCAN_COLS[0]
        return eng.tensor_tensor(s.decays[i % DECAYS][0:rows, c0:c1], s.decays[i % DECAYS][0:rows, c0:c1],
                                 s.cb[0:rows, i // 16, off + c0:off + c1], ALU.mult)

    def xd(i):
        return s.xd[:, (i % XD) * 192:(i % XD) * 192 + 192].rearrange("p (j c) -> p j c", j=3)

    def ada_products(pe, r, k):
        if k == 0:
            pe.wait_ge(c_ready, 1)
            for j in range(4):
                w.wait(pe, u_ada + 4 * r + j)
            if r == 2:
                pe.wait_ge(ada_row, 4)
        for j in range(4):
            last = pe.matmul(s.ps[32 * j:32 * j + 1, 6 + r % 2, :], s.c_act[:, k:k + 1],
                             w.view(u_ada + 4 * r + j)[:, k, :], start=k == 0, stop=k == KT - 1)
        if k == KT - 1:
            last.then_inc(ada_done, 1)

    with nc.Block() as block:

        @block.sync
        def _(sp):
            w.refill(sp, u_ada, 12)

        @block.tensor
        def _(pe):
            def decay_row(i):
                h, d = i // 2, i % 2
                if i >= ROWS:
                    pe.wait_ge(held, 3 * (i - ROWS + 1))
                pe.matmul(s.ps[:, i % ROWS, 0:T], s.ident[0:64, 32 * d + h:32 * d + h + 1].to_broadcast([64, P]),
                          s.csT[:, :], start=True, stop=True).then_inc(row, 1)

            for i in range(AHEAD):
                decay_row(i)
            for i in range(PASSES):
                h, d = i // 2, i % 2
                for r, at in enumerate(ADA_PASSES):
                    if i in at:
                        ada_products(pe, r, at.index(i))
                if i + AHEAD < PASSES:
                    decay_row(i + AHEAD)
                if h % 2 == 0 and d == 0 and h >= 4:
                    pe.wait_ge(y_out, h // 2 - 1)
                out = s.ps[64 * (h % 2):64 * (h % 2) + 64, 4 + h // 2 % 2, :]
                pe.wait_ge(scaled, i + 1)
                pe.wait_ge(weighted, i + 1)
                pe.wait_ge(weighted_last, i + 1)
                for j, (t0, n) in enumerate(TT):
                    c0, width, at = SCANS[d][j]
                    last = pe.matmul(out[:, c0:c0 + width], xd(i)[0:n, j, :], s.decays[i % DECAYS][0:n, at:at + width],
                                     start=d == 0 and j == 0, stop=d == 1 and j == 2, skip_group_check=True)
                last.then_inc(head_done, 1)
            pe.wait_ge(ada_sent, 16 * 12)
            pe.matmul(s.ps[:, 7, 0:48], s.mod48[0:48, :], s.ident[0:48, 0:48], is_transpose=True,
                      start=True, stop=True).then_inc(ada_t, 1)

        @block.scalar
        def _(act):
            def scale_x(i):
                h, d = i // 2, i % 2
                if i >= XD:
                    act.wait_ge(head_done, i - XD + 1)
                for j, (t0, n) in enumerate(TT):
                    last = act.activation(xd(i)[0:n, j, :], s.x_tok[0:n, j, 64 * h:64 * h + 64], ACT.Copy,
                                          scale=s.dt[0:n, j, 32 * d + h:32 * d + h + 1])
                last.then_inc(scaled, 1)

            act.activation(s.c_act[:, :], s.col("c"), ACT.Silu).then_inc(c_ready, 1)
            scale_x(0)
            for i in range(PASSES):
                h, d = i // 2, i % 2
                if i in (at.stop + 3 for at in ADA_PASSES):
                    r = i // 22
                    act.wait_ge(ada_done, r + 1)
                    for j in range(4):
                        act.activation(s.modrow[32 * j:32 * j + 1, r, :], s.ps[32 * j:32 * j + 1, 6 + r % 2, :],
                                       ACT.Copy).then_inc(ada_row, 1)
                    act.wait_ge(ada_row, 4 * r + 4)
                    for j in range(4):
                        n = 4 * r + j
                        act.dma_start(s.mod48[4 * n:4 * n + 4, :],
                                      s.modrow[32 * j:32 * j + 1, r, :].rearrange("o (q n) -> o q n", q=4))\
                           .then_inc(ada_sent, 16)
                for rows, c0, c1 in SPANS[d]:
                    act.wait_ge(held, span_held(i, rows))
                    act.activation(s.decays[i % DECAYS][0:rows, c0:c1], s.decays[i % DECAYS][0:rows, c0:c1],
                                   ACT.Exp).then_inc(decayed, 1)
                if i + 1 < PASSES:
                    scale_x(i + 1)

        @block.gpsimd
        def _(pool):
            for i in range(PASSES):
                pool.wait_ge(decayed, 2 * i + 1)
                weigh(pool, i, 0).then_inc(weighted, 1)

        @block.vector
        def _(dve):
            def finish(m):
                dve.wait_ge(head_done, 4 * (m + 1))
                dve.scalar_tensor_tensor(s.xbc[:, m, :], s.xbc[:, m, :], s.col("ssm_d")[:, m:m + 1],
                                         s.ps[:, 4 + m % 2, 0:T], ALU.mult, ALU.add).then_inc(y_out, 1)
                dve.wait_ge(y_out, m + 1)
                dve.tensor_tensor(s.xbc[:, m, :], s.xbc[:, m, :], s.zs[:, m, :], ALU.mult).then_inc(y_mid, 1)

            def exponents(i):
                h, d = i // 2, i % 2
                dve.wait_ge(row, i + 1)
                if i >= DECAYS:
                    dve.wait_ge(head_done, i - DECAYS + 1)
                for j, (t0, n) in enumerate(TT):
                    c0, width, at = SCANS[d][j]
                    dve.tensor_scalar(s.decays[i % DECAYS][0:n, at:at + width], s.ps[0:n, i % ROWS, c0:c0 + width],
                                      s.neg_cs[0:n, j, 32 * d + h:32 * d + h + 1], 0.0, ALU.add, ALU.min)\
                       .then_inc(held, 1)

            exponents(0)
            for i in range(PASSES):
                h, d = i // 2, i % 2
                if i + 1 < PASSES:
                    exponents(i + 1)
                dve.wait_ge(decayed, 2 * i + 2)
                weigh(dve, i, 1).then_inc(weighted_last, 1)
                if i % 4 == 1 and i > 4:
                    finish(i // 4 - 1)
            finish(HEADS // 2 - 1)
            dve.wait_ge(y_mid, HEADS // 2)
            dve.wait_ge(ada_t, 1)
            s.dve.link(dve, dve.tensor_tensor(s.mod[:, :], s.ps[:, 7, 0:48], s.col("ada_b"), ALU.add))


def project(nc, s, name, units, tiles, src, n, evacuate):
    BANKS = 8
    tiled, out = s.sem(f"{name}_tiled"), s.sem(f"{name}_out")
    kt = src.shape[1]
    for i, (unit, _, _) in enumerate(tiles):
        s.w.freed[unit] = (tiled, i + 1)
    with nc.Block() as block:

        @block.sync
        def _(sp):
            s.w.refill(sp, units[0], len(units))

        @block.tensor
        def _(pe):
            for i, (unit, c, width) in enumerate(tiles):
                wt = s.w.wait(pe, unit)
                if i >= BANKS:
                    pe.wait_ge(out, i - BANKS + 1)
                for k in range(kt):
                    last = pe.matmul(s.ps[0:width, i % BANKS, 0:n], wt[:, k, c:c + width], src[:, k, :],
                                     start=k == 0, stop=k == kt - 1)
                last.then_inc(tiled, 1)

        @block.vector
        def _(dve):
            for i, (_, _, width) in enumerate(tiles):
                dve.wait_ge(tiled, i + 1)
                evacuate(dve, i, s.ps[0:width, i % BANKS, 0:n]).then_inc(out, 1)
            dve.wait_ge(out, len(tiles))


def grid(first, tiles_per_unit, count):
    return [(first + m // tiles_per_unit, m % tiles_per_unit * P, P) for m in range(count)]


def mixer_out(nc, s):
    merged, gated = s.u, s.sem("branch_gated")
    u0 = s.conf_first
    project(nc, s, "conf_out", range(u0, u0 + 2), grid(u0, 4, KT), s.conf, T,
            lambda dve, m, prod: dve.tensor_tensor(merged[:, m, :], prod, s.gates[:, m, :], ALU.mult))

    def add_ssm(dve, m, prod):
        dve.tensor_tensor(s.gates[:, KT + m, :], prod, s.gates[:, KT + m, :], ALU.mult).then_inc(gated, 1)
        dve.wait_ge(gated, m + 1)
        return dve.tensor_tensor(merged[:, m, :], merged[:, m, :], s.gates[:, KT + m, :], ALU.add)

    project(nc, s, "ssm_out", range(u0 + 2, u0 + 6), grid(u0 + 2, 2, KT), s.xbc[:, 0:IT, :], T, add_ssm)
    project(nc, s, "mix_out", range(u0 + 6, u0 + 8), grid(u0 + 6, 4, KT), merged, T,
            lambda dve, m, prod: dve.tensor_tensor(s.h[:, m, :], s.h[:, m, :], prod, ALU.add))



SLOTS = EXPERTS * CAP
HALF = 64
PAIR = HALF + CAP
ROUNDS = -(-CAP // 8)


def route(nc, s):
    hn, aff, exp = s.u, s.aff, s.aff_exp
    names = ("logits", "copied", "shifted", "exp", "aff", "turned", "lists", "lists_t", "index_rows", "index_out",
             "onehot", "tok", "tok_out", "tok_rest", "gathered", "gathered_out")
    (logits, copied, shifted, exped, aff_ready, turned, lists, lists_t, index_rows, index_out, onehot, tok, tok_out, tok_rest,
     gathered, gathered_out) = (s.sem(f"route_{k}") for k in names)
    wr = s.w_router

    with nc.Block() as block:

        @block.sync
        def _(sp):
            for u in range(RING, EXPERT_RING):
                s.w.load_expert_unit(sp, 0, u)

        @block.tensor
        def _(pe):
            pe.wait_ge(s.router_in, 16)
            for j, (t0, n) in enumerate(TT):
                for k in range(KT):
                    last = pe.matmul(s.ps[0:n, 0, EXPERTS * j:EXPERTS * j + EXPERTS], hn[:, k, t0:t0 + n], wr[:, k, :],
                                     start=k == 0, stop=k == KT - 1)
            last.then_inc(logits, 1)
            for j, (t0, n) in enumerate(TT):
                for q in range(2):
                    i = 2 * j + q
                    if i >= 3:
                        pe.wait_ge(tok_out, i - 2)
                        pe.wait_ge(tok_rest, i - 2)
                    for r in range(4):
                        last = pe.matmul(s.ps[0:n, 5 + i % 3, P * r:P * r + P], hn[:, 4 * q + r, t0:t0 + n],
                                         s.ident[:, :], is_transpose=True, start=True, stop=True)
                    last.then_inc(tok, 1)
            pe.wait_ge(aff_ready, 1)
            for j, (t0, n) in enumerate(TT):
                last = pe.matmul(s.ps[0:EXPERTS, 1, t0:t0 + n], aff[0:n, j, :], s.ident[0:n, 0:n],
                                 is_transpose=True, start=True, stop=True)
            last.then_inc(turned, 1)
            pe.wait_ge(lists, 1)
            for q, rows in enumerate((s.index2, s.aff2)):
                last = pe.matmul(s.ps[0:PAIR, 2, EXPERTS * q:EXPERTS * q + EXPERTS], rows[:, :],
                                 s.ident[0:EXPERTS, 0:EXPERTS], is_transpose=True, start=True, stop=True)
            last.then_inc(lists_t, 1)
            for e in range(EXPERTS):
                last = pe.matmul(s.ps[:, 3 + e // 8, CAP * (e % 8):CAP * (e % 8) + CAP],
                                 s.ident[0:EXPERTS, e:e + 1].to_broadcast([EXPERTS, P]), s.index2[:, 0:CAP],
                                 start=True, stop=True)
            last.then_inc(index_rows, 1)
            pe.wait_ge(onehot, 1)
            pe.wait_ge(tok_rest, 6)
            for half in range(2):
                for m in range(KT):
                    i = KT * half + m
                    if i >= 3:
                        pe.wait_ge(gathered_out, i - 2)
                    for j, (t0, n) in enumerate(TT):
                        for part in (s.tok_hi, s.tok_lo):
                            last = pe.matmul(s.ps[:, 5 + i % 3, 0:SLOTS // 2], part[0:n, j, P * m:P * m + P],
                                             s.onehot[0:n, j, SLOTS // 2 * half:SLOTS // 2 * (half + 1)],
                                             start=j == 0 and part is s.tok_hi, stop=j == 2 and part is s.tok_lo)
                    last.then_inc(gathered, 1)

        @block.scalar
        def _(act):
            for j, (t0, n) in enumerate(TT):
                for q in range(2):
                    i = 2 * j + q
                    act.wait_ge(tok, i + 1)
                    act.activation(s.tok_hi[0:n, j, 512 * q:512 * q + 512], s.ps[0:n, 5 + i % 3, :], ACT.Copy)\
                       .then_inc(tok_out, 1)
            act.wait_ge(shifted, 1)
            act.activation(exp[:, :, :], exp[:, :, :], ACT.Exp).then_inc(exped, 1)
            for half in range(2):
                for m in range(KT):
                    i = KT * half + m
                    act.wait_ge(gathered, i + 1)
                    act.activation(s.picked[:, m, SLOTS // 2 * half:SLOTS // 2 * (half + 1)],
                                   s.ps[:, 5 + i % 3, 0:SLOTS // 2], ACT.Copy).then_inc(gathered_out, 1)
            act.wait_ge(gathered_out, 2 * KT)

        @block.vector
        def _(dve):
            link = lambda ins: s.dve.link(dve, ins)
            dve.memset(exp[:, :, :], 0.0)
            dve.memset(s.index2[:, :], -1.0)
            link(dve.memset(s.aff2[:, :], 0.0))
            dve.wait_ge(logits, 1)
            dve.tensor_copy(exp[:, 0:2, :], s.ps[:, 0, 0:2 * EXPERTS].rearrange("p (j e) -> p j e", j=2))
            link(dve.tensor_copy(exp[0:TT[2][1], 2, :], s.ps[0:TT[2][1], 0, 2 * EXPERTS:3 * EXPERTS]))
            link(dve.tensor_reduce(s.row3[:, 0:3], exp[:, :, :], AX_X, ALU.max))
            dve.tensor_tensor(exp[:, :, :], exp[:, :, :], s.row3[:, 0:3].unsqueeze(2).to_broadcast([P, 3, EXPERTS]),
                              ALU.subtract).then_inc(shifted, 1)
            for i in range(6):
                j, q, n = i // 2, i % 2, TT[i // 2][1]
                dve.wait_ge(tok_out, i + 1)
                dve.tensor_tensor(s.tok_lo[0:n, j, 512 * q:512 * q + 512], s.ps[0:n, 5 + i % 3, :],
                                  s.tok_hi[0:n, j, 512 * q:512 * q + 512].bitcast(F32), ALU.subtract).then_inc(tok_rest, 1)
            dve.wait_ge(exped, 1)
            link(dve.tensor_reduce(s.row3[:, 0:3], exp[:, :, :], AX_X, ALU.add))
            link(dve.reciprocal(s.row3[:, 0:3], s.row3[:, 0:3]))
            dve.tensor_tensor(aff[:, :, :], exp[:, :, :], s.row3[:, 0:3].unsqueeze(2).to_broadcast([P, 3, EXPERTS]),
                              ALU.mult).then_inc(aff_ready, 1)
            dve.wait_ge(turned, 1)
            link(dve.tensor_copy(s.work[:, :], s.ps[0:EXPERTS, 1, 0:T]))
            for r in range(ROUNDS):
                at = slice(8 * r, 8 * r + 8)
                link(dve.max(s.top[:, at], s.work[:, :]))
                link(dve.max_index(s.top_at[:, at], s.top[:, at], s.work[:, :]))
                if r + 1 < ROUNDS:
                    link(dve.match_replace(s.work[:, :], s.top[:, at], s.work[:, :], -1.0))
            for c in (0, HALF):
                dve.tensor_copy(s.index2[:, c:c + CAP], s.top_at[:, 0:CAP])
                last = dve.tensor_copy(s.aff2[:, c:c + CAP], s.top[:, 0:CAP])
            last.then_inc(lists, 1)
            dve.wait_ge(lists_t, 1)
            link(dve.tensor_copy(s.list_t[:, :], s.ps[0:PAIR, 2, 0:2 * EXPERTS]))
            dve.wait_ge(index_rows, 1)
            for j in range(3):
                for half in range(2):
                    last = dve.tensor_scalar(s.onehot[:, j, SLOTS // 2 * half:SLOTS // 2 * (half + 1)],
                                             s.ps[:, 3 + half, 0:SLOTS // 2], s.row[:, j:j + 1], None, ALU.is_equal)
            last.then_inc(onehot, 1)


EXPERT_RING = 6
UNITS = 12


def expert_slot(s, u):
    q = u % EXPERT_RING
    return s.w.slots[:, (s.expert_first + q) % RING, :] if q < RING else s.extra[:, q - RING, :]


def expert_loader(s):
    def load(sp, e, u):
        if u < 8:
            src = (s.d["w_gate"], s.d["w_up"])[u // 2 % 2][e].rearrange("(k p) f -> p k f", p=P)
            c = FF // 2 * (u // 4) + 512 * (u % 2)
            src, a = src[:, :, c:c + 512], KT
        else:
            src, a = s.d["w_down"][e, 512 * (u - 8):512 * (u - 8) + 512, :].rearrange("(k p) n -> p k n", p=P), 4
        sp.dma_start(expert_slot(s, u).rearrange("p (a b) -> p a b", a=a), src).then_inc(s.expert_in[u % EXPERT_RING], 16)

    return load


def experts(nc, s):
    names = ("picked", "products", "silu", "hidden", "turned", "turned_out", "down", "y", "onehot", "scattered", "added")
    (picked, products, silu, hidden, turned, turned_out, down, y_out, onehot, scattered, added) = (
        s.sem(f"expert_{k}") for k in names)
    w, load = s.w, s.w.load_expert_unit

    def arrived(pe, e, u):
        pe.wait_ge(s.expert_in[u % EXPERT_RING], 16 * (UNITS // EXPERT_RING) * e + 16 * (u // EXPERT_RING + 1))
        return expert_slot(s, u)

    def freed(sp, e, u):
        if u < 8:
            sp.wait_ge(products, 4 * e + u // 2 + 1 + FIRST)
        else:
            sp.wait_ge(down, 4 * e + u - 8 + 1 + FIRST)

    with nc.Block() as block:

        @block.sync
        def _(sp):
            with sp.Fori(0, EXPERTS - 1) as e:
                following = sp.snap(e + 1)
                for pair in range(0, UNITS, 2):
                    freed(sp, e, pair + 1)
                    for u in (pair + 1, pair):
                        load(sp, e if u + EXPERT_RING < UNITS else following, (u + EXPERT_RING) % UNITS)
            for u in range(EXPERT_RING + RING):
                freed(sp, EXPERTS - 1, u)
                if u + EXPERT_RING < UNITS:
                    load(sp, EXPERTS - 1, u + EXPERT_RING)
                else:
                    w.fetch(sp, s.in2_first + u - EXPERT_RING)

        @block.gpsimd
        def _(pool):
            with pool.Fori(0, EXPERTS) as e:
                pool.wait_ge(products, 4 * e + FIRST)
                pool.tensor_copy(s.tokens[:, :, :], s.picked[:, :, bass.ds(e * CAP, CAP)]).then_inc(picked, 1)

        @block.tensor
        def _(pe):
            for sem in (products, turned, down, scattered):
                pe.sem_inc(sem, FIRST)
            with pe.Fori(0, EXPERTS) as e:
                pe.wait_ge(picked, e + 1)
                for c in range(2):
                    for q in range(2):
                        halves = [arrived(pe, e, 4 * c + 2 * q + j).rearrange("p (k f) -> p k f", k=KT) for j in range(2)]
                        for k in range(KT):
                            for j in range(2):
                                last = pe.matmul(s.ps[HALF * j:HALF * j + CAP, 2 * c + q, :], s.tokens[:, k, :],
                                                 halves[j][:, k, :], start=k == 0, stop=k == KT - 1)
                        last.then_inc(products, 1)
                for c in range(2):
                    pe.wait_ge(hidden, 2 * e + c + 1 + FIRST)
                    for q in range(4):
                        last = pe.matmul(s.ps[:, 4, PAIR * q:PAIR * q + PAIR], s.hidden[:, c, P * q:P * q + P],
                                         s.ident[0:PAIR, 0:PAIR], is_transpose=True, start=True, stop=True)
                    last.then_inc(turned, 1)
                    pe.wait_ge(turned_out, 2 * e + c + 1)
                    for j in range(2):
                        wd = arrived(pe, e, 8 + 2 * c + j).rearrange("p (q n) -> p q n", q=4)
                        for q in range(4):
                            for half in range(2):
                                last = pe.matmul(s.ps[HALF * half:HALF * half + CAP, 5, :],
                                                 s.hidden_t[:, c, q, HALF * j:HALF * j + CAP],
                                                 wd[:, q, 512 * half:512 * half + 512],
                                                 start=c + j + q == 0, stop=c == 1 and j == 1 and q == 3)
                        last.then_inc(down, 1)
                pe.wait_ge(y_out, e + 1)
                pe.wait_ge(onehot, e + 1)
                for m in range(KT):
                    r = HALF * (m // 4)
                    pe.wait_ge(added, KT * e + max(m - 1, 0) + FIRST)
                    pe.matmul(s.ps[:, 6 + m % 2, 0:T], s.y[r:r + CAP, P * (m % 4):P * (m % 4) + P],
                              s.spread[r:r + CAP, :], start=True, stop=True).then_inc(scattered, 1)

        @block.scalar
        def _(act):
            with act.Fori(0, EXPERTS) as e:
                for c in range(2):
                    act.wait_ge(products, 4 * e + 2 * c + 1 + FIRST)
                    act.wait_ge(hidden, 2 * e + FIRST)
                    act.activation(s.silu[:, c, :], s.ps[0:PAIR, 2 * c, :], ACT.Silu).then_inc(silu, 1)
                act.wait_ge(down, 4 * e + 4 + FIRST)
                act.wait_ge(scattered, KT * e + FIRST)
                act.activation(s.y[:, :], s.ps[0:PAIR, 5, :], ACT.Copy).then_inc(y_out, 1)

        @block.vector
        def _(dve):
            for sem in (hidden, added):
                dve.sem_inc(sem, FIRST)
            with dve.Fori(0, EXPERTS) as e:
                dve.wait_ge(scattered, KT * e + FIRST)
                dve.tensor_scalar(s.spread[:, :], s.iota[0:PAIR, :], s.list_t[:, bass.ds(e, 1)],
                                  s.list_t[:, bass.ds(e + EXPERTS, 1)], ALU.is_equal, ALU.mult).then_inc(onehot, 1)
                for c in range(2):
                    dve.wait_ge(silu, 2 * e + c + 1)
                    dve.wait_ge(products, 4 * e + 2 * c + 2 + FIRST)
                    dve.wait_ge(turned, 2 * e + FIRST)
                    dve.tensor_tensor(s.hidden[:, c, :], s.silu[:, c, :], s.ps[0:PAIR, 2 * c + 1, :], ALU.mult)\
                       .then_inc(hidden, 1)
                    dve.wait_ge(turned, 2 * e + c + 1 + FIRST)
                    dve.wait_ge(down, 4 * e + FIRST)
                    dve.tensor_copy(s.hidden_t[:, c, :, :], s.ps[:, 4, 0:4 * PAIR].rearrange("p (q t) -> p q t", q=4))\
                       .then_inc(turned_out, 1)
                for m in range(KT):
                    dve.wait_ge(scattered, KT * e + m + 1 + FIRST)
                    dve.tensor_tensor(s.h[:, m, :], s.h[:, m, :], s.ps[:, 6 + m % 2, 0:T], ALU.add).then_inc(added, 1)
            dve.wait_ge(added, KT * EXPERTS + FIRST)



GLA_HEADS, GLA_DK, GLA_DV = 4, 64, 128
GLA_BLOCK = 16
GLA_BLOCKS = SEQ // GLA_BLOCK
KEPT = [GLA_BLOCK * b * (b + 1) // 2 for b in range(GLA_BLOCKS + 1)]
LIMIT = 80.0
QT = SEQ // P
SWA_HEADS = 8


def by_tokens(nc, s):
    m1, w = s.m1, s.w
    done, out, alpha = s.sem("values_done"), s.sem("values_out"), s.sem("alpha_done")
    u_mix, u_v = s.in2_first + 3, s.in2_first + 4
    w.freed[u_mix] = w.freed[u_v] = (done, 4)
    with nc.Block() as block:

        @block.sync
        def _(sp):
            w.refill(sp, u_mix, 2)

        @block.tensor
        def _(pe):
            pe.wait_ge(s.alpha_in, 16)
            for m in range(2):
                last = pe.matmul(s.ps[:, 4 + m, 0:SEQ], s.gla_alpha[:, P * m:P * m + P], s.a_lr[:, :], start=True, stop=True)
            last.then_inc(alpha, 1)
            wm, wv = w.wait(pe, u_mix), w.wait(pe, u_v)
            for j in range(QT):
                for q, (wt, c0, n) in enumerate(((wv, 0, 512), (wm, P + 16, P))):
                    for k in range(KT):
                        last = pe.matmul(s.ps[:, 2 * j + q, 0:n], m1[:, k, P * j:P * j + P], wt[:, k, c0:c0 + n],
                                         start=k == 0, stop=k == KT - 1)
                    last.then_inc(done, 1)

        @block.scalar
        def _(act):
            for j in range(QT):
                act.wait_ge(done, 2 * j + 1)
                act.activation(s.v_gla[:, j, :], s.ps[:, 2 * j, :], ACT.Copy)
                act.wait_ge(done, 2 * j + 2)
                act.activation(s.v_swa[:, j, :], s.ps[:, 2 * j + 1, 0:P], ACT.Copy).then_inc(out, 1)
            act.activation(s.r_gla[:, :, :], s.r_gla[:, :, :], ACT.Silu)
            act.wait_ge(out, QT)

        @block.vector
        def _(dve):
            dve.memset(s.one_row[:, :], 1.0)
            dve.wait_ge(alpha, 1)
            for m in range(2):
                last = dve.tensor_scalar(s.cum[:, m, :], s.ps[:, 4 + m, 0:SEQ], s.col("gla_b")[:, m:m + 1], -1.0,
                                         ALU.add, ALU.mult)
            s.dve.link(dve, last)

    softplus(nc, s, "gla", s.cum[:, :, :], s.cum[:, :, :], s.scratch, (2, SEQ))


def linear_attention(nc, s):
    cum, names = s.cum, ("refs", "q_in", "q_exp", "q_out", "k_in", "k_exp", "k_out", "scores", "masked", "o", "o_copied",
                         "squared", "summed", "std", "done")
    refs, q_in, q_exp, q_out, k_in, k_exp, k_out, scores, masked, o_done, o_out, squared, summed, std, done = (
        s.sem(f"gla_{k}") for k in names)
    tiles = [(b, j) for b in range(GLA_BLOCKS) for j in range(QT) if GLA_BLOCK * (b + 1) > P * j]

    with nc.Block() as block:

        @block.vector
        def _(dve):
            link = lambda ins: s.dve.link(dve, ins)
            dve.memset(s.ps[:, 0:4, :], 0.0).then_inc(refs, 1)
            link(dve.tensor_scalar(cum[:, :, :], cum[:, :, :], -1.0 / 16.0, None, ALU.mult))
            for m in range(2):
                last = dve.tensor_tensor_scan(s.b[:, m, :], s.one_row[:, :], cum[:, m, :], 0.0, ALU.mult, ALU.add)
            link(last)
            b4 = s.b[:, :, :].rearrange("p m (b t) -> p (m b) t", t=GLA_BLOCK)
            ref = b4[:, :, GLA_BLOCK // 2:GLA_BLOCK // 2 + 1]
            link(dve.tensor_copy(s.ref[:, :], ref.rearrange("p a o -> p (a o)")))
            dq = s.dq[:, :, :].rearrange("p m (b t) -> p (m b) t", t=GLA_BLOCK)
            link(dve.tensor_tensor(dq, b4, s.ref[:, :].unsqueeze(2).to_broadcast([P, 2 * GLA_BLOCKS, GLA_BLOCK]),
                                   ALU.subtract))
            dve.tensor_scalar(s.dq[:, :, :], s.dq[:, :, :], LIMIT, None, ALU.min).then_inc(q_in, 1)
            for m in range(2):
                for b in range(GLA_BLOCKS):
                    n = GLA_BLOCK * (b + 1)
                    last = dve.tensor_scalar(s.keys[:, m, KEPT[b]:KEPT[b] + n], s.b[:, m, 0:n],
                                             s.ref[:, m * GLA_BLOCKS + b:m * GLA_BLOCKS + b + 1], -LIMIT,
                                             ALU.subtract, ALU.max)
                last.then_inc(k_in, 1)
            dve.wait_ge(q_exp, 1)
            dve.tensor_tensor(s.dq[:, :, :], s.dq[:, :, :], s.qk_gla[:, 0:2, :], ALU.mult).then_inc(q_out, 1)
            for m in range(2):
                dve.wait_ge(k_exp, m + 1)
                for b in range(GLA_BLOCKS):
                    n = GLA_BLOCK * (b + 1)
                    last = dve.tensor_tensor(s.keys[:, m, KEPT[b]:KEPT[b] + n], s.keys[:, m, KEPT[b]:KEPT[b] + n],
                                             s.qk_gla[:, 2 + m, 0:n], ALU.mult)
                last.then_inc(k_out, 1)
            dve.wait_ge(done, 2)
            for h in range(GLA_HEADS):
                dve.wait_ge(scores, h + 1)
                dve.tensor_tensor(s.sc_gla[:, h, :, :], s.ps[:, h, :].rearrange("p (j t) -> p j t", j=QT),
                                  s.causal[:, :, :], ALU.mult).then_inc(masked, 1)
            dve.wait_ge(std, 1)
            dve.wait_ge(o_out, GLA_HEADS)
            link(dve.reciprocal(s.rstd_gla[:, :], s.rstd_gla[:, :]))
            for h in range(GLA_HEADS):
                last = dve.scalar_tensor_tensor(s.cat[:, h, :], s.cat[:, h, :], s.col("gla_norm")[:, h:h + 1],
                                                s.rstd_gla[:, h * SEQ:(h + 1) * SEQ], ALU.mult, ALU.mult)
            link(last)
            link(dve.tensor_tensor(s.cat[:, 0:4, :], s.cat[:, 0:4, :], s.r_gla[:, :, :], ALU.mult))

        @block.gpsimd
        def _(pool):
            pool.memset(s.causal[:, :, :], 1.0).then_inc(done, 1)
            pool.wait_ge(done, 1)
            pool.affine_select(out=s.causal[:, :, :], in_=s.causal[:, :, :], compare_op=ALU.is_ge, fill=0.0,
                               base=0, pattern=[[-P, QT], [1, SEQ]], channel_multiplier=-1).then_inc(done, 1)

        @block.scalar
        def _(act):
            act.wait_ge(q_in, 1)
            act.activation(s.dq[:, :, :], s.dq[:, :, :], ACT.Exp).then_inc(q_exp, 1)
            for m in range(2):
                act.wait_ge(k_in, m + 1)
                act.activation(s.keys[:, m, :], s.keys[:, m, :], ACT.Exp, scale=-1.0).then_inc(k_exp, 1)
            for h in range(GLA_HEADS):
                act.wait_ge(o_done, h + 1)
                act.activation(s.sq_gla[:, SEQ * h:SEQ * h + SEQ], s.ps[:, 4 + h % 2, 0:SEQ], ACT.Square).then_inc(squared, 1)
                act.activation(s.cat[:, h, :], s.ps[:, 4 + h % 2, 0:SEQ], ACT.Copy).then_inc(o_out, 1)
            act.wait_ge(summed, 1)
            act.activation(s.rstd_gla[:, :], s.ps[:, 6:8, :].rearrange("p a b -> p (a b)"), ACT.Sqrt,
                           bias=s.eps[:, 0:1], scale=1.0 / GLA_DV).then_inc(std, 1)

        @block.tensor
        def _(pe):
            pe.wait_ge(refs, 1)
            pe.wait_ge(q_out, 1)
            for h in range(GLA_HEADS):
                m, r = h // 2, 64 * (h % 2)
                if h % 2 == 0:
                    pe.wait_ge(k_out, m + 1)
                for b, j in tiles:
                    n = min(P, GLA_BLOCK * (b + 1) - P * j)
                    c = P * j + KEPT[b]
                    t0 = GLA_BLOCK * b
                    last = pe.matmul(s.ps[0:n, h, SEQ * j + t0:SEQ * j + t0 + GLA_BLOCK], s.keys[r:r + 64, m, c:c + n],
                                     s.dq[r:r + 64, m, t0:t0 + GLA_BLOCK], start=True, stop=True)
                last.then_inc(scores, 1)
            for h in range(GLA_HEADS):
                pe.wait_ge(masked, h + 1)
                if h >= 2:
                    pe.wait_ge(o_out, h - 1)
                for j in range(QT):
                    last = pe.matmul(s.ps[:, 4 + h % 2, 0:SEQ], s.v_gla[:, j, GLA_DV * h:GLA_DV * h + GLA_DV],
                                     s.sc_gla[:, h, j, :], start=j == 0, stop=j == QT - 1)
                last.then_inc(o_done, 1)
            for q in range(2):
                pe.wait_ge(squared, 2 * q + 2)
                last = pe.matmul(s.ps[:, 6 + q, :], s.ones[:, :], s.sq_gla[:, 512 * q:512 * q + 512], start=True, stop=True)
            last.then_inc(summed, 1)


def window_attention(nc, s):
    PARTS = ((0, P, P), (P, 2 * P, 0))
    names = ("consts", "far", "scores", "maxed", "exp", "normed", "turned", "copied", "o", "o_out", "shift")
    consts, far, scores, maxed, exped, normed, turned, copied, o_done, o_out, shift = (s.sem(f"swa_{k}") for k in names)
    W = 3 * P
    with nc.Block() as block:

        @block.gpsimd
        def _(pool):
            pool.iota(s.dist[:, :], pattern=[[-1, 2 * P]], base=P, channel_multiplier=1,
                      allow_small_or_imprecise_dtypes=True).then_inc(consts, 1)
            pool.wait_ge(consts, 1)
            pool.affine_select(out=s.dist[:, :], in_=s.dist[:, :], compare_op=ALU.is_ge, fill=-NEG,
                               base=P, pattern=[[-1, 2 * P]], channel_multiplier=1).then_inc(consts, 1)
            pool.wait_ge(consts, 2)
            pool.affine_select(out=s.dist[:, :], in_=s.dist[:, :], compare_op=ALU.is_ge, fill=-NEG,
                               base=-1, pattern=[[1, 2 * P]], channel_multiplier=-1).then_inc(far, 1)

        @block.tensor
        def _(pe):
            for h in range(SWA_HEADS):
                r, m = 64 * (h // 4), h % 4
                pe.matmul(s.ps[:, h, 0:P], s.q_swa[r:r + 64, m, 0:P], s.k_swa[r:r + 64, 0:P], start=True, stop=True)
                pe.matmul(s.ps[:, h, P:W], s.q_swa[r:r + 64, m, P:SEQ], s.k_swa[r:r + 64, 0:SEQ],
                          start=True, stop=True).then_inc(scores, 1)
            def turn(h):
                pe.wait_ge(normed, h + 1)
                if h >= 2:
                    pe.wait_ge(copied, h - 1)
                for q in range(3):
                    last = pe.matmul(s.ps[:, h % 2, P * q:P * q + P], s.sc_swa[:, h, P * q:P * q + P], s.ident[:, :],
                                     is_transpose=True, start=True, stop=True)
                last.then_inc(turned, 1)

            turn(0)
            for h in range(SWA_HEADS):
                r, m = 64 * (h // 4), h % 4
                if h + 1 < SWA_HEADS:
                    turn(h + 1)
                pe.wait_ge(copied, h + 1)
                out, v = s.ps[r:r + 64, 4 + m, :], s.v_swa
                pe.matmul(out[:, 0:P], v[:, 0, r:r + 64], s.p_t[:, h % 2, 0:P], start=True, stop=True)
                pe.matmul(out[:, P:SEQ], v[:, 0, r:r + 64], s.p_t[:, h % 2, P:2 * P], start=True, stop=False)
                pe.matmul(out[:, P:SEQ], v[:, 1, r:r + 64], s.p_t[:, h % 2, 2 * P:W], start=False, stop=True)\
                  .then_inc(o_done, 1)

        @block.vector
        def _(dve):
            link = lambda ins: s.dve.link(dve, ins)
            dve.wait_ge(far, 1)
            for h in range(SWA_HEADS):
                dve.wait_ge(scores, h + 1)
                for c, n, c0 in PARTS:
                    last = dve.scalar_tensor_tensor(s.sc_swa[:, h, c:c + n], s.dist[:, c0:2 * P],
                                                    -(2.0 ** -(h + 1)), s.ps[:, h, c:c + n], ALU.mult, ALU.add)
            link(last)
            for q, (c, n, _) in enumerate(PARTS):
                last = dve.tensor_reduce(s.max_swa[:, q, :], s.sc_swa[:, :, c:c + n], AX_X, ALU.max)
            link(last)
            for q in range(2):
                last = dve.tensor_tensor(s.max_swa[:, q, :], s.max_swa[:, q, :], s.col("sinks"), ALU.max)
            link(last)
            for q in range(2):
                last = dve.tensor_tensor(s.sink[:, q, :], s.col("sinks"), s.max_swa[:, q, :], ALU.subtract)
            link(last)
            dve.tensor_scalar(s.max_swa[:, :, :], s.max_swa[:, :, :], -1.0, None, ALU.mult).then_inc(maxed, 1)
            dve.wait_ge(exped, 1)
            link(dve.tensor_tensor(s.sum_swa[:, :, :], s.sum_swa[:, :, :], s.sink[:, :, :], ALU.add))
            link(dve.reciprocal(s.sum_swa[:, :, :], s.sum_swa[:, :, :]))
            for h in range(SWA_HEADS):
                for q, (c, n, _) in enumerate(PARTS):
                    last = dve.tensor_scalar(s.sc_swa[:, h, c:c + n], s.sc_swa[:, h, c:c + n],
                                             s.sum_swa[:, q, h:h + 1], None, ALU.mult)
                last.then_inc(normed, 1)
            for m in range(4):
                dve.wait_ge(o_done, m + 5)
                last = dve.tensor_copy(s.cat[:, 4 + m, :], s.ps[:, 4 + m, 0:SEQ])
            link(last)

        @block.scalar
        def _(act):
            act.wait_ge(maxed, 1)
            act.activation(s.sink[:, :, :], s.sink[:, :, :], ACT.Exp)
            for h in range(SWA_HEADS):
                for q, (c, n, _) in enumerate(PARTS):
                    last = act.activation(s.sc_swa[:, h, c:c + n], s.sc_swa[:, h, c:c + n], ACT.Exp,
                                          bias=s.max_swa[:, q, h:h + 1], accum_out=s.sum_swa[:, q, h:h + 1])
            last.then_inc(exped, 1)
            for h in range(SWA_HEADS):
                act.wait_ge(turned, h + 1)
                if h >= 2:
                    act.wait_ge(o_done, h - 1)
                act.activation(s.p_t[:, h % 2, :], s.ps[:, h % 2, 0:W], ACT.Copy).then_inc(copied, 1)


KEYS = 128
PEER_HEADS = 8
TOPK = 16
LISTS = PEER_HEADS * TOPK


def peer_lists(nc, s):
    link_of = lambda dve: (lambda ins: s.dve.link(dve, ins))
    w, u_q = s.w, s.in2_first + 7
    BANKS, BATCHES = 4, 2
    QUERIES = 2 * PEER_HEADS
    names = ("query", "query_out", "scores", "scores_out", "shifted", "exp", "lists", "turned", "turned_out")
    query, query_out, scores, scores_out, shifted, exped, lists, turned, turned_out = (s.sem(f"peer_{k}") for k in names)

    def scores_at(h, j):
        return s.ps[:, 4 + h % 4, 2 * P * j:2 * P * j + 2 * P]

    with nc.Block() as block:

        @block.tensor
        def _(pe):
            def score(m):
                h, half = m // 2, m % 2
                pe.wait_ge(query_out, m + 1)
                if h >= 4:
                    pe.wait_ge(scores_out, QT * (h - 3))
                for j in range(QT):
                    last = pe.matmul(scores_at(h, j)[:, P * half:P * half + P], s.q_peer[:, m, P * j:P * j + P],
                                     s.peer_keys[:, half, :], start=True, stop=True)
                if half:
                    last.then_inc(scores, 1)

            pe.wait_ge(s.keys_in, 16)
            for m in range(QUERIES):
                wt = w.wait(pe, u_q + m // 4)
                if m >= BANKS:
                    pe.wait_ge(query_out, m - BANKS + 1)
                for k in range(KT):
                    last = pe.matmul(s.ps[:, m % BANKS, 0:SEQ], wt[:, k, P * (m % 4):P * (m % 4) + P], s.m2[:, k, :],
                                     start=k == 0, stop=k == KT - 1)
                last.then_inc(query, 1)
                if m:
                    score(m - 1)
            score(QUERIES - 1)
            for b in range(BATCHES):
                pe.wait_ge(lists, b + 1)
                for j in range(QT):
                    for q in range(3):
                        last = pe.matmul(s.ps[HALF * b:HALF * b + HALF, j, P * q:P * q + P],
                                         s.lists[:, b, q, HALF * j:HALF * j + HALF], s.ident[:, :],
                                         start=True, stop=True)
                last.then_inc(turned, 1)

        @block.scalar
        def _(act):
            def scores_of(h):
                act.wait_ge(scores, h + 1)
                for j in range(QT):
                    act.activation(s.peer_s[:, j, :, :].rearrange("p (a h) n -> p h a n", a=2)[:, h],
                                   scores_at(h, j).rearrange("p (a n) -> p a n", a=2), ACT.Copy).then_inc(scores_out, 1)

            def exp_of(b):
                act.wait_ge(shifted, b + 1)
                act.activation(s.lists[:, b, 2, :], s.lists[:, b, 2, :], ACT.Exp).then_inc(exped, 1)

            for m in range(QUERIES):
                act.wait_ge(query, m + 1)
                act.activation(s.q_peer[:, m, :], s.ps[:, m % BANKS, 0:SEQ], ACT.Copy).then_inc(query_out, 1)
                if m % 2 == 0 and m:
                    scores_of(m // 2 - 1)
                if m == QUERIES - 2:
                    exp_of(0)
            scores_of(PEER_HEADS - 1)
            exp_of(1)
            for b in range(BATCHES):
                act.wait_ge(turned, b + 1)
                rows = slice(HALF * b, HALF * b + HALF)
                for j in range(QT):
                    act.activation(s.lists_t[rows, :, P * j:P * j + P],
                                   s.ps[rows, j, 0:3 * P].rearrange("p (q t) -> p q t", q=3), ACT.Copy).then_inc(turned_out, 1)
            act.wait_ge(turned_out, BATCHES * QT)

        @block.vector
        def _(dve):
            link = link_of(dve)

            def top16(values, best, where):
                n = len(values)
                for i in range(n):
                    last = dve.max(best[i][:, 0:8], values[i])
                link(last)
                for i in range(n):
                    last = dve.max_index(where[i][:, 0:8], best[i][:, 0:8], values[i])
                link(last)
                for i in range(n):
                    last = dve.match_replace(values[i], best[i][:, 0:8], values[i], -3.0e38)
                link(last)
                for i in range(n):
                    last = dve.max(best[i][:, 8:16], values[i])
                link(last)
                for i in range(n):
                    last = dve.max_index(where[i][:, 8:16], best[i][:, 8:16], values[i])
                link(last)

            def best_of(h):
                dve.wait_ge(scores_out, QT * (h + 1))
                at = [(j, half) for j in range(QT) for half in range(2)]
                where = [PEER_HEADS * half + 4 * j + h % 4 for j, half in at]
                top16([s.peer_s[:, j, PEER_HEADS * half + h, :] for j, half in at],
                      [s.best[:, h // 4, i, :] for i in where], [s.place[:, h // 4, i, :] for i in where])

            for b in range(BATCHES):
                for h in range(4 * b, 4 * b + 4):
                    best_of(h)
                shape = [P, PEER_HEADS, TOPK, TOPK]
                v1, v2 = s.best[:, b, 0:PEER_HEADS, :], s.best[:, b, PEER_HEADS:2 * PEER_HEADS, :]
                dve.tensor_copy(s.place_f[:, :, :], s.place[:, b, :, :])
                link(dve.tensor_tensor(s.cand[:, :, :, :], v1.unsqueeze(3).to_broadcast(shape),
                                       v2.unsqueeze(2).to_broadcast(shape), ALU.add))
                flat = s.cand[:, :, :, :].rearrange("p h a b -> p h (a b)")
                gate = s.lists[:, b, 2, :].rearrange("p (h k) -> p h k", h=PEER_HEADS)
                top16([flat[:, h, :] for h in range(PEER_HEADS)], [gate[:, h, :] for h in range(PEER_HEADS)],
                      [s.pair[:, h, :] for h in range(PEER_HEADS)])
                dve.tensor_scalar(s.half_i[:, 0, :, :], s.pair[:, :, :], 4, None, ALU.logical_shift_right)
                link(dve.tensor_scalar(s.half_i[:, 1, :, :], s.pair[:, :, :], TOPK - 1, None, ALU.bitwise_and))
                link(dve.tensor_copy(s.half_f[:, :, :, :], s.half_i[:, :, :, :]))
                link(dve.tensor_copy(s.first[:, :], gate[:, :, 0:1].rearrange("p h o -> p (h o)")))
                dve.tensor_tensor(gate, gate, s.first[:, :].unsqueeze(2).to_broadcast([P, PEER_HEADS, TOPK]), ALU.subtract)\
                   .then_inc(shifted, 1)
                for q in range(2):
                    hit = s.cand[:, :, :, :]
                    link(dve.tensor_tensor(hit.rearrange("p h k a -> p (h k) a"),
                                           s.half_f[:, q, :, :].rearrange("p h k -> p (h k)").unsqueeze(2).to_broadcast([P, LISTS, TOPK]),
                                           s.iota[:, 0:TOPK].unsqueeze(1).to_broadcast([P, LISTS, TOPK]), ALU.is_equal))
                    link(dve.tensor_tensor(hit, hit, s.place_f[:, PEER_HEADS * q:PEER_HEADS * (q + 1), :].unsqueeze(2)
                                           .to_broadcast(shape), ALU.mult))
                    link(dve.tensor_reduce(s.lists[:, b, q, :], hit.rearrange("p h k a -> p (h k) a"), AX_X, ALU.add))
                dve.wait_ge(exped, b + 1)
                link(dve.tensor_reduce(s.first[:, :], gate, AX_X, ALU.add))
                link(dve.reciprocal(s.first[:, :], s.first[:, :]))
                dve.tensor_tensor(gate, gate, s.first[:, :].unsqueeze(2).to_broadcast([P, PEER_HEADS, TOPK]), ALU.mult)\
                   .then_inc(lists, 1)


TOKENS = 4
BANKS_W = 4
BODY = BANKS_W * TOKENS


def peer_weights(nc, s):
    e1, e2, gate = (s.lists_t[:, q, :] for q in range(3))
    hot1, gated, hot2, product, out, m2_hi, m2_lo = (
        s.sem(f"weights_{k}") for k in ("hot1", "gated", "hot2", "product", "out", "m2_hi", "m2_lo"))
    shape = [P, TOKENS, KEYS]

    with nc.Block() as block:

        @block.sync
        def _(sp):
            for q in range(PEER_SLOTS):
                sp.dma_start(s.v_rows[:, q, :], s.d["peer_v"][:, q, :]).then_inc(s.v_in[q], 16)
            sp.wait_ge(m2_lo, 1)
            for q in range(PEER_SLOTS):
                sp.dma_start(s.u_rows[:, q, :], s.d["peer_u"][q]).then_inc(s.u_in[q], 16)

        @block.vector
        def _(dve):
            dve.wait_ge(m2_hi, 1)
            dve.tensor_tensor(s.m2_lo[:, :, :], s.m2, s.m2_hi[:, :, :].bitcast(F32), ALU.subtract).then_inc(m2_lo, 1)
            with dve.Fori(0, SEQ // BODY) as g:
                for b in range(BANKS_W):
                    dve.wait_ge(product, BANKS_W * g + b + 1)
                    at = bass.ds(g * BODY + b * TOKENS, TOKENS)
                    for hot, e, sem in ((s.hot1, e1, hot1), (s.hot2, e2, hot2)):
                        dve.tensor_tensor(hot[:, b, :, :], s.iota[:, 0:KEYS].unsqueeze(1).to_broadcast(shape),
                                          e[:, at].unsqueeze(2).to_broadcast(shape), ALU.is_equal).then_inc(sem, 1)

        @block.gpsimd
        def _(pool):
            with pool.Fori(0, SEQ // BODY) as g:
                for b in range(BANKS_W):
                    pool.wait_ge(hot1, BANKS_W * g + b + 1)
                    pool.tensor_tensor(s.hot1[:, b, :, :], s.hot1[:, b, :, :],
                                       gate[:, bass.ds(g * BODY + b * TOKENS, TOKENS)].unsqueeze(2).to_broadcast(shape),
                                       ALU.mult).then_inc(gated, 1)

        @block.tensor
        def _(pe):
            pe.sem_inc(product, BANKS_W)
            with pe.Fori(0, SEQ // BODY) as g:
                for b in range(BANKS_W):
                    pe.wait_ge(gated, BANKS_W * g + b + 1)
                    pe.wait_ge(hot2, BANKS_W * g + b + 1)
                    pe.wait_ge(out, BANKS_W * g + b + 1)
                    for t in range(TOKENS):
                        last = pe.matmul(s.ps[:, b, P * t:P * t + P], s.hot1[:, b, t, :], s.hot2[:, b, t, :],
                                         start=True, stop=True)
                    last.then_inc(product, 1)

        @block.scalar
        def _(act):
            act.activation(s.m2_hi[:, :, :], s.m2, ACT.Copy).then_inc(m2_hi, 1)
            act.sem_inc(out, BANKS_W)
            with act.Fori(0, SEQ // BODY) as g:
                for b in range(BANKS_W):
                    act.wait_ge(product, BANKS_W * g + b + 1 + BANKS_W)
                    act.activation(s.weight[:, bass.ds(g * BODY + b * TOKENS, TOKENS), :],
                                   s.ps[:, b, :].rearrange("p (t e) -> p t e", t=TOKENS), ACT.Copy).then_inc(out, 1)
            act.wait_ge(out, SEQ // TOKENS + BANKS_W)


PEER_SLOTS = 2
PEER_BODY = 4


def peer_experts(nc, s):
    names = ("hidden", "gelu", "weighted", "used", "zero", "y", "u_hi", "u_lo", "v_hi", "v_lo", "act_hi", "act_lo")
    hidden, gelu, weighted, used, zero, y_out, u_hi, u_lo, v_hi, v_lo, act_hi, act_lo = (
        s.sem(f"expert2_{k}") for k in names)
    BODIES = KEYS // PEER_BODY

    def arrived(eng, sems, g, q):
        eng.wait_ge(sems[q % PEER_SLOTS], 16 * (PEER_BODY // PEER_SLOTS) * g + 16 * (q // PEER_SLOTS + 1))

    def u_products(pe, g, q):
        i = PEER_BODY * g + q
        pe.wait_ge(u_hi, i + 1)
        out = s.ps[:, q % 2, 0:SEQ]
        for k in range(KT):
            for m in (s.m2_hi, s.m2_lo):
                pe.matmul(out, s.u_hi[:, P * k:P * k + P], m[:, k, :], start=k == 0 and m is s.m2_hi, stop=False)
        pe.wait_ge(u_lo, i + 1)
        for k in range(KT):
            last = pe.matmul(out, s.u_lo[:, P * k:P * k + P], s.m2_hi[:, k, :], start=False, stop=k == KT - 1)
        last.then_inc(hidden, 1)

    def v_products(pe, g, q, stop=False):
        i = PEER_BODY * g + q
        pe.wait_ge(act_hi, i + 1)
        pe.wait_ge(v_hi, i + 1)
        for a, v, sem in ((s.act_hi, s.v_hi, act_lo), (s.act_lo, s.v_hi, v_lo), (s.act_hi, s.v_lo, None)):
            for j in range(QT):
                for half in range(2):
                    last = pe.matmul(s.ps[:, 4 + 2 * j + half, :], a[:, q % 2, P * j:P * j + P],
                                     v[:, 512 * half:512 * half + 512], start=False, stop=stop and sem is None,
                                     skip_group_check=True)
            if sem is not None:
                pe.wait_ge(sem, i + 1)
        last.then_inc(used, 1)

    def upper_u(act, g, q):
        arrived(act, s.u_in, g, q)
        act.activation(s.u_hi[:, :], s.u_rows[:, q % PEER_SLOTS, :], ACT.Copy).then_inc(u_hi, 1)

    def rest_u(dve, g, q):
        dve.wait_ge(u_hi, PEER_BODY * g + q + 1)
        dve.tensor_tensor(s.u_lo[:, :], s.u_rows[:, q % PEER_SLOTS, :], s.u_hi[:, :].bitcast(F32),
                          ALU.subtract).then_inc(u_lo, 1)

    with nc.Block() as block:

        @block.sync
        def _(sp):
            def reload(g, q, ahead):
                i = PEER_BODY * g + q
                sp.wait_ge(u_lo, i + 1)
                sp.dma_start(s.u_rows[:, q % PEER_SLOTS, :], s.d["peer_u"][ahead]).then_inc(s.u_in[q % PEER_SLOTS], 16)
                sp.wait_ge(v_lo, i + 1)
                sp.dma_start(s.v_rows[:, q % PEER_SLOTS, :], s.d["peer_v"][:, ahead, :]).then_inc(s.v_in[q % PEER_SLOTS], 16)

            with sp.Fori(0, BODIES - 1) as g:
                for q in range(PEER_BODY):
                    reload(g, q, g * PEER_BODY + (q + PEER_SLOTS))
            for q in range(PEER_BODY - PEER_SLOTS):
                reload(BODIES - 1, q, KEYS - PEER_BODY + q + PEER_SLOTS)

        @block.tensor
        def _(pe):
            pe.sem_inc(used, FIRST)
            pe.wait_ge(zero, 1)
            for bank in range(4):
                pe.matmul(s.ps[:, 4 + bank, :], s.zeros[:, 0:P], s.zeros[:, :], start=True, stop=False,
                          skip_group_check=True)
            u_products(pe, 0, 0)
            with pe.Fori(0, BODIES - 1) as g:
                for q in range(PEER_BODY):
                    u_products(pe, g, q + 1)
                    v_products(pe, g, q)
            for q in range(PEER_BODY):
                if q + 1 < PEER_BODY:
                    u_products(pe, BODIES - 1, q + 1)
                v_products(pe, BODIES - 1, q, stop=q == PEER_BODY - 1)

        @block.scalar
        def _(act):
            def key(g, q, last=False):
                i = PEER_BODY * g + q
                act.wait_ge(hidden, i + 1)
                act.activation(s.gelu2[:, :], s.ps[:, q % 2, 0:SEQ], ACT.Gelu).then_inc(gelu, 1)
                if not last:
                    upper_u(act, g, q + 1)
                act.wait_ge(weighted, i + 1)
                act.activation(s.act_hi[:, q % 2, :], s.act2[:, q % 2, :], ACT.Copy).then_inc(act_hi, 1)
                arrived(act, s.v_in, g, q)
                act.wait_ge(used, i + FIRST)
                act.activation(s.v_hi[:, :], s.v_rows[:, q % PEER_SLOTS, :], ACT.Copy).then_inc(v_hi, 1)

            upper_u(act, 0, 0)
            with act.Fori(0, BODIES - 1) as g:
                for q in range(PEER_BODY):
                    key(g, q)
            for q in range(PEER_BODY):
                key(BODIES - 1, q, last=q == PEER_BODY - 1)
            act.wait_ge(used, KEYS + FIRST)
            for bank in range(4):
                act.activation(s.y2[:, bank // 2, 512 * (bank % 2):512 * (bank % 2) + 512], s.ps[:, 4 + bank, :],
                               ACT.Copy).then_inc(y_out, 1)
            act.wait_ge(y_out, 4)

        @block.vector
        def _(dve):
            def key(g, q, last=False):
                i = PEER_BODY * g + q
                if not last:
                    rest_u(dve, g, q + 1)
                dve.wait_ge(gelu, i + 1)
                dve.tensor_tensor(s.act2[:, q % 2, :], s.gelu2[:, :],
                                  s.weight[:, :, bass.ds(g * PEER_BODY + q, 1)].rearrange("p t o -> p (t o)"),
                                  ALU.mult).then_inc(weighted, 1)
                dve.wait_ge(act_hi, i + 1)
                dve.tensor_tensor(s.act_lo[:, q % 2, :], s.act2[:, q % 2, :], s.act_hi[:, q % 2, :].bitcast(F32),
                                  ALU.subtract).then_inc(act_lo, 1)
                dve.wait_ge(v_hi, i + 1)
                dve.tensor_tensor(s.v_lo[:, :], s.v_rows[:, q % PEER_SLOTS, :], s.v_hi[:, :].bitcast(F32),
                                  ALU.subtract).then_inc(v_lo, 1)

            dve.memset(s.zeros[:, :], 0.0).then_inc(zero, 1)
            rest_u(dve, 0, 0)
            with dve.Fori(0, BODIES - 1) as g:
                for q in range(PEER_BODY):
                    key(g, q)
            for q in range(PEER_BODY):
                key(BODIES - 1, q, last=q == PEER_BODY - 1)


def peer_residual(nc, s):
    turned, added = s.sem("resid_turned"), s.sem("resid_added")
    with nc.Block() as block:

        @block.tensor
        def _(pe):
            for k in range(KT):
                for j in range(QT):
                    last = pe.matmul(s.ps[:, k, P * j:P * j + P], s.y2[:, j, P * k:P * k + P], s.ident[:, :],
                                     is_transpose=True, start=True, stop=True)
                last.then_inc(turned, 1)

        @block.vector
        def _(dve):
            for k in range(KT):
                dve.wait_ge(turned, k + 1)
                dve.scalar_tensor_tensor(s.x[:, k, :], s.ps[:, k, 0:SEQ], s.mod[:, 5 * KT + k:5 * KT + k + 1],
                                         s.x[:, k, :], ALU.mult, ALU.add).then_inc(added, 1)
            dve.wait_ge(added, KT)


def second_block(nc, s, opener, first_part):
    mod = lambda i: s.mod[:, KT * i:KT * i + KT]
    u0 = s.in2_first
    with ExitStack() as stage:
        sb = opener(stage)
        s.qk_gla, s.r_gla, s.q_swa = sb("qk_gla", [P, 4, SEQ]), sb("r_gla", [P, 4, SEQ]), sb("q_swa", [P, 4, SEQ])
        s.k_swa, s.a_lr, s.cat = sb("k_swa", [P, SEQ]), sb("a_lr", [16, SEQ]), sb("cat", [P, KT, SEQ])
        s.v_gla, s.v_swa = sb("v_gla", [P, QT, 512]), sb("v_swa", [P, QT, P])
        s.one_row, s.cum, s.b, s.dq = sb("one_row", [P, SEQ]), sb("cum", [P, 2, SEQ]), sb("b", [P, 2, SEQ]), sb("dq", [P, 2, SEQ])
        s.scratch = sb("scratch_2", [P, KT * T])
        s.gla_alpha = sb("gla_alpha", [16, 2 * P])
        s.alpha_in = start_load(nc, s, "alpha", s.gla_alpha[:, :], s.d["gla_alpha"])
        rms(nc, s, "final_norm", s.h[:, :, META:T], s.col("norm_final"), s.x, KT, SEQ)
        rms(nc, s, "norm1", s.x[:, :, :], s.col("norm1"), s.m1, KT, SEQ, gain=mod(1), shift=mod(0))
        tiles = grid(u0, 4, 12) + [(u0 + 3, 0, P), (u0 + 3, P, 16)]

        def evacuate(dve, i, prod):
            if i < 2 or 8 <= i < 12:
                out = s.qk_gla[:, i, :] if i < 2 else s.q_swa[:, i - 8, :]
                return dve.tensor_scalar(out, prod, 0.125, None, ALU.mult)
            out = s.qk_gla[:, i, :] if i < 4 else s.r_gla[:, i - 4, :] if i < 8 else s.k_swa[:, :] if i == 12 else s.a_lr[:, :]
            return dve.tensor_copy(out, prod)

        project(nc, s, "in2", range(u0, u0 + 3), tiles, s.m1, SEQ, evacuate)
        by_tokens(nc, s)
        with ExitStack() as inner:
            sb = opener(inner)
            s.ref, s.keys = sb("ref", [P, 2 * GLA_BLOCKS]), sb("keys", [P, 2, KEPT[-1]])
            s.sc_gla, s.causal = sb("sc_gla", [P, GLA_HEADS, QT, SEQ]), sb("causal", [P, QT, SEQ])
            s.sq_gla, s.rstd_gla = s.scratch[:, 0:4 * SEQ], s.scratch[:, 4 * SEQ:8 * SEQ]
            linear_attention(nc, s)
        with ExitStack() as inner:
            sb = opener(inner)
            s.dist, s.sc_swa, s.p_t = sb("dist", [P, 2 * P]), sb("sc_swa", [P, SWA_HEADS, 3 * P]), sb("p_t", [P, 2, 3 * P])
            s.max_swa, s.sink, s.sum_swa = (sb(k, [P, 2, SWA_HEADS]) for k in ("max_swa", "sink", "sum_swa"))
            window_attention(nc, s)
        rms(nc, s, "swa_norm", s.cat[:, 4:8, :], s.col("swa_norm"), s.cat[:, 4:8, :], 4, SEQ)
        project(nc, s, "out2", range(u0 + 5, u0 + 7), grid(u0 + 5, 4, KT), s.cat, SEQ,
                lambda dve, m, prod: dve.scalar_tensor_tensor(s.x[:, m, :], prod, mod(2)[:, m:m + 1], s.x[:, m, :],
                                                              ALU.mult, ALU.add))
        rms(nc, s, "norm2", s.x[:, :, :], s.col("norm2"), s.m2, KT, SEQ, gain=mod(4), shift=mod(3))
    with ExitStack() as stage:
        sb = opener(stage)
        s.q_peer, s.peer_keys = sb("q_peer", [P, 2 * PEER_HEADS, SEQ]), sb("peer_keys", [P, 2, KEYS])
        s.keys_in = start_load(nc, s, "keys", s.peer_keys[:, :, :], s.d["peer_keys"].rearrange("a d n -> d a n"))
        s.peer_s = sb("peer_s", [P, QT, 2 * PEER_HEADS, KEYS])
        s.best, s.place = (sb(k, [P, QT, 2 * PEER_HEADS, TOPK], dt) for k, dt in (("best", F32), ("place", U32)))
        s.place_f, s.cand = sb("place_f", [P, 2 * PEER_HEADS, TOPK]), sb("cand", [P, PEER_HEADS, TOPK, TOPK])
        s.pair, s.half_i = sb("pair", [P, PEER_HEADS, TOPK], U32), sb("half_i", [P, 2, PEER_HEADS, TOPK], U32)
        s.half_f, s.first = sb("half_f", [P, 2, PEER_HEADS, TOPK]), sb("first", [P, PEER_HEADS])
        s.lists = sb("lists", [P, QT, 3, LISTS])
        peer_lists(nc, s)
    first_part.close()
    with ExitStack() as stage:
        sb = opener(stage)
        s.weight = sb("weight", [P, SEQ, KEYS])
        flat = s.u[:, :, :].rearrange("p k t -> p (k t)")
        s.u_rows = flat[:, 0:PEER_SLOTS * D].rearrange("p (q n) -> p q n", q=PEER_SLOTS)
        flat = s.weight[:, :, :].rearrange("p t e -> p (t e)")
        s.y2 = flat[:, 0:QT * D].rearrange("p (j n) -> p j n", j=QT)
        s.v_rows = sb("v_rows", [P, PEER_SLOTS, D])
        s.m2_hi, s.m2_lo = sb("m2_hi", [P, KT, SEQ], F32R), sb("m2_lo", [P, KT, SEQ], F32R)
        with ExitStack() as inner:
            hot = opener(inner)
            s.hot1, s.hot2 = (hot(k, [P, BANKS_W, TOKENS, KEYS]) for k in ("hot1", "hot2"))
            peer_weights(nc, s)
        s.zeros, s.gelu2, s.act2 = sb("zeros", [P, 512]), sb("gelu2", [P, SEQ]), sb("act2", [P, 2, SEQ])
        s.u_hi, s.u_lo, s.v_hi, s.v_lo = (sb(k, [P, D], F32R) for k in ("u_hi", "u_lo", "v_hi", "v_lo"))
        s.act_hi, s.act_lo = (sb(k, [P, 2, SEQ], F32R) for k in ("act_hi", "act_lo"))
        peer_experts(nc, s)
        peer_residual(nc, s)
    with ExitStack() as stage:
        s.scratch = opener(stage)("scratch_3", [P, KT * SEQ])
        rms(nc, s, "out_norm", s.x[:, :, :], s.col("final_g"), s.x, KT, SEQ)


def build_program(nc, d, out):
    s = Core()
    s.nc, s.d, s.out = nc, d, out
    with ExitStack() as whole:

        def opener(stack):
            return lambda name, shape, dt=F32: stack.enter_context(nc.sbuf_tensor(name, shape, dt))

        stage_sems = []
        s.sem = lambda name: whole.enter_context(nc.semaphore(name))
        s.ps = whole.enter_context(nc.psum_tensor("ps", [P, 8, 512], F32))
        keep = opener(whole)
        s.dve, s.const_set, s.small_in, s.cb_out = Chain(s.sem("dve_step")), s.sem("const_set"), s.sem("small_in"), s.sem("cb_out")
        s.small = keep("small", [P, SMALL_COLS])
        s.col = lambda name: s.small[:, SMALL[name][0]:SMALL[name][0] + SMALL[name][1]]
        s.ident, s.ones = keep("ident", [P, P]), keep("ones", [P, P])
        s.iota, s.row, s.eps = keep("iota", [P, T]), keep("row", [P, len(TT)]), keep("eps", [P, 1])
        s.std, s.gain, s.mod = keep("std", [P, T]), keep("gain", [P, KT]), keep("mod", [P, 48])

        s.h, s.u = keep("h", [P, KT, T]), keep("u", [P, KT, T])
        s.x, s.m1, s.m2 = s.h[:, :, META:T], s.u[:, :, 0:SEQ], s.u[:, :, 0:SEQ]
        s.lists_t = keep("lists_t", [P, 3, SEQ])
        s.u_in, s.v_in = ([s.sem(f"{k}_in{q}") for q in range(PEER_SLOTS)] for k in "uv")
        first_part = whole.enter_context(ExitStack())
        s.w = Weights(opener(first_part)("ring", [P, RING, SLOT]), [s.sem(f"slot{i}_in") for i in range(RING)])

        def stage_sem(name):
            stage_sems.append(nc.alloc_semaphore(name))
            return stage_sems[-1]

        s.sem = stage_sem
        s.expert_in = [s.sem(f"expert_in{q}") for q in range(EXPERT_RING)]
        plan_weights(s)
        s.w.load_expert_unit = expert_loader(s)

        with ExitStack() as mixer:
            sb = opener(mixer)
            s.zs, s.gates, s.conf = sb("zs", [P, IT, T]), sb("gates", [P, 2 * KT, T]), sb("conf", [P, KT, T])
            s.xbc, s.dt_raw = sb("xbc", [P, XT, T]), sb("dt_raw", [P, len(TT), 64])
            with ExitStack() as stage:
                sb = opener(stage)
                s.cpad, s.xpad = sb("cpad", [P, KT, T + 2 * CONF_PAD]), sb("xpad", [P, XT, T + 2 * SSM_PAD])
                s.sig = sb("sig", [P, 2, T])
                constants(nc, s)
                s.scratch = s.xbc[:, :, :].rearrange("p k t -> p (k t)")
                rms(nc, s, "mix_norm", s.h[:, :, :], s.col("norm_mix"), s.u, KT, T)
                in_projection(nc, s)
            with ExitStack() as stage:
                sb = opener(stage)
                s.x_tok = sb("x_tok", [P, len(TT), INNER])
                s.cb = sb("cb", [P, GROUPS, sum(SCAN_COLS)])
                s.decay = sb("decay", [P, DECAYS - 1, max(SCAN_COLS)])
                spare = s.lists_t[:, :, :].rearrange("p a b -> p (a b)")
                s.decays = [s.decay[:, i, :] for i in range(DECAYS - 1)] + [spare[:, 0:max(SCAN_COLS)]]
                flat = s.decay[:, :, :].rearrange("p a b -> p (a b)")
                s.upto, s.since = (flat[:, i * 3 * T:(i + 1) * 3 * T].rearrange("p (j t) -> p j t", j=3) for i in range(2))
                flat, at = s.u[:, :, :].rearrange("p k t -> p (k t)"), 0
                cut = {}
                for k, n in (("dt", 192), ("a", 192), ("neg_cs", 192), ("a_exp", 64), ("csT", T), ("xd", 4 * 192), ("c_act", KT)):
                    cut[k], at = flat[:, at:at + n], at + n
                s.dt, s.a, s.neg_cs = (cut[k].rearrange("p (j h) -> p j h", j=3) for k in ("dt", "a", "neg_cs"))
                s.a_exp, s.csT, s.xd, s.c_act = cut["a_exp"], cut["csT"][0:64, :], cut["xd"], cut["c_act"]
                ssd_prepare(nc, s)
                flat = s.xbc[:, IT:XT, :].rearrange("p k t -> p (k t)")
                s.modrow = flat[:, 0:3 * 512].rearrange("p (r n) -> p r n", r=3)
                s.mod48 = flat[0:48, 3 * 512:3 * 512 + P]
                ssd_scan(nc, s)
            with ExitStack() as stage:
                s.scratch = opener(stage)("scratch", [P, IT * T])
                rms(nc, s, "ssm_norm", s.xbc[:, 0:IT, :], s.col("ssm_norm"), s.xbc[:, 0:IT, :], IT, T)
                mixer_out(nc, s)
        s.w_router = opener(first_part)("w_router", [P, KT, EXPERTS])
        s.router_in = start_load(nc, s, "router", s.w_router[:, :, :], s.d["w_router"].rearrange("(k p) e -> p k e", p=P))
        with ExitStack() as stage:
            s.scratch = opener(stage)("scratch_ffn", [P, KT * T])
            rms(nc, s, "ffn_norm", s.h[:, :, :], s.col("norm_ffn"), s.u, KT, T)
        with ExitStack() as stage:
            sb = opener(stage)
            s.extra = sb("extra", [P, EXPERT_RING - RING, SLOT])
            s.picked, s.list_t = sb("picked", [P, KT, SLOTS]), sb("list_t", [PAIR, 2 * EXPERTS])
            with ExitStack() as inner:
                sb = opener(inner)
                s.aff, s.aff_exp, s.row3 = sb("aff", [P, 3, EXPERTS]), sb("aff_exp", [P, 3, EXPERTS]), sb("row3", [P, 3])
                s.index2, s.aff2, s.work = sb("index2", [EXPERTS, PAIR]), sb("aff2", [EXPERTS, PAIR]), sb("work", [EXPERTS, T])
                s.top, s.top_at = sb("top", [EXPERTS, 8 * ROUNDS]), sb("top_at", [EXPERTS, 8 * ROUNDS], U32)
                s.tok_hi, s.tok_lo = sb("tok_hi", [P, 3, D], F32R), sb("tok_lo", [P, 3, D], F32R)
                s.onehot = sb("onehot", [P, 3, SLOTS], F32R)
                route(nc, s)
            sb = opener(stage)
            s.tokens, s.silu, s.hidden = sb("tokens", [P, KT, CAP]), sb("silu", [PAIR, 2, 512]), sb("hidden", [PAIR, 2, 512])
            s.hidden_t, s.y, s.spread = sb("hidden_t", [P, 2, 4, PAIR]), sb("y", [PAIR, 512]), sb("spread", [PAIR, T])
            clear_banks(nc, s)
            experts(nc, s)
        nc.clear_and_free_semaphores(list(stage_sems))
        nc.all_engine_barrier()
        second_block(nc, s, opener, first_part)
        finish(nc, s)


def clear_banks(nc, s):
    with nc.Block() as block:

        @block.vector
        def _(dve):
            dve.memset(s.ps[0:P, 0:6, :], 0.0)


def plan_weights(s):
    w, d = s.w, s.d
    s.in_first = 0
    for c in range(0, 2 * D, 512):
        w.add_columns(d["w_in"], c, 512)
    for c in range(OFF_XBC, OFF_DT, 512):
        w.add_columns(d["w_in"], c, 512)
    w.add_columns(d["w_in"], OFF_DT, 2 * HEADS)
    for c in list(range(OFF_Z, OFF_XBC, 512)) + list(range(OFF_GATE, OFF_GATE + 2 * D, 512)):
        w.add_columns(d["w_in"], c, 512)
    s.ada_first = len(w.units)
    for c in range(0, 6 * D, 512):
        w.add_columns(d["w_ada"], c, 512)
    s.conf_first = len(w.units)
    for c in range(0, D, 512):
        w.add_columns(d["w_conf_out"], c, 512)
    for c in range(0, D, 256):
        w.add_columns(d["w_ssm_out"], c, 256, IT)
    for c in range(0, D, 512):
        w.add_columns(d["w_out"], c, 512)
    s.expert_first = len(w.units)
    for u in range(RING):
        w.add_expert(u, s.expert_in)
    s.in2_first = len(w.units)
    for c, n in ((0, 512), (512, 512), (1024, 512), (1536, 272), (1808, 512)):
        w.add_columns(d["w_in2"], c, n)
    for c in range(0, D, 512):
        w.add_columns(d["w_out2"], c, 512)
    for c in range(0, 2 * D, 512):
        w.add_columns(d["w_peer_q"], c, 512)


def finish(nc, s):
    done = s.sem("out_done")
    with nc.Block() as block:

        @block.sync
        def _(sp):
            sp.dma_start(s.out.rearrange("(k p) t -> p k t", p=P), s.x[:, :, :]).then_inc(done, 16)
            sp.wait_ge(done, 16)


def declare(nc, arrays):
    d = {k: nc.dram_tensor(f"in_{k}", a.shape, mybir.dt.from_np(a.dtype), kind="ExternalInput").ap()
         for k, a in arrays.items()}
    return d, nc.dram_tensor("out_T", (D, SEQ), F32, kind="ExternalOutput").ap()


def layout(x):
    import numpy as np

    def cols(a):
        return np.asarray(a).reshape(-1, P).T

    def taps(a, kt):
        a = np.asarray(a)[0]
        return a.reshape(a.shape[0], kt, P).transpose(2, 1, 0).reshape(P, -1)

    def everywhere(a):
        a = np.asarray(a).reshape(1, -1)
        return np.broadcast_to(a, (P, a.shape[1]))

    order = [h for i in range(4) for h in (i, i + 4)]
    swa = np.concatenate([np.arange(64 * h, 64 * h + 64) for h in order])
    parts = {
        "norm_mix": cols(x["w_norm_mix"]), "conf_b": cols(x["b_conf_dw"]), "ln_g": cols(x["conf_ln_g"]),
        "ln_b": cols(x["conf_ln_b"]), "ssm_b": cols(x["b_ssm_conv"]),
        "ssm_d": cols(np.repeat(np.asarray(x["ssm_d"]).reshape(-1), HEAD_DIM)), "ssm_norm": cols(x["w_ssm_norm"]),
        "norm_ffn": cols(x["w_norm_ffn"]), "norm_final": cols(x["w_norm_final"]), "norm1": cols(x["norm1_g_2"]),
        "norm2": cols(x["norm2_g_2"]), "final_g": cols(x["final_g_2"]), "gla_norm": cols(x["gla_norm_g_2"]),
        "swa_norm": cols(np.asarray(x["swa_norm_g_2"])[0][swa]), "gla_b": cols(x["b_gla_alpha_2"]),
        "ada_b": cols(x["b_ada_2"]), "c": cols(x["c_2"]), "conf_w": taps(x["w_conf_dw"], KT),
        "ssm_w": taps(x["w_ssm_conv"], XT), "dt_bias": everywhere(x["ssm_dt_bias"]),
        "a_log": everywhere(x["ssm_a_log"]), "sinks": everywhere(x["swa_sinks_2"]),
    }
    small = np.concatenate([parts[k] for k in SMALL], axis=1)
    hT = np.concatenate([np.asarray(x["meta_tokens"]).T, np.asarray(x["x"])[0].T], axis=1)
    arrays = {"small": small, "hT": hT, "w_in": np.asarray(x["w_in"])[0], "w_ada": np.asarray(x["w_ada_2"])[0],
              "w_conf_out": np.asarray(x["w_conf_out"])[0], "w_ssm_out": np.asarray(x["w_ssm_out"])[0],
              "w_out": np.asarray(x["w_out"])[0], "w_router": np.asarray(x["w_router"])[0],
              "w_gate": np.asarray(x["w_exp_gate"])[0], "w_up": np.asarray(x["w_exp_up"])[0],
              "w_down": np.asarray(x["w_exp_down"])[0]}
    w_in2, w_out2 = np.asarray(x["w_in_2"])[0], np.asarray(x["w_out_2"])[0]
    q_g, v_g, a_lr, r_g, q_s, k_s, v_s = np.split(w_in2, [512, 1024, 1040, 1552, 2064, 2192], axis=1)
    arrays["w_in2"] = np.concatenate([q_g, r_g, q_s[:, swa], k_s, a_lr, v_s, v_g], axis=1)
    arrays["w_out2"] = np.concatenate([w_out2[:512], w_out2[512:][swa]], axis=0)
    arrays["w_peer_q"] = np.asarray(x["w_peer_q_2"])[0]
    arrays["gla_alpha"] = np.asarray(x["w_gla_alpha_2"])[0]
    arrays["peer_keys"] = np.stack([np.asarray(x["peer_keys_1_2"])[0].T, np.asarray(x["peer_keys_2_2"])[0].T])
    u = np.asarray(x["peer_u_2"])[0].reshape(KEYS, KEYS, KT, P)
    arrays["peer_u"] = u.transpose(1, 3, 2, 0).reshape(KEYS, P, D)
    arrays["peer_v"] = np.asarray(x["peer_v_2"])[0].reshape(KEYS, KEYS, D)
    return {k: np.ascontiguousarray(v) for k, v in arrays.items()}


def kernel(**inputs):
    import concourse.bacc as _bacc
    from concourse.bass_utils import run_bass_kernel_spmd as _run

    nc = _bacc.Bacc("TRN2", target_bir_lowering=False, num_devices=1)
    arrays = layout(inputs)
    build_program(nc, *declare(nc, arrays))
    r = _run(nc, [{f"in_{k}": a for k, a in arrays.items()}], core_ids=[0])
    return r.results[0]["out_T"].T.reshape(1, SEQ, D)
```
